# Optimizing a Trainium2 kernel written in Bass

```python
import jax, jax.numpy as jnp
from jax import lax
import numpy as np

D_MODEL = 1024
BATCH = 1
SEQ = 1024
DEPTH = 1

D_MIX = D_MODEL
MLA_HEADS = 8
QK_NOPE = 64
QK_ROPE = 32
V_HEAD = 64
Q_LORA = 256
KV_LORA = 128
ROPE_THETA = 10000.0
Q_BLOCK = 128
SG_HEADS = 8
SG_HEAD_DIM = 64
SG_CHUNK = 128
N_EXPERTS = 32
TOP_K = 4
D_EXPERT = D_MODEL
SWIGLU_LIMIT = 7.0
SWIGLU_ALPHA = 1.702
MOE_BLOCK = 128
D_PLE = 256
EPS = 1e-6
IN_COLS = Q_LORA + KV_LORA + QK_ROPE + 2 * SG_HEADS * SG_HEAD_DIM
MLA_WIDTH = MLA_HEADS * V_HEAD
SG_WIDTH = SG_HEADS * SG_HEAD_DIM

kernel_name = "hymba_mla_sgmlp_moe_sandwich_ple"

def rmsnorm(x, g):
    xf = x.astype(jnp.float32)
    y = xf * lax.rsqrt(jnp.mean(xf * xf, axis=-1, keepdims=True) + EPS)
    return (y * g.astype(jnp.float32)).astype(x.dtype)

def rope_tables(positions):
    inv_freq = 1.0 / (ROPE_THETA ** (jnp.arange(0, QK_ROPE, 2, dtype=jnp.float32) / QK_ROPE))
    ang = positions.astype(jnp.float32)[..., None] * inv_freq
    return jnp.cos(ang), jnp.sin(ang)

def apply_rope(x, cos, sin):
    xf = x.astype(jnp.float32)
    half = xf.shape[-1] // 2
    x1, x2 = xf[..., :half], xf[..., half:]
    return jnp.concatenate([x1 * cos - x2 * sin, x2 * cos + x1 * sin], axis=-1).astype(x.dtype)

def mla_attention(c_q, c_kv, k_rope, cos, sin, q_norm_g, w_uq, kv_norm_g, w_ukv):
    B, S, _ = c_q.shape
    q = jnp.einsum('bsr,rhd->bshd', rmsnorm(c_q, q_norm_g), w_uq)
    q = jnp.concatenate([q[..., :QK_NOPE], apply_rope(q[..., QK_NOPE:], cos[:, :, None], sin[:, :, None])], axis=-1)
    kv = jnp.einsum('bsr,rhd->bshd', rmsnorm(c_kv, kv_norm_g), w_ukv)
    k_nope, v = kv[..., :QK_NOPE], kv[..., QK_NOPE:]
    k_r = apply_rope(k_rope, cos, sin)
    k = jnp.concatenate([k_nope, jnp.broadcast_to(k_r[:, :, None], (B, S, MLA_HEADS, QK_ROPE))], axis=-1)
    scale = (QK_NOPE + QK_ROPE) ** -0.5
    nqb = S // Q_BLOCK
    qb = q.reshape(B, nqb, Q_BLOCK, MLA_HEADS, QK_NOPE + QK_ROPE).transpose(1, 0, 2, 3, 4)
    key_pos = jnp.arange(S)

    def query_block(args):
        i, q_blk = args
        s = jnp.einsum('bqhd,bkhd->bhqk', q_blk, k).astype(jnp.float32) * scale
        q_pos = i * Q_BLOCK + jnp.arange(Q_BLOCK)
        s = jnp.where(key_pos[None, :] <= q_pos[:, None], s, -jnp.inf)
        pr = jax.nn.softmax(s, axis=-1).astype(v.dtype)
        return jnp.einsum('bhqk,bkhd->bqhd', pr, v)

    o = lax.map(query_block, (jnp.arange(nqb), qb))
    return o.transpose(1, 0, 2, 3, 4).reshape(B, S, MLA_WIDTH)

def spatial_gating(z, v_norm_g, w_s, b_s):
    B, S, _ = z.shape
    nc = S // SG_CHUNK
    z = jax.nn.gelu(z)
    u, v = jnp.split(z, 2, axis=-1)
    u = u.reshape(B, nc, SG_CHUNK, SG_HEADS, SG_HEAD_DIM)
    v = rmsnorm(v.reshape(B, nc, SG_CHUNK, SG_HEADS, SG_HEAD_DIM), v_norm_g)
    causal = jnp.tril(jnp.ones((SG_CHUNK, SG_CHUNK), dtype=bool))
    w = jnp.where(causal[None], w_s, jnp.zeros_like(w_s))
    vm = jnp.einsum('hts,bnshc->bnthc', w, v) + b_s.T[None, None, :, :, None]
    return (u * vm).reshape(B, S, SG_WIDTH)

def moe(h, w_router, b_router, w_gate_up, b_gate_up, w_down, b_down):
    B, S, D = h.shape
    N = B * S
    xt = h.reshape(N, D)
    logits = (xt @ w_router + b_router).astype(jnp.float32)
    top_val, top_idx = lax.top_k(logits, TOP_K)
    gate = jax.nn.softmax(top_val, axis=-1)
    A = N * TOP_K
    e_flat = top_idx.reshape(A)
    tok_flat = jnp.repeat(jnp.arange(N, dtype=jnp.int32), TOP_K)
    w_flat = gate.reshape(A)
    order = jnp.argsort(e_flat)
    e_sorted, tok_sorted, w_sorted = e_flat[order], tok_flat[order], w_flat[order]
    counts = jnp.zeros((N_EXPERTS,), jnp.int32).at[e_flat].add(1)
    start = jnp.cumsum(counts) - counts
    padded = (counts + MOE_BLOCK - 1) // MOE_BLOCK * MOE_BLOCK
    pad_end = jnp.cumsum(padded)
    pad_start = pad_end - padded
    dest = pad_start[e_sorted] + (jnp.arange(A, dtype=jnp.int32) - start[e_sorted])
    n_blocks = A // MOE_BLOCK + N_EXPERTS
    P = n_blocks * MOE_BLOCK
    row_tok = jnp.zeros((P,), jnp.int32).at[dest].set(tok_sorted)
    row_w = jnp.zeros((P,), jnp.float32).at[dest].set(w_sorted)
    block_start = jnp.arange(n_blocks, dtype=jnp.int32) * MOE_BLOCK
    block_expert = jnp.minimum(jnp.sum(pad_end[None, :] <= block_start[:, None], axis=-1), N_EXPERTS - 1)
    x_rows = xt[row_tok].reshape(n_blocks, MOE_BLOCK, D)

    def expert_block(args):
        e, xb = args
        gu = xb @ w_gate_up[e] + b_gate_up[e]
        g, u = jnp.split(gu, 2, axis=-1)
        g = jnp.minimum(g, SWIGLU_LIMIT)
        u = jnp.clip(u, -SWIGLU_LIMIT, SWIGLU_LIMIT)
        act = (u + 1.0) * (g * jax.nn.sigmoid(SWIGLU_ALPHA * g))
        return act @ w_down[e] + b_down[e]

    y_rows = lax.map(expert_block, (block_expert, x_rows)).reshape(P, D)
    y = jax.ops.segment_sum(y_rows * row_w[:, None].astype(y_rows.dtype), row_tok, num_segments=N)
    return y.reshape(B, S, D)

def setup_inputs(seed: int = 0) -> dict:
    key = jax.random.key(seed)
    ks = jax.random.split(key, 32)
    f32 = jnp.float32

    def nrm(k, shape, scale):
        return jax.random.normal(k, shape, f32) * scale

    def gain(k, shape):
        return 1.0 + 0.05 * jax.random.normal(k, shape, f32)

    L = DEPTH
    return {
        "x": nrm(ks[0], (BATCH, SEQ, D_MODEL), 1.0),
        "p": nrm(ks[1], (DEPTH, BATCH, SEQ, D_PLE), 1.0),
        "positions": jnp.broadcast_to(jnp.arange(SEQ, dtype=jnp.int32), (BATCH, SEQ)),
        "attn_pre_g": gain(ks[2], (L, D_MODEL)),
        "w_in": nrm(ks[3], (L, D_MODEL, IN_COLS), D_MODEL ** -0.5),
        "q_norm_g": gain(ks[4], (L, Q_LORA)),
        "w_uq": nrm(ks[5], (L, Q_LORA, MLA_HEADS, QK_NOPE + QK_ROPE), Q_LORA ** -0.5),
        "kv_norm_g": gain(ks[6], (L, KV_LORA)),
        "w_ukv": nrm(ks[7], (L, KV_LORA, MLA_HEADS, QK_NOPE + V_HEAD), KV_LORA ** -0.5),
        "sg_norm_g": gain(ks[8], (L, SG_HEADS, SG_HEAD_DIM)),
        "w_spatial": nrm(ks[9], (L, SG_HEADS, SG_CHUNK, SG_CHUNK), SG_CHUNK ** -0.5),
        "b_spatial": 1.0 + 0.1 * jax.random.normal(ks[10], (L, SG_HEADS, SG_CHUNK), f32),
        "mla_out_g": gain(ks[11], (L, MLA_WIDTH)),
        "sg_out_g": gain(ks[12], (L, SG_WIDTH)),
        "w_out": nrm(ks[13], (L, D_MIX, D_MODEL), D_MIX ** -0.5),
        "attn_post_g": gain(ks[14], (L, D_MODEL)),
        "ffn_pre_g": gain(ks[15], (L, D_MODEL)),
        "w_router": nrm(ks[16], (L, D_MODEL, N_EXPERTS), D_MODEL ** -0.5),
        "b_router": nrm(ks[17], (L, N_EXPERTS), 0.01),
        "w_gate_up": nrm(ks[18], (L, N_EXPERTS, D_MODEL, 2 * D_EXPERT), D_MODEL ** -0.5),
        "b_gate_up": nrm(ks[19], (L, N_EXPERTS, 2 * D_EXPERT), 0.02),
        "w_down": nrm(ks[20], (L, N_EXPERTS, D_EXPERT, D_MODEL), D_EXPERT ** -0.5),
        "b_down": nrm(ks[21], (L, N_EXPERTS, D_MODEL), 0.02),
        "ffn_post_g": gain(ks[22], (L, D_MODEL)),
        "w_ple_gate": nrm(ks[23], (L, D_MODEL, D_MODEL), D_MODEL ** -0.5),
        "b_ple_gate": nrm(ks[24], (L, D_MODEL), 0.02),
        "w_ple_proj": nrm(ks[25], (L, D_PLE, D_MODEL), D_PLE ** -0.5),
        "ple_norm_g": gain(ks[26], (L, D_MODEL)),
    }

def reference(x, p, positions, attn_pre_g, w_in, q_norm_g, w_uq, kv_norm_g, w_ukv, sg_norm_g, w_spatial,
              b_spatial, mla_out_g, sg_out_g, w_out, attn_post_g, ffn_pre_g, w_router, b_router, w_gate_up,
              b_gate_up, w_down, b_down, ffn_post_g, w_ple_gate, b_ple_gate, w_ple_proj, ple_norm_g):
    cos, sin = rope_tables(positions)
    splits = [Q_LORA, Q_LORA + KV_LORA, Q_LORA + KV_LORA + QK_ROPE]
    for i in range(DEPTH):
        h = rmsnorm(x, attn_pre_g[i])
        z = h @ w_in[i]
        c_q, c_kv, k_rope, z_sg = jnp.split(z, splits, axis=-1)
        o_mla = mla_attention(c_q, c_kv, k_rope, cos, sin, q_norm_g[i], w_uq[i], kv_norm_g[i], w_ukv[i])
        o_sg = spatial_gating(z_sg, sg_norm_g[i], w_spatial[i], b_spatial[i])
        mix = jnp.concatenate([rmsnorm(o_mla, mla_out_g[i]), rmsnorm(o_sg, sg_out_g[i])], axis=-1)
        x = x + rmsnorm(mix @ w_out[i], attn_post_g[i])
        y = moe(rmsnorm(x, ffn_pre_g[i]), w_router[i], b_router[i], w_gate_up[i], b_gate_up[i], w_down[i], b_down[i])
        x = x + rmsnorm(y, ffn_post_g[i])
        g = jax.nn.sigmoid(x @ w_ple_gate[i] + b_ple_gate[i])
        x = x + rmsnorm(g * (p[i] @ w_ple_proj[i]), ple_norm_g[i])
    return x


_drawn_inputs = setup_inputs


def setup_inputs(seed=0):
    import zlib

    import numpy as np

    out = dict(_drawn_inputs(seed))
    spreads = {}
    factors = {'b_gate_up': 4.318, 'b_down': 4.939, 'b_ple_gate': 8.0}
    for name, (base, spread) in spreads.items():
        noise = np.random.default_rng([zlib.crc32(name.encode()), seed]).standard_normal(out[name].shape)
        drawn = base * np.exp(spread * noise) if base else spread * noise
        out[name] = __import__('jax').numpy.asarray(drawn.astype(out[name].dtype))
    for name, factor in factors.items():
        out[name] = (out[name] * factor).astype(out[name].dtype)
    return out
```

```python
from contextlib import ExitStack

import numpy as np

import concourse.bass as bass
from concourse import mybir

ALU = mybir.AluOpType
ACT = mybir.ActivationFunctionType
AX = mybir.AxisListType
F32 = mybir.dt.float32
I32 = mybir.dt.int32
U32 = mybir.dt.uint32

P = 128
D = 1024
SEQ = 1024
T = SEQ // P
KD = D // P
H = 8
NOPE, ROPE, VH = 64, 32, 64
HR = ROPE // 2
QK = NOPE + ROPE
QL, KVL = 256, 128
QC = QL // P
A_COLS = QL + KVL + ROPE
SGW = 512
IN_COLS = A_COLS + 2 * SGW
HC = SGW // H
E = 32
TOPK = 4
F = 1024
KF = F // P
DP = 256
KP = DP // P
EPS = 1e-6
SCALE = float(QK) ** -0.5
LIMIT, ALPHA = 7.0, 1.702
THETA = 10000.0
NEG = -3.0e38
TWO_PI = 2 * np.pi
PI_A = 6.28125
PI_B = float(TWO_PI - PI_A)
ROUND = 1.5 * 2.0 ** 23
R_MAX = 3.1415925

CT = 256
CH = CT // P
MORE = TOPK * SEQ // (CT + 1)
MAX_ITEMS = E + MORE
TAB = MAX_ITEMS + 1
UNIT = KD * 256
N_UNITS = 12
GU_UNITS = 8


class Chain:

    def __init__(self, m, eng, own):
        self.eng, self.own, self.count = eng, own, m.count

    def __call__(self, ins, signal=None):
        s = self.own if signal is None else signal
        self.count[s.name] = self.count.get(s.name, 0) + 1
        ins.then_inc(s, 1)
        self.eng.wait_ge(s, self.count[s.name])


class Buffers:

    def __init__(self, nc, ctx):
        def sb(name, shape, dt=F32):
            return ctx.enter_context(nc.sbuf_tensor(name, shape, dt))

        self.sem = lambda name: ctx.enter_context(nc.semaphore(name))
        self.count = {}
        self.act_step, self.dve_step, self.pool_step = (self.sem(f"{e}_step") for e in ("act", "dve", "pool"))
        self.x_loaded = [self.sem(f"x_loaded{t}") for t in range(T)]
        self.h_rows = nc.dram_tensor("h_rows", [SEQ, D], F32).ap()
        self.tok_list = nc.dram_tensor("tok_list", [TAB * CT, 1], I32).ap()
        self.y_rows = nc.dram_tensor("y_rows", [MAX_ITEMS * CT, D], F32).ap()
        self.ps = ctx.enter_context(nc.psum_tensor("ps", [P, 8, 512], F32))

        xa = sb("xa", [P, T * D])
        ring = sb("ring", [P, N_UNITS * UNIT])
        work = sb("work", [P, 16384])
        self.xa, self.ring, self.work = xa, ring, work
        self.x_sb = xa[:, :].rearrange("p (t d) -> p t d", t=T)
        self.za = xa[:, 0:T * A_COLS].rearrange("p (t c) -> p t c", t=T)
        self.qT = xa[0:QK, :].rearrange("p (h s) -> p h s", h=H)
        n_in = KD * IN_COLS
        self.w_in = ring[:, 0:n_in].rearrange("p (k n) -> p k n", k=KD)
        self.w_uq = ring[:, n_in:n_in + 1536].rearrange("p (k n) -> p k n", k=QC)
        self.w_ukv = ring[:, 13056:14080].rearrange("p (h n) -> p h n", h=H)
        self.cqT = ring[:, 14080:16128].rearrange("p (k s) -> p k s", k=QC)
        self.ckvT = ring[:, 16128:17152]
        self.krT = ring[0:QK, 17152:18176]
        self.v_sb = ring[:, 0:4096].rearrange("p (t n) -> p t n", t=T)
        self.probs = ring[:, 4096:6144].rearrange("p (b s) -> p b s", b=2)
        self.probsT = ring[:, 6144:8192].rearrange("p (b s) -> p b s", b=2)
        self.w_spT = ring[:, 8192:9216].rearrange("p (h s) -> p h s", h=H)
        self.w_sp = ring[:, 9216:10240].rearrange("p (h s) -> p h s", h=H)
        self.sg_g = ring[:, 10240:10752]
        self.w_out = ring[:, 12288:20480].rearrange("p (k n) -> p k n", k=KD)
        self.o_sb = ring[:, 20480:24576].rearrange("p (t c) -> p t c", t=T)
        self.post_g = ring[:, 0:1024]
        self.ffn_g = ring[:, 1024:2048]
        self.y_row = ring[:, 2048:4096].rearrange("p (b d) -> p b d", b=2)
        self.h_row = ring[:, 4096:6144].rearrange("p (b d) -> p b d", b=2)
        self.hT = ring[:, 6144:7168].rearrange("p (k s) -> p k s", k=KD)
        self.w_router = ring[:, 7168:7424].rearrange("p (k e) -> p k e", k=KD)
        self.logits = ring[:, 7424:7680].rearrange("p (t e) -> p t e", t=T)
        self.hot = ring[:, 7680:8704].rearrange("p (t k e) -> p t k e", t=T, k=TOPK)
        self.taken = ring[:, 8704:8960].rearrange("p (t e) -> p t e", t=T)
        self.place = ring[:, 8960:9216].rearrange("p (t e) -> p t e", t=T)
        self.scr = ring[:, 9216:12288]
        self.unit = [ring[:, u * UNIT:(u + 1) * UNIT].rearrange("p (k n) -> p k n", k=KD) for u in range(N_UNITS)]
        self.xT = work[:, 0:8192].rearrange("p (k s) -> p k s", k=KD)
        self.kT = work[0:QK, 0:8192].rearrange("p (h s) -> p h s", h=H)
        self.mixT = work[:, 0:8192].rearrange("p (k s) -> p k s", k=KD)
        self.u_sg = work[:, 8192:12288].rearrange("p (t c) -> p t c", t=T)
        self.v_sg = work[:, 12288:16384].rearrange("p (t c) -> p t c", t=T)

        self.junk = sb("junk", [P, D])
        self.ident = sb("ident", [P, P])
        self.causal = sb("causal", [P, P])
        self.before = sb("before", [P, P])
        self.ones = sb("ones", [P, P])
        self.gains = sb("gains", [P, 20])
        self.stat = sb("stat", [P, 160])
        self.small = sb("small", [P, 64])
        self.cosb = sb("cosb", [P, T, HR])
        self.sinb = sb("sinb", [P, T, HR])
        self.rtmp = [sb(f"rtmp{i}", [P, T, HR]) for i in range(4)]
        self.invf = sb("invf", [P, HR])
        self.posi = sb("posi", [P, T], I32)
        self.posf = sb("posf", [P, T])
        self.small_row = sb("small_row", [P, 256])
        self.b_sp = sb("b_sp", [P, H])
        self.b_r = sb("b_r", [P, E])
        self.gates = sb("gates", [P, T, TOPK])
        self.slots = sb("slots", [P, T, TOPK], I32)
        self.tokid = sb("tokid", [P, T], I32)
        self.items = sb("items", [1, TAB + 1], I32)
        self.bias_cols = sb("bias_cols", [P, 2 * KF + KD, E])
        self.bias_now = sb("bias_now", [P, 2 * KF + KD])
        self.idx_now = sb("idx_now", [P, 2, CH], I32)
        self.g_x, self.g_q, self.g_kv = self.gains[:, 0:8], self.gains[:, 8:10], self.gains[:, 10:11]
        self.g_mix = self.gains[:, 11:19]

    def bank(self, i, rows=P):
        return self.ps[0:rows, i, :]


def columns(vector, k):
    return vector.rearrange("l (k p) -> p (l k)", k=k)


def on_all(vector):
    return vector.rearrange("l n -> (l n)").partition_broadcast(P)


def rope(v, step, x1, x2, cos, sin, tmp, signal=None):
    step(v.tensor_tensor(tmp[0], x1, cos, ALU.mult))
    step(v.tensor_tensor(tmp[1], x2, sin, ALU.mult))
    step(v.tensor_tensor(tmp[2], x2, cos, ALU.mult))
    step(v.tensor_tensor(tmp[3], x1, sin, ALU.mult))
    step(v.tensor_tensor(x1, tmp[0], tmp[1], ALU.subtract))
    step(v.tensor_tensor(x2, tmp[2], tmp[3], ALU.add), signal)


def input_projection(nc, m, x, positions, attn_pre_g, w_in, q_norm_g, w_uq, kv_norm_g, w_ukv, b_spatial, mla_out_g,
                     sg_out_g, b_router, b_gate_up, b_down):
    with ExitStack() as ctx:
        sem = m.sem

        x_loaded = m.x_loaded
        biases_loaded = sem("biases_loaded")
        small_loaded = sem("small_loaded")
        w_in_loaded = sem("w_in_loaded")
        w_mid_loaded = sem("w_mid_loaded")
        consts_ready = sem("consts_ready")
        w_in_scaled = sem("w_in_scaled")
        biasT_psum = sem("biasT_psum")
        biasT_copied = sem("biasT_copied")
        xT_psum = sem("xT_psum")
        xT_act = sem("xT_act")
        xT_dve = sem("xT_dve")
        squares_x = sem("squares_x")
        mean_x = sem("mean_x")
        root_x = sem("root_x")
        rstd_x = sem("rstd_x")
        angles = sem("angles")
        sines = sem("sines")
        z_psum = sem("z_psum")
        z_latent = sem("z_latent")
        z_gated = sem("z_gated")
        mean_latent = sem("mean_latent")
        root_latent = sem("root_latent")
        latent_ready = sem("latent_ready")
        latentT_psum = sem("latentT_psum")
        latentT_copied = sem("latentT_copied")
        block = ctx.enter_context(nc.Block())
        bgu_rows = m.work[0:E, 8192:8192 + 2 * F]
        bd_rows = m.work[0:E, 8192 + 2 * F:8192 + 2 * F + D]
        ssx = m.stat[:, 0:T]
        ms = m.stat[:, T:2 * T]
        lat = m.stat[:, 2 * T:4 * T]
        n_bias = 2 * KF + KD

        @block.sync
        def _(sp):
            x_t = x.rearrange("b (t p) d -> p (b t) d", p=P)
            for t in range(T):
                sp.dma_start(m.x_sb[:, t, :], x_t[:, t, :]).then_inc(x_loaded[t], 16)
                if t == 1:
                    sp.dma_start(bgu_rows, b_gate_up.rearrange("l e n -> (l e) n")).then_inc(biases_loaded, 16)
                    sp.dma_start(bd_rows, b_down.rearrange("l e n -> (l e) n")).then_inc(biases_loaded, 16)
            wi = w_in.rearrange("l (k p) n -> p (l k) n", p=P)
            for k in range(0, KD, 2):
                sp.dma_start(m.w_in[:, k:k + 2, :], wi[:, k:k + 2, :]).then_inc(w_in_loaded, 16)
            sp.dma_start(m.w_uq, w_uq.rearrange("l (k p) h c -> p (l k) (h c)", p=P)).then_inc(w_mid_loaded, 16)
            sp.dma_start(m.w_ukv, w_ukv.rearrange("l p h c -> (l p) h c")).then_inc(w_mid_loaded, 16)

        @block.gpsimd
        def _(pool):
            g = nc.gpsimd
            step = Chain(m, pool, m.pool_step)
            pool.dma_start(m.g_x, columns(attn_pre_g, KD)).then_inc(small_loaded, 16)
            pool.dma_start(m.posi[:, :], positions.rearrange("b (t p) -> p (b t)", p=P)).then_inc(small_loaded, 16)
            pool.dma_start(m.g_q, columns(q_norm_g, QC)).then_inc(small_loaded, 16)
            pool.dma_start(m.g_kv, columns(kv_norm_g, 1)).then_inc(small_loaded, 16)
            pool.dma_start(m.g_mix[:, 0:4], columns(mla_out_g, 4)).then_inc(small_loaded, 16)
            pool.dma_start(m.g_mix[:, 4:8], columns(sg_out_g, 4)).then_inc(small_loaded, 16)
            pool.dma_start(m.b_sp[:, :], b_spatial.rearrange("l h t -> t (l h)")).then_inc(small_loaded, 16)
            pool.dma_start(m.b_r[:, :], on_all(b_router)).then_inc(small_loaded, 16)
            step(g.memset(m.ident[:, :], 0.0))
            step(g.affine_select(out=m.ident[:, :], in_=m.ident[:, :], compare_op=ALU.not_equal, fill=1.0, base=0,
                                 pattern=[[-1, P]], channel_multiplier=1), consts_ready)
            inv = (np.float32(1.0) / np.power(np.float32(THETA), np.arange(0, ROPE, 2, dtype=np.float32)
                                              / np.float32(ROPE))).astype(np.float32)
            for i in range(HR):
                step(g.memset(m.invf[:, i:i + 1], float(inv[i])), consts_ready)
            step(g.memset(m.causal[:, :], 0.0))
            step(g.affine_select(out=m.causal[:, :], in_=m.causal[:, :], compare_op=ALU.is_ge, fill=NEG, base=0,
                                 pattern=[[-1, P]], channel_multiplier=1))
            step(g.memset(m.ones[:, :], 1.0))
            step(g.affine_select(out=m.before[:, :], in_=m.ones[:, :], compare_op=ALU.is_gt, fill=0.0, base=0,
                                 pattern=[[1, P]], channel_multiplier=-1))
            step(g.iota(m.tokid[:, :], pattern=[[P, T]], base=0, channel_multiplier=1))
            pool.wait_ge(small_loaded, 8 * 16)
            pool.wait_ge(w_in_loaded, 4 * 16)
            for k in range(KD):
                step(g.tensor_scalar(m.w_in[:, k, :], m.w_in[:, k, :], m.g_x[:, k:k + 1], None, ALU.mult),
                     w_in_scaled)
            pool.wait_ge(w_mid_loaded, 2 * 16)
            for k in range(QC):
                step(g.tensor_scalar(m.w_uq[:, k, :], m.w_uq[:, k, :], m.g_q[:, k:k + 1], None, ALU.mult))
            step(g.tensor_scalar(m.w_ukv, m.w_ukv, m.g_kv, None, ALU.mult))

        @block.scalar
        def _(act):
            s = nc.scalar
            step = Chain(m, act, m.act_step)
            for t in range(T):
                act.wait_ge(x_loaded[t], 16)
                step(s.activation(m.junk[:, :], m.x_sb[:, t, :], ACT.Square, accum_out=ssx[:, t:t + 1]), squares_x)
                act.wait_ge(xT_psum, t + 1)
                step(s.activation(m.xT[:, 0:4, t * P:(t + 1) * P], m.bank(2 * (t % 2)).rearrange(
                    "p (k s) -> p k s", k=4), ACT.Copy), xT_act)
            act.wait_ge(mean_x, 1)
            step(s.activation(ms, ms, ACT.Sqrt), root_x)
            act.wait_ge(angles, 1)
            step(s.activation(m.sinb[:, :, :], m.rtmp[0][:, :, :], ACT.Sin))
            step(s.activation(m.cosb[:, :, :], m.rtmp[0][:, :, :], ACT.Sin, scale=0.5), sines)
            act.wait_ge(rstd_x, 1)
            act.wait_ge(biasT_psum, 2)
            for t in range(T):
                act.wait_ge(z_psum, t + 1)
                b = 3 * (t % 2)
                step(s.activation(m.u_sg[:, t, :], m.bank(b + 1), ACT.Gelu_apprx_tanh, scale=ms[:, t:t + 1]), z_gated)
                step(s.activation(m.v_sg[:, t, :], m.bank(b + 2), ACT.Gelu_apprx_tanh, scale=ms[:, t:t + 1]), z_gated)
            act.wait_ge(mean_latent, 1)
            step(s.activation(lat, lat, ACT.Sqrt), root_latent)

        @block.vector
        def _(dve):
            v = nc.vector
            step = Chain(m, dve, m.dve_step)
            for t in range(T):
                dve.wait_ge(xT_psum, t + 1)
                step(v.tensor_copy(m.xT[:, 4:8, t * P:(t + 1) * P], m.bank(2 * (t % 2) + 1).rearrange(
                    "p (k s) -> p k s", k=4)), xT_dve)
            dve.wait_ge(squares_x, T)
            step(v.tensor_scalar(ms, ssx, 1.0 / D, EPS, ALU.mult, ALU.add), mean_x)
            dve.wait_ge(small_loaded, 8 * 16)
            dve.wait_ge(consts_ready, 1 + HR)
            step(v.tensor_copy(m.posf[:, :], m.posi[:, :]))
            r0, r1 = m.rtmp[0][:, :, :], m.rtmp[1][:, :, :]
            wide = [P, T, HR]
            step(v.tensor_tensor(r0, m.posf[:, :].unsqueeze(2).broadcast_to(wide),
                                 m.invf[:, :].unsqueeze(1).broadcast_to(wide), ALU.mult))
            step(v.tensor_scalar(r1, r0, float(1.0 / TWO_PI), ROUND, ALU.mult, ALU.add))
            step(v.tensor_scalar(r1, r1, ROUND, None, ALU.subtract))
            step(v.scalar_tensor_tensor(r0, r1, -PI_A, r0, ALU.mult, ALU.add))
            step(v.scalar_tensor_tensor(r0, r1, -PI_B, r0, ALU.mult, ALU.add))
            step(v.tensor_scalar(r0, r0, R_MAX, -R_MAX, ALU.min, ALU.max), angles)
            dve.wait_ge(root_x, 1)
            step(v.reciprocal(ms, ms), rstd_x)
            for i in range(2):
                dve.wait_ge(biasT_psum, i + 1)
                n = min(16, n_bias - 16 * i)
                step(v.tensor_copy(m.bias_cols[:, 16 * i:16 * i + n, :], m.bank(6 + i)[:, 0:n * E].rearrange(
                    "p (c e) -> p c e", e=E)), biasT_copied)
            dve.wait_ge(sines, 1)
            step(v.tensor_tensor(m.cosb[:, :, :], m.cosb[:, :, :], m.cosb[:, :, :], ALU.mult))
            step(v.tensor_scalar(m.cosb[:, :, :], m.cosb[:, :, :], -2.0, 1.0, ALU.mult, ALU.add))
            dve.wait_ge(rstd_x, 1)
            for t in range(T):
                dve.wait_ge(z_psum, t + 1)
                step(v.tensor_scalar(m.za[:, t, :], m.bank(3 * (t % 2))[:, 0:A_COLS], ms[:, t:t + 1], None, ALU.mult),
                     z_latent)
                for a, b, c in ((0, QL, t), (QL, QL + KVL, T + t)):
                    step(v.tensor_tensor_reduce(out=m.small_row[:, 0:b - a], in0=m.za[:, t, a:b], in1=m.za[:, t, a:b],
                                                scale=1.0, scalar=0.0, op0=ALU.mult, op1=ALU.add,
                                                accum_out=lat[:, c:c + 1]))
            step(v.tensor_scalar(lat[:, 0:T], lat[:, 0:T], 1.0 / QL, EPS, ALU.mult, ALU.add))
            step(v.tensor_scalar(lat[:, T:2 * T], lat[:, T:2 * T], 1.0 / KVL, EPS, ALU.mult, ALU.add), mean_latent)
            rope(v, step, m.za[:, :, QL + KVL:QL + KVL + HR], m.za[:, :, QL + KVL + HR:A_COLS], m.cosb[:, :, :],
                 m.sinb[:, :, :], [r[:, :, :] for r in m.rtmp])
            dve.wait_ge(root_latent, 1)
            step(v.reciprocal(lat, lat))
            for t in range(T + 1):
                if t < T:
                    step(v.tensor_scalar(m.za[:, t, 0:QL], m.za[:, t, 0:QL], lat[:, t:t + 1], None, ALU.mult))
                    step(v.tensor_scalar(m.za[:, t, QL:QL + KVL], m.za[:, t, QL:QL + KVL], lat[:, T + t:T + t + 1],
                                         None, ALU.mult), latent_ready)
                if t >= 1:
                    dve.wait_ge(latentT_psum, t)
                    tok = slice((t - 1) * P, t * P)
                    b = m.bank(6 + (t - 1) % 2)
                    step(v.tensor_copy(m.cqT[:, :, tok], b[:, 0:QL].rearrange("p (k s) -> p k s", k=QC)))
                    step(v.tensor_copy(m.ckvT[:, tok], b[:, QL:QL + P]))
                    step(v.tensor_copy(m.krT[NOPE:QK, tok], b[NOPE:QK, QL + P:QL + 2 * P]), latentT_copied)

        @block.tensor
        def _(pe):
            mm, tr = nc.tensor.matmul, nc.tensor.transpose
            pe.wait_ge(consts_ready, 1)

            def transpose_biases(i):
                pe.wait_ge(biases_loaded, 32)
                for c in range(16 * i, min(16 * i + 16, n_bias)):
                    last = tr(m.bank(6 + i)[:, (c - 16 * i) * E:(c - 16 * i + 1) * E],
                              m.work[0:E, 8192 + c * P:8192 + (c + 1) * P], m.ident[0:E, 0:E])
                last.then_inc(biasT_psum, 1)

            for t in range(T):
                pe.wait_ge(x_loaded[t], 16)
                if t >= 2:
                    pe.wait_ge(xT_act, t - 1)
                    pe.wait_ge(xT_dve, t - 1)
                for k in range(KD):
                    last = tr(m.bank(2 * (t % 2) + k // 4)[:, (k % 4) * P:(k % 4 + 1) * P],
                              m.x_sb[:, t, k * P:(k + 1) * P], m.ident[:, :])
                last.then_inc(xT_psum, 1)
            for i in range(2):
                transpose_biases(i)
            pe.wait_ge(xT_act, T)
            pe.wait_ge(xT_dve, T)
            for t in range(T):
                if t >= 2:
                    pe.wait_ge(z_latent, t - 1)
                    pe.wait_ge(z_gated, 2 * (t - 1))
                for k in range(KD):
                    if t == 0:
                        pe.wait_ge(w_in_scaled, k + 1)
                    for j, (a, b) in enumerate(((0, A_COLS), (A_COLS, A_COLS + SGW), (A_COLS + SGW, IN_COLS))):
                        last = mm(m.bank(3 * (t % 2) + j)[:, 0:b - a], m.xT[:, k, t * P:(t + 1) * P],
                                  m.w_in[:, k, a:b], start=(k == 0), stop=(k == KD - 1))
                last.then_inc(z_psum, 1)
            pe.wait_ge(biasT_copied, 2)
            for t in range(T):
                pe.wait_ge(latent_ready, t + 1)
                if t >= 2:
                    pe.wait_ge(latentT_copied, t - 1)
                b = m.bank(6 + t % 2)
                for i in range(3):
                    tr(b[:, i * P:(i + 1) * P], m.za[:, t, i * P:(i + 1) * P], m.ident[:, :])
                tr(b[0:QK, 3 * P:4 * P], m.za[:, t, A_COLS - QK:A_COLS], m.ident[:, :]).then_inc(latentT_psum, 1)


def attention_operands(nc, m, w_spatial, sg_norm_g):
    with ExitStack() as ctx:
        sem = m.sem

        w_sp_loaded = sem("w_sp_loaded")
        kr_copied = sem("kr_copied")
        w_spT_psum = sem("w_spT_psum")
        w_spT_copied = sem("w_spT_copied")
        w_spT_masked = sem("w_spT_masked")
        v_squares = sem("v_squares")
        v_mean = sem("v_mean")
        v_root = sem("v_root")
        v_normed = sem("v_normed")
        q_psum = sem("q_psum")
        q_copied = sem("q_copied")
        q_roped = sem("q_roped")
        qT_psum = sem("qT_psum")
        qT_act = sem("qT_act")
        qT_dve = sem("qT_dve")
        kv_psum = sem("kv_psum")
        kv_act = sem("kv_act")
        kv_dve = sem("kv_dve")
        sg_psum = sem("sg_psum")
        sg_gated = sem("sg_gated")
        block = ctx.enter_context(nc.Block())
        q_row = m.ring[:, 20480:20480 + 2 * H * QK].rearrange("p (b h c) -> p b h c", b=2, h=H)
        squares = m.ring[:, 4096:8192]
        sgs = m.stat[:, 32:32 + T * H]
        half = H // 2
        kv_jobs = [("k", h, s) for h in range(H) for s in range(2)] + [("v", t, 0) for t in range(T)]

        @block.sync
        def _(sp):
            sp.dma_start(m.w_sp, w_spatial.rearrange("l h t s -> t (l h) s")).then_inc(w_sp_loaded, 16)
            sp.dma_start(m.sg_g, on_all(sg_norm_g.rearrange("l h c -> l (h c)"))).then_inc(w_sp_loaded, 16)

        @block.gpsimd
        def _(pool):
            g = nc.gpsimd
            step = Chain(m, pool, m.pool_step)
            for h in range(H):
                step(g.tensor_copy(m.kT[NOPE:QK, h, :], m.krT[NOPE:QK, :]), kr_copied)
            for i in range(2):
                pool.wait_ge(w_spT_copied, i + 1)
                part = m.w_spT[:, 4 * i:4 * i + 4, :]
                step(g.affine_select(out=part, in_=part, compare_op=ALU.is_ge, fill=0.0, base=0,
                                     pattern=[[0, 4], [1, P]], channel_multiplier=-1), w_spT_masked)

        @block.scalar
        def _(act):
            s = nc.scalar
            step = Chain(m, act, m.act_step)
            step(s.activation(squares, m.v_sg.rearrange("p t c -> p (t c)"), ACT.Square), v_squares)
            for i in range(2):
                act.wait_ge(w_spT_psum, i + 1)
                step(s.activation(m.w_spT[:, 4 * i:4 * i + 4, :], m.bank(6 + i).rearrange("p (h s) -> p h s", h=4),
                                  ACT.Copy), w_spT_copied)
            act.wait_ge(v_mean, 1)
            step(s.activation(sgs, sgs, ACT.Sqrt), v_root)
            for t in range(T + 1):
                if t < T:
                    act.wait_ge(q_psum, t + 1)
                    if t >= 2:
                        act.wait_ge(qT_psum, t - 1)
                    for i in range(2):
                        step(s.activation(q_row[:, t % 2, half * i:half * i + half, :],
                                          m.bank(2 * (t % 2) + i)[:, 0:half * QK].rearrange(
                                              "p (h c) -> p h c", h=half), ACT.Copy), q_copied)
                if t >= 1:
                    act.wait_ge(qT_psum, t)
                    step(s.activation(m.qT[:, 0:half, (t - 1) * P:t * P], m.bank(4, QK).rearrange(
                        "p (h s) -> p h s", h=half), ACT.Copy), qT_act)
            for n, (kind, i, j) in enumerate(kv_jobs):
                if n % 2 == 0:
                    act.wait_ge(kv_psum, n + 1)
                    if kind == "k":
                        step(s.activation(m.kT[0:NOPE, i, j * 512:(j + 1) * 512], m.bank(6, NOPE), ACT.Copy), kv_act)
                    else:
                        step(s.activation(m.v_sb[:, i, :], m.bank(6), ACT.Copy), kv_act)

        @block.vector
        def _(dve):
            v = nc.vector
            step = Chain(m, dve, m.dve_step)
            dve.wait_ge(v_squares, 1)
            step(v.tensor_reduce(out=sgs, in_=squares.rearrange("p (g c) -> p g c", c=HC), op=ALU.add, axis=AX.X))
            step(v.tensor_scalar(sgs, sgs, 1.0 / HC, EPS, ALU.mult, ALU.add), v_mean)
            dve.wait_ge(v_root, 1)
            step(v.reciprocal(sgs, sgs))
            grouped = m.v_sg.rearrange("p t (h c) -> p (t h) c", h=H)
            step(v.tensor_tensor(grouped, grouped, sgs.unsqueeze(2).broadcast_to([P, T * H, HC]), ALU.mult))
            dve.wait_ge(w_sp_loaded, 32)
            step(v.tensor_tensor(m.v_sg, m.v_sg, m.sg_g.unsqueeze(1).broadcast_to([P, T, SGW]), ALU.mult), v_normed)
            for t in range(T + 1):
                if t < T:
                    dve.wait_ge(q_copied, 2 * (t + 1))
                    q = q_row[:, t % 2, :, :]
                    turn = [P, H, HR]
                    rope(v, step, q[:, :, NOPE:NOPE + HR], q[:, :, NOPE + HR:QK],
                         m.cosb[:, t, :].unsqueeze(1).broadcast_to(turn),
                         m.sinb[:, t, :].unsqueeze(1).broadcast_to(turn), [r[:, :, :] for r in m.rtmp], q_roped)
                if t >= 1:
                    dve.wait_ge(qT_psum, t)
                    step(v.tensor_copy(m.qT[:, half:H, (t - 1) * P:t * P], m.bank(5, QK).rearrange(
                        "p (h s) -> p h s", h=half)), qT_dve)
            for n, (kind, i, j) in enumerate(kv_jobs):
                if n % 2 == 1:
                    dve.wait_ge(kv_psum, n + 1)
                    if kind == "k":
                        step(v.tensor_copy(m.kT[0:NOPE, i, j * 512:(j + 1) * 512], m.bank(7, NOPE)), kv_dve)
                    else:
                        step(v.tensor_copy(m.v_sb[:, i, :], m.bank(7)), kv_dve)
            for h in range(H):
                dve.wait_ge(sg_psum, h + 1)
                u = m.u_sg[:, :, h * HC:(h + 1) * HC]
                step(v.scalar_tensor_tensor(u, m.bank(h % 4).rearrange("p (t c) -> p t c", t=T), m.b_sp[:, h:h + 1],
                                            u, ALU.add, ALU.mult), sg_gated)

        @block.tensor
        def _(pe):
            mm, tr = nc.tensor.matmul, nc.tensor.transpose
            pe.wait_ge(w_sp_loaded, 32)
            for i in range(2):
                for h in range(4):
                    last = tr(m.bank(6 + i)[:, h * P:(h + 1) * P], m.w_sp[:, 4 * i + h, :], m.ident[:, :])
                last.then_inc(w_spT_psum, 1)
            for t in range(T + 1):
                if t < T:
                    if t >= 2:
                        pe.wait_ge(q_copied, 2 * (t - 1))
                    for i in range(2):
                        for k in range(QC):
                            last = mm(m.bank(2 * (t % 2) + i)[:, 0:half * QK], m.cqT[:, k, t * P:(t + 1) * P],
                                      m.w_uq[:, k, i * half * QK:(i + 1) * half * QK], start=(k == 0),
                                      stop=(k == QC - 1))
                    last.then_inc(q_psum, 1)
                if t >= 1:
                    pe.wait_ge(q_roped, t)
                    if t >= 2:
                        pe.wait_ge(qT_act, t - 1)
                        pe.wait_ge(qT_dve, t - 1)
                    for h in range(H):
                        last = tr(m.bank(4 + h // half, QK)[:, (h % half) * P:(h % half + 1) * P],
                                  q_row[:, (t - 1) % 2, h, :], m.ident[:, :])
                    last.then_inc(qT_psum, 1)
            pe.wait_ge(w_spT_copied, 2)
            for n, (kind, i, j) in enumerate(kv_jobs):
                if n >= 2:
                    pe.wait_ge(kv_act if n % 2 == 0 else kv_dve, n // 2)
                if kind == "k":
                    last = mm(m.bank(6 + n % 2, NOPE), m.w_ukv[:, i, 0:NOPE], m.ckvT[:, j * 512:(j + 1) * 512],
                              start=True, stop=True)
                else:
                    last = mm(m.bank(6 + n % 2), m.ckvT[:, i * P:(i + 1) * P], m.w_ukv[:, :, NOPE:NOPE + VH],
                              start=True, stop=True)
                last.then_inc(kv_psum, 1)
            pe.wait_ge(v_normed, 1)
            pe.wait_ge(w_spT_masked, 2)
            for h in range(H):
                if h >= 4:
                    pe.wait_ge(sg_gated, h - 3)
                mm(m.bank(h % 4), m.w_spT[:, h, :], m.v_sg[:, :, h * HC:(h + 1) * HC], start=True,
                   stop=True).then_inc(sg_psum, 1)


def attention(nc, m, w_out, w_out_loaded, w_out_scaled):
    with ExitStack() as ctx:
        sem = m.sem

        zeros_ready = sem("zeros_ready")
        cleared = sem("cleared")
        scores_psum = sem("scores_psum")
        max_ready = sem("max_ready")
        probs_ready = sem("probs_ready")
        pT_psum = sem("pT_psum")
        pT_act = sem("pT_act")
        pT_dve = sem("pT_dve")
        o_psum = sem("o_psum")
        o_ready = sem("o_ready")
        block = ctx.enter_context(nc.Block())
        jobs = [(h, i) for h in range(H) for i in range(T)]
        N = len(jobs)
        nmax, rsum, rinv = m.stat[:, 96:100], m.stat[:, 100:104], m.stat[:, 104:108]

        def wide(n):
            return sum(i >= 4 for _, i in jobs[:n])

        @block.sync
        def _(sp):
            wo = w_out.rearrange("l (k p) n -> p (l k) n", p=P)
            for k in range(0, KD, 4):
                sp.dma_start(m.w_out[:, k:k + 4, :], wo[:, k:k + 4, :]).then_inc(w_out_loaded, 16)
            sp.wait_ge(zeros_ready, 1)
            sp.dma_start(m.tok_list.rearrange("(p c) o -> p (c o)", p=P),
                         m.junk[:, 0:TAB * CT // P].bitcast(I32)).then_inc(cleared, 16)
            spare = m.y_rows[E * CT:MAX_ITEMS * CT, :].rearrange("(c p) d -> p c d", p=P)
            n_spare = MORE * CT // P
            for c in range(0, n_spare, 6):
                sp.dma_start(spare[:, c:c + 6, :], m.junk[:, :].unsqueeze(1).broadcast_to([P, 6, D])
                             ).then_inc(cleared, 16)
            sp.wait_ge(cleared, 16 + 16 * len(range(0, n_spare, 6)))

        @block.gpsimd
        def _(pool):
            g = nc.gpsimd
            step = Chain(m, pool, m.pool_step)
            step(g.memset(m.junk[:, :], 0.0), zeros_ready)
            pool.wait_ge(w_out_loaded, 32)
            for k in range(KD):
                step(g.tensor_scalar(m.w_out[:, k, :], m.w_out[:, k, :], m.g_mix[:, k:k + 1], None, ALU.mult),
                     w_out_scaled)

        @block.scalar
        def _(act):
            s = nc.scalar
            step = Chain(m, act, m.act_step)
            for n in range(N + 1):
                if n < N:
                    w = (jobs[n][1] + 1) * P
                    act.wait_ge(max_ready, n + 1)
                    if n >= 2:
                        act.wait_ge(pT_psum, n - 1)
                    if n >= 4:
                        act.wait_ge(o_ready, n - 3)
                    step(s.activation(m.probs[:, n % 2, 0:w], m.ps[:, 2 * (n % 2):2 * (n % 2) + 2, :].rearrange(
                        "p b c -> p (b c)")[:, 0:w], ACT.Exp, bias=nmax[:, n % 4:n % 4 + 1], scale=SCALE,
                        accum_out=rsum[:, n % 4:n % 4 + 1]), probs_ready)
                if n >= 1:
                    l = n - 1
                    w = min(4, jobs[l][1] + 1) * P
                    act.wait_ge(pT_psum, l + 1)
                    if l >= 2:
                        act.wait_ge(o_psum, l - 1)
                    step(s.activation(m.probsT[:, l % 2, 0:w], m.bank(4)[:, 0:w], ACT.Copy), pT_act)

        @block.vector
        def _(dve):
            v = nc.vector
            step = Chain(m, dve, m.dve_step)
            for n in range(N + 2):
                if n < N:
                    i = jobs[n][1]
                    w = (i + 1) * P
                    s = m.ps[:, 2 * (n % 2):2 * (n % 2) + 2, :].rearrange("p b c -> p (b c)")
                    dve.wait_ge(scores_psum, n + 1)
                    if n >= 4:
                        dve.wait_ge(probs_ready, n - 3)
                    step(v.tensor_tensor(s[:, w - P:w], s[:, w - P:w], m.causal[:, :], ALU.add))
                    step(v.reduce_max(nmax[:, n % 4:n % 4 + 1], s[:, 0:w], AX.X))
                    step(v.tensor_scalar(nmax[:, n % 4:n % 4 + 1], nmax[:, n % 4:n % 4 + 1], -SCALE, None, ALU.mult),
                         max_ready)
                l = n - 1
                if 0 <= l < N and jobs[l][1] >= 4:
                    w = (jobs[l][1] - 3) * P
                    dve.wait_ge(pT_psum, l + 1)
                    if l >= 2:
                        dve.wait_ge(o_psum, l - 1)
                    step(v.tensor_copy(m.probsT[:, l % 2, 512:512 + w], m.bank(5)[:, 0:w]), pT_dve)
                l = n - 2
                if l >= 0:
                    h, i = jobs[l]
                    dve.wait_ge(probs_ready, l + 1)
                    step(v.reciprocal(rinv[:, l % 4:l % 4 + 1], rsum[:, l % 4:l % 4 + 1]))
                    dve.wait_ge(o_psum, l + 1)
                    step(v.tensor_scalar(m.o_sb[:, i, h * VH:(h + 1) * VH], m.bank(6 + l % 2)[:, 0:VH],
                                         rinv[:, l % 4:l % 4 + 1], None, ALU.mult), o_ready)

        @block.tensor
        def _(pe):
            mm, tr = nc.tensor.matmul, nc.tensor.transpose
            for n in range(-1, N + 1):
                if n + 1 < N:
                    l = n + 1
                    h, i = jobs[l]
                    if l >= 2:
                        pe.wait_ge(probs_ready, l - 1)
                    for b in range(i // 4 + 1):
                        w = min(512, (i + 1) * P - 512 * b)
                        last = mm(m.bank(2 * (l % 2) + b)[:, 0:w], m.qT[:, h, i * P:(i + 1) * P],
                                  m.kT[:, h, 512 * b:512 * b + w], start=True, stop=True)
                    last.then_inc(scores_psum, 1)
                if 0 <= n < N:
                    i = jobs[n][1]
                    pe.wait_ge(probs_ready, n + 1)
                    if n >= 1:
                        pe.wait_ge(pT_act, n)
                    if wide(n):
                        pe.wait_ge(pT_dve, wide(n))
                    for j in range(i + 1):
                        last = tr(m.bank(4 + j // 4)[:, (j % 4) * P:(j % 4 + 1) * P],
                                  m.probs[:, n % 2, j * P:(j + 1) * P], m.ident[:, :])
                    last.then_inc(pT_psum, 1)
                if n >= 1:
                    l = n - 1
                    h, i = jobs[l]
                    pe.wait_ge(pT_act, l + 1)
                    if wide(l + 1):
                        pe.wait_ge(pT_dve, wide(l + 1))
                    if l >= 2:
                        pe.wait_ge(o_ready, l - 1)
                    for j in range(i + 1):
                        last = mm(m.bank(6 + l % 2)[:, 0:VH], m.probsT[:, l % 2, j * P:(j + 1) * P],
                                  m.v_sb[:, j, h * VH:(h + 1) * VH], start=(j == 0), stop=(j == i))
                    last.then_inc(o_psum, 1)


def output_and_router(nc, m, x, w_out_scaled, attn_post_g, ffn_pre_g, w_router):
    with ExitStack() as ctx:
        sem = m.sem

        gains_loaded = sem("gains_loaded")
        iotas_ready = sem("iotas_ready")
        mix_squares = sem("mix_squares")
        mix_mean = sem("mix_mean")
        mix_root = sem("mix_root")
        mix_normed = sem("mix_normed")
        mixT_psum = sem("mixT_psum")
        mixT_act = sem("mixT_act")
        mixT_dve = sem("mixT_dve")
        y_psum = sem("y_psum")
        y_squares = sem("y_squares")
        y_mean = sem("y_mean")
        y_root = sem("y_root")
        y_scaled = sem("y_scaled")
        x1_ready = sem("x1_ready")
        x1_squares = sem("x1_squares")
        x1_mean = sem("x1_mean")
        x1_root = sem("x1_root")
        h_ready = sem("h_ready")
        h_stored = [sem(f"h_stored{b}") for b in range(2)]
        hT_psum = sem("hT_psum")
        hT_act = sem("hT_act")
        hT_dve = sem("hT_dve")
        logits_psum = sem("logits_psum")
        logits_ready = sem("logits_ready")
        tops_ready = sem("tops_ready")
        exps_ready = sem("exps_ready")
        taken_ready = sem("taken_ready")
        ranks_psum = sem("ranks_psum")
        slots_ready = sem("slots_ready")
        list_written = sem("list_written")
        block = ctx.enter_context(nc.Block())
        mix_s = m.stat[:, 0:2 * T]
        ys, xs = m.stat[:, 16:20], m.stat[:, 20:24]
        top8 = m.scr[:, 0:64].rearrange("p (t k) -> p t k", t=T)
        idx8 = m.scr[:, 64:128].bitcast(U32).rearrange("p (t k) -> p t k", t=T)
        idxf = m.scr[:, 128:160].rearrange("p (t k) -> p t k", t=T)
        shifted = m.scr[:, 160:192].rearrange("p (t k) -> p t k", t=T)
        gate_sum = m.scr[:, 192:200]
        slotf = m.scr[:, 200:232].rearrange("p (t k) -> p t k", t=T)
        expert_no = m.scr[:, 256:288]
        first_slot = m.scr[:, 288:320]
        picked = m.scr[:, 1024:2048].rearrange("p (t k e) -> p t k e", t=T, k=TOPK)
        cnt, more, ends, jump = (m.scr[:, 320 + i * E:320 + (i + 1) * E] for i in range(4))
        number = m.scr[:, 448:448 + MORE + 1]
        tab = m.scr[0:1, 512:512 + TAB + 1]
        passed = m.scr[0:1, 2048:2048 + (MORE + 1) * E].rearrange("p (j e) -> p j e", e=E)

        @block.sync
        def _(sp):
            sp.dma_start(m.post_g, on_all(attn_post_g)).then_inc(gains_loaded, 16)
            sp.dma_start(m.ffn_g, on_all(ffn_pre_g)).then_inc(gains_loaded, 16)
            x_t = x.rearrange("b (t p) d -> p (b t) d", p=P)
            for t in range(T):
                sp.dma_start(m.x_sb[:, t, :], x_t[:, t, :]).then_inc(m.x_loaded[t], 16)
            sp.dma_start(m.w_router, w_router.rearrange("l (k p) e -> p (l k) e", p=P)).then_inc(gains_loaded, 16)
            h_t = m.h_rows.rearrange("(t p) d -> p t d", p=P)
            for t in range(T):
                sp.wait_ge(h_ready, t + 1)
                sp.dma_start(h_t[:, t, :], m.h_row[:, t % 2, :]).then_inc(h_stored[t % 2], 16)
            for b in range(2):
                sp.wait_ge(h_stored[b], 16 * (T // 2))

        @block.gpsimd
        def _(pool):
            g = nc.gpsimd
            step = Chain(m, pool, m.pool_step)
            exact = dict(allow_small_or_imprecise_dtypes=True)
            step(g.iota(expert_no, pattern=[[1, E]], base=0, channel_multiplier=0, **exact))
            step(g.iota(first_slot, pattern=[[CT, E]], base=0, channel_multiplier=0, **exact))
            step(g.iota(number, pattern=[[1, MORE + 1]], base=0, channel_multiplier=0, **exact), iotas_ready)
            pool.wait_ge(slots_ready, 1)
            for t in range(T):
                for k in range(TOPK):
                    pool.indirect_dma_start(m.tok_list, bass.IndirectOffsetOnAxis(m.slots[:, t, k:k + 1], 0),
                                            m.tokid[:, t:t + 1], None).then_inc(list_written, 16)
            pool.wait_ge(list_written, 16 * T * TOPK)

        @block.scalar
        def _(act):
            s = nc.scalar
            step = Chain(m, act, m.act_step)
            for t in range(T):
                step(s.activation(m.junk[:, 0:512], m.o_sb[:, t, :], ACT.Square, accum_out=mix_s[:, t:t + 1]),
                     mix_squares)
                step(s.activation(m.junk[:, 512:1024], m.u_sg[:, t, :], ACT.Square,
                                  accum_out=mix_s[:, T + t:T + t + 1]), mix_squares)
            act.wait_ge(mix_mean, 1)
            step(s.activation(mix_s, mix_s, ACT.Sqrt), mix_root)
            for t in range(T):
                act.wait_ge(mixT_psum, t + 1)
                step(s.activation(m.mixT[:, 0:4, t * P:(t + 1) * P], m.bank(0).rearrange("p (k s) -> p k s", k=4),
                                  ACT.Copy), mixT_act)
            for t in range(T + 1):
                if t < T:
                    act.wait_ge(y_psum, t + 1)
                    b = 2 + 2 * (t % 2)
                    step(s.activation(m.junk[:, :], m.ps[:, b:b + 2, :].rearrange("p b c -> p (b c)"), ACT.Square,
                                      accum_out=ys[:, 0:1]), y_squares)
                    act.wait_ge(y_mean, t + 1)
                    step(s.activation(ys[:, 1:2], ys[:, 1:2], ACT.Sqrt), y_root)
                    act.wait_ge(x1_ready, t + 1)
                    step(s.activation(m.junk[:, :], m.x_sb[:, t, :], ACT.Square, accum_out=xs[:, 0:1]), x1_squares)
                    act.wait_ge(x1_mean, t + 1)
                    step(s.activation(xs[:, 1:2], xs[:, 1:2], ACT.Sqrt), x1_root)
                    act.wait_ge(hT_psum, t + 1)
                    if t >= 1:
                        act.wait_ge(logits_psum, t)
                    step(s.activation(m.hT[:, 0:4, :], m.bank(6).rearrange("p (k s) -> p k s", k=4), ACT.Copy),
                         hT_act)
            act.wait_ge(tops_ready, 1)
            step(s.activation(shifted, shifted, ACT.Exp), exps_ready)

        @block.vector
        def _(dve):
            v = nc.vector
            step = Chain(m, dve, m.dve_step)
            dve.wait_ge(mix_squares, 2 * T)
            step(v.tensor_scalar(mix_s, mix_s, 1.0 / SGW, EPS, ALU.mult, ALU.add), mix_mean)
            dve.wait_ge(mix_root, 1)
            step(v.reciprocal(mix_s, mix_s))
            for t in range(T + 1):
                if t < T:
                    step(v.tensor_scalar(m.o_sb[:, t, :], m.o_sb[:, t, :], mix_s[:, t:t + 1], None, ALU.mult))
                    step(v.tensor_scalar(m.u_sg[:, t, :], m.u_sg[:, t, :], mix_s[:, T + t:T + t + 1], None, ALU.mult),
                         mix_normed)
                if t >= 1:
                    dve.wait_ge(mixT_psum, t)
                    step(v.tensor_copy(m.mixT[:, 4:8, (t - 1) * P:t * P], m.bank(1).rearrange(
                        "p (k s) -> p k s", k=4)), mixT_dve)
            dve.wait_ge(gains_loaded, 48)
            for t in range(T):
                b = 2 + 2 * (t % 2)
                dve.wait_ge(y_squares, t + 1)
                step(v.tensor_scalar(ys[:, 1:2], ys[:, 0:1], 1.0 / D, EPS, ALU.mult, ALU.add), y_mean)
                dve.wait_ge(y_root, t + 1)
                step(v.reciprocal(ys[:, 2:3], ys[:, 1:2]))
                y = m.y_row[:, 0, :]
                step(v.scalar_tensor_tensor(y, m.ps[:, b:b + 2, :].rearrange("p b c -> p (b c)"), ys[:, 2:3],
                                            m.post_g, ALU.mult, ALU.mult), y_scaled)
                dve.wait_ge(m.x_loaded[t], 32)
                step(v.tensor_tensor(m.x_sb[:, t, :], m.x_sb[:, t, :], y, ALU.add), x1_ready)
                dve.wait_ge(x1_squares, t + 1)
                step(v.tensor_scalar(xs[:, 1:2], xs[:, 0:1], 1.0 / D, EPS, ALU.mult, ALU.add), x1_mean)
                dve.wait_ge(x1_root, t + 1)
                step(v.reciprocal(xs[:, 2:3], xs[:, 1:2]))
                if t >= 2:
                    dve.wait_ge(h_stored[t % 2], 16 * (t // 2))
                step(v.scalar_tensor_tensor(m.h_row[:, t % 2, :], m.x_sb[:, t, :], xs[:, 2:3], m.ffn_g, ALU.mult,
                                            ALU.mult), h_ready)
                dve.wait_ge(hT_psum, t + 1)
                if t >= 1:
                    dve.wait_ge(logits_psum, t)
                step(v.tensor_copy(m.hT[:, 4:8, :], m.bank(7).rearrange("p (k s) -> p k s", k=4)), hT_dve)
                dve.wait_ge(logits_psum, t + 1)
                step(v.tensor_tensor(m.logits[:, t, :], m.bank(0)[:, 0:E], m.b_r[:, :], ALU.add), logits_ready)
                step(v.max(top8[:, t, :], m.logits[:, t, :]))
                step(v.max_index(idx8[:, t, :], top8[:, t, :], m.logits[:, t, :]))
            step(v.tensor_tensor(shifted, top8[:, :, 0:TOPK], top8[:, :, 0:1].broadcast_to([P, T, TOPK]),
                                 ALU.subtract), tops_ready)
            step(v.tensor_copy(idxf, idx8[:, :, 0:TOPK]))
            dve.wait_ge(exps_ready, 1)
            step(v.tensor_reduce(out=gate_sum, in_=shifted, op=ALU.add, axis=AX.X))
            step(v.reciprocal(gate_sum, gate_sum))
            step(v.tensor_tensor(m.gates[:, :, :], shifted, gate_sum.unsqueeze(2).broadcast_to([P, T, TOPK]),
                                 ALU.mult))
            dve.wait_ge(iotas_ready, 1)
            for t in range(T):
                step(v.tensor_tensor(m.hot[:, t, :, :], expert_no.unsqueeze(1).broadcast_to([P, TOPK, E]),
                                     idxf[:, t, :].unsqueeze(2).broadcast_to([P, TOPK, E]), ALU.is_equal))
            step(v.tensor_tensor(m.taken, m.hot[:, :, 0, :], m.hot[:, :, 1, :], ALU.add))
            step(v.tensor_tensor(m.taken, m.taken, m.hot[:, :, 2, :], ALU.add))
            step(v.tensor_tensor(m.taken, m.taken, m.hot[:, :, 3, :], ALU.add), taken_ready)
            dve.wait_ge(ranks_psum, 2)
            step(v.tensor_copy(cnt, m.bank(3)[:, 0:E]))
            step(v.tensor_scalar(more, cnt, float(CT), None, ALU.is_gt))
            for c in range(2, SEQ // CT):
                step(v.scalar_tensor_tensor(more, cnt, float(c * CT), more, ALU.is_gt, ALU.add))
            step(v.tensor_tensor_scan(ends, m.ones[:, 0:E], more, 0.0, ALU.mult, ALU.add))
            step(v.tensor_tensor(jump, ends, more, ALU.subtract))
            step(v.tensor_scalar(jump, jump, float(E - 1), float(CT), ALU.add, ALU.mult))
            step(v.tensor_tensor(jump, jump, first_slot, ALU.subtract))
            ranks = m.bank(2)[:, 0:T * E].rearrange("p (t e) -> p t e", t=T)
            step(v.scalar_tensor_tensor(m.place, ranks, float(CT), jump.unsqueeze(1).broadcast_to([P, T, E]),
                                        ALU.is_ge, ALU.mult))
            step(v.tensor_tensor(m.place, m.place, ranks, ALU.add))
            step(v.tensor_tensor(m.place, m.place, first_slot.unsqueeze(1).broadcast_to([P, T, E]), ALU.add))
            for t in range(T):
                step(v.tensor_tensor(picked[:, t, :, :], m.hot[:, t, :, :],
                                     m.place[:, t, :].unsqueeze(1).broadcast_to([P, TOPK, E]), ALU.mult))
            step(v.tensor_reduce(out=slotf, in_=picked, op=ALU.add, axis=AX.X))
            step(v.tensor_copy(m.slots[:, :, :], slotf), slots_ready)
            over = [1, MORE + 1, E]
            step(v.tensor_tensor(passed, ends[0:1, :].unsqueeze(1).broadcast_to(over),
                                 number[0:1, :].unsqueeze(2).broadcast_to(over), ALU.is_le))
            step(v.tensor_copy(tab[:, 0:E], expert_no[0:1, :]))
            step(v.tensor_reduce(out=tab[:, E:TAB], in_=passed, op=ALU.add, axis=AX.X))
            step(v.tensor_scalar(tab[:, E:TAB], tab[:, E:TAB], float(E - 1), None, ALU.min))
            step(v.tensor_scalar(tab[:, TAB:TAB + 1], ends[0:1, E - 1:E], float(E), None, ALU.add))
            step(v.tensor_copy(m.items[:, :], tab))

        @block.tensor
        def _(pe):
            mm, tr = nc.tensor.matmul, nc.tensor.transpose
            for t in range(T):
                pe.wait_ge(mix_normed, t + 1)
                if t >= 1:
                    pe.wait_ge(mixT_act, t)
                    pe.wait_ge(mixT_dve, t)
                for k in range(KD):
                    src = m.o_sb if k < 4 else m.u_sg
                    last = tr(m.bank(k // 4)[:, (k % 4) * P:(k % 4 + 1) * P],
                              src[:, t, (k % 4) * P:(k % 4 + 1) * P], m.ident[:, :])
                last.then_inc(mixT_psum, 1)
            pe.wait_ge(mixT_act, T)
            pe.wait_ge(mixT_dve, T)
            pe.wait_ge(w_out_scaled, KD)
            pe.wait_ge(gains_loaded, 48)
            for t in range(T + 1):
                if t < T:
                    if t >= 2:
                        pe.wait_ge(y_scaled, t - 1)
                    for k in range(KD):
                        for j in range(2):
                            last = mm(m.bank(2 + 2 * (t % 2) + j), m.mixT[:, k, t * P:(t + 1) * P],
                                      m.w_out[:, k, j * 512:(j + 1) * 512], start=(k == 0), stop=(k == KD - 1))
                    last.then_inc(y_psum, 1)
                if t >= 1:
                    pe.wait_ge(h_ready, t)
                    if t >= 2:
                        pe.wait_ge(hT_act, t - 1)
                        pe.wait_ge(hT_dve, t - 1)
                    for k in range(KD):
                        last = tr(m.bank(6 + k // 4)[:, (k % 4) * P:(k % 4 + 1) * P],
                                  m.h_row[:, (t - 1) % 2, k * P:(k + 1) * P], m.ident[:, :])
                    last.then_inc(hT_psum, 1)
                    pe.wait_ge(hT_act, t)
                    pe.wait_ge(hT_dve, t)
                    if t >= 2:
                        pe.wait_ge(logits_ready, t - 1)
                    for k in range(KD):
                        last = mm(m.bank(0)[:, 0:E], m.hT[:, k, :], m.w_router[:, k, :], start=(k == 0),
                                  stop=(k == KD - 1))
                    last.then_inc(logits_psum, 1)
            pe.wait_ge(taken_ready, 1)
            for t in range(T):
                for j in range(t + 1):
                    last = mm(m.bank(2)[:, t * E:(t + 1) * E], m.ones[:, :] if j < t else m.before[:, :],
                              m.taken[:, j, :], start=(j == 0), stop=(j == t))
            last.then_inc(ranks_psum, 1)
            for j in range(T):
                last = mm(m.bank(3)[:, 0:E], m.ones[:, :], m.taken[:, j, :], start=(j == 0), stop=(j == T - 1))
            last.then_inc(ranks_psum, 1)


def experts(nc, m, w_gate_up, w_down):
    with ExitStack() as ctx:
        sem = m.sem

        unit_loaded = [sem(f"unit_loaded{u}") for u in range(N_UNITS)]
        index_loaded = sem("index_loaded")
        rows_gathered = sem("rows_gathered")
        gather_started = sem("gather_started")
        rowsT_psum = sem("rowsT_psum")
        rowsT_ready = sem("rowsT_ready")
        bias_ready = sem("bias_ready")
        gate_up_psum = sem("gate_up_psum")
        gate_ready = sem("gate_ready")
        gate_up_read = sem("gate_up_read")
        dve_step = sem("dve_step5")
        sigmoid_ready = sem("sigmoid_ready")
        act_ready = sem("act_ready")
        down_psum = sem("down_psum")
        down_read = sem("down_read")
        yT_psum = sem("yT_psum")
        y_read = sem("y_read")
        y_stored = sem("y_stored")
        y_free = sem("y_free")
        block = ctx.enter_context(nc.Block())

        wk = m.work
        rowsT = wk[:, 0:2048].rearrange("p (k s) -> p k s", k=KD)
        act_T = wk[:, 2048:4096].rearrange("p (k s) -> p k s", k=KF)
        rows = wk[:, 4096:6144].rearrange("p (c d) -> p c d", c=CH)
        y_out = wk[:, 6144:8192].rearrange("p (c d) -> p c d", c=CH)
        gate = wk[:, 8192:8704].rearrange("p (b s) -> p b s", b=2)
        up = wk[:, 8704:9216].rearrange("p (b s) -> p b s", b=2)
        sig = wk[:, 9216:9728].rearrange("p (b s) -> p b s", b=2)
        yT = wk[:, 9728:10240].rearrange("p (b s) -> p b s", b=2)
        n_at = TAB

        def load_unit(eng, u, expert):
            if u < GU_UNITS:
                src = w_gate_up.rearrange("l e (k p) n -> (l e) p k n", p=P)
                c = (u // 2) * 256 + (u % 2) * F
            else:
                src = w_down.rearrange("l e (k p) n -> (l e) p k n", p=P)
                c = (u - GU_UNITS) * 256
            src = src[bass.ds(expert, 1), :, :, c:c + 256].rearrange("e p k n -> (e p) k n")
            eng.dma_start(m.unit[u], src).then_inc(unit_loaded[u], 16)

        @block.sync
        def _(sp):
            for u in range(N_UNITS):
                load_unit(sp, u, 0)
            n_items = sp.value_load(m.items[0:1, n_at:n_at + 1], min_val=E, max_val=MAX_ITEMS)
            with sp.Fori(0, MAX_ITEMS) as i:
                with sp.If(i + 1 < n_items):
                    expert = sp.value_load(m.items[0:1, bass.ds(i + 1, 1)], min_val=0, max_val=E - 1)
                    for u in range(N_UNITS):
                        if u < GU_UNITS:
                            sp.wait_ge(gate_up_psum, i * KF + 2 * (u // 2) + 2)
                        else:
                            sp.wait_ge(down_psum, i * KD + 2 * (u - GU_UNITS) + 2)
                        load_unit(sp, u, expert)

        @block.gpsimd
        def _(pool):
            n_items = pool.value_load(m.items[0:1, n_at:n_at + 1], min_val=E, max_val=MAX_ITEMS)

            def load_index(first):
                pool.dma_start(m.idx_now[:, 0, :], m.tok_list[bass.ds(first, CT), :].rearrange(
                    "(c p) o -> p (c o)", p=P)).then_inc(index_loaded, 16)

            load_index(0)
            pool.wait_ge(index_loaded, 16)
            for c in range(CH):
                pool.indirect_dma_start(rows[:, c, :], None, m.h_rows,
                                        bass.IndirectOffsetOnAxis(m.idx_now[:, 0, c:c + 1], 0)
                                        ).then_inc(rows_gathered, 16)
            with pool.Fori(0, MAX_ITEMS) as i:
                with pool.If(i < n_items):
                    pool.wait_ge(rows_gathered, i * (16 * CH) + 16 * CH)
                    load_index(i * CT + CT)
                    pool.wait_ge(index_loaded, i * 16 + 32)
                    pool.wait_ge(rowsT_psum, i * 4 + 4)
                    pool.sem_inc(gather_started, 1)
                    for c in range(CH):
                        pool.indirect_dma_start(rows[:, c, :], None, m.h_rows,
                                                bass.IndirectOffsetOnAxis(m.idx_now[:, 0, c:c + 1], 0)
                                                ).then_inc(rows_gathered, 16)
            pool.wait_ge(rows_gathered, n_items * (16 * CH) + 16 * CH)

        @block.scalar
        def _(act):
            s = nc.scalar
            n_items = act.value_load(m.items[0:1, n_at:n_at + 1], min_val=E, max_val=MAX_ITEMS)

            def copy_rowsT(base):
                for f in range(4):
                    act.wait_ge(rowsT_psum, base + (f + 1))
                    s.activation(rowsT[:, 2 * f:2 * f + 2, :], m.bank(f % 2).rearrange("p (k s) -> p k s", k=2),
                                 ACT.Copy).then_inc(rowsT_ready, 1)

            act.sem_inc(down_read, 2)
            act.sem_inc(y_free, 1)
            copy_rowsT(0)
            with act.Fori(0, MAX_ITEMS) as i:
                with act.If(i < n_items):
                    for f in range(KF):
                        act.wait_ge(gate_ready, i * KF + f + 1)
                        s.activation(sig[:, f % 2, :], gate[:, f % 2, :], ACT.Sigmoid,
                                     scale=ALPHA).then_inc(sigmoid_ready, 1)
                    copy_rowsT(i * 4 + 4)
                    for d in range(KD):
                        act.wait_ge(down_psum, i * KD + d + 1)
                        s.activation(yT[:, d % 2, :], m.bank(6 + d % 2)[:, 0:CT], ACT.Identity,
                                     bias=m.bias_now[:, 2 * KF + d:2 * KF + d + 1]).then_inc(down_read, 1)
                    act.wait_ge(y_read, i * 4 + 5)
                    act.dma_start(m.y_rows[bass.ds(i * CT, CT), :].rearrange("(c p) d -> p c d", p=P),
                                  y_out).then_inc(y_stored, 16)
                    act.wait_ge(y_stored, i * 16 + 16)
                    act.sem_inc(y_free, 1)

        @block.vector
        def _(dve):
            v = nc.vector
            n_items = dve.value_load(m.items[0:1, n_at:n_at + 1], min_val=E, max_val=MAX_ITEMS)
            dve.sem_inc(gate_up_read, 2)
            dve.sem_inc(y_read, 1)
            with dve.Fori(0, MAX_ITEMS) as i:
                with dve.If(i < n_items):
                    expert = dve.value_load(m.items[0:1, bass.ds(i, 1)], min_val=0, max_val=E - 1)
                    dve.wait_ge(down_read, i * KD + 2)
                    v.tensor_copy(m.bias_now[:, :], m.bias_cols[:, :, bass.ds(expert, 1)].rearrange(
                        "p c e -> p (c e)")).then_inc(bias_ready, 1)
                    dve.wait_ge(bias_ready, i + 1)
                    for f in range(KF + 1):
                        if f < KF:
                            dve.wait_ge(gate_up_psum, i * KF + f + 1)
                            v.tensor_scalar(gate[:, f % 2, :], m.bank(2 + f % 2)[:, 0:CT], m.bias_now[:, f:f + 1],
                                            LIMIT, ALU.add, ALU.min).then_inc(gate_ready, 1)
                            v.tensor_scalar(up[:, f % 2, :], m.bank(4 + f % 2)[:, 0:CT],
                                            m.bias_now[:, KF + f:KF + f + 1], LIMIT, ALU.add,
                                            ALU.min).then_inc(gate_up_read, 1)
                            dve.wait_ge(gate_up_read, i * KF + f + 3)
                        if f >= 1:
                            b = (f - 1) % 2
                            v.tensor_scalar(up[:, b, :], up[:, b, :], -LIMIT, 1.0, ALU.max,
                                            ALU.add).then_inc(dve_step, 1)
                            dve.wait_ge(sigmoid_ready, i * KF + f)
                            v.tensor_tensor(gate[:, b, :], gate[:, b, :], sig[:, b, :],
                                            ALU.mult).then_inc(dve_step, 1)
                            dve.wait_ge(dve_step, i * (2 * KF) + 2 * f)
                            v.tensor_tensor(act_T[:, f - 1, :], gate[:, b, :], up[:, b, :],
                                            ALU.mult).then_inc(act_ready, 1)
                            dve.wait_ge(act_ready, i * KF + f)
                    for part in range(2):
                        dve.wait_ge(yT_psum, i * KD + 4 * part + 4)
                        if part == 0:
                            dve.wait_ge(y_free, i + 1)
                        for c in range(CH):
                            v.tensor_copy(y_out[:, c, part * 512:(part + 1) * 512],
                                          m.bank(c)).then_inc(y_read, 1)

        @block.tensor
        def _(pe):
            mm, tr = nc.tensor.matmul, nc.tensor.transpose
            n_items = pe.value_load(m.items[0:1, n_at:n_at + 1], min_val=E, max_val=MAX_ITEMS)

            def transpose_rows(gathered, read, copied):
                pe.wait_ge(rows_gathered, gathered)
                pe.wait_ge(y_read, read)
                for f in range(4):
                    if f >= 2:
                        pe.wait_ge(rowsT_ready, copied + (f - 1))
                    for k in range(2):
                        for c in range(CH):
                            last = tr(m.bank(f % 2)[:, k * CT + c * P:k * CT + (c + 1) * P],
                                      rows[:, c, (2 * f + k) * P:(2 * f + k + 1) * P], m.ident[:, :])
                    last.then_inc(rowsT_psum, 1)

            transpose_rows(16 * CH, 1, 0)
            with pe.Fori(0, MAX_ITEMS) as i:
                with pe.If(i < n_items):
                    pe.wait_ge(rowsT_ready, i * 4 + 4)
                    for f in range(KF):
                        if f % 2 == 0:
                            pe.wait_ge(unit_loaded[f], i * 16 + 16)
                            pe.wait_ge(unit_loaded[f + 1], i * 16 + 16)
                        pe.wait_ge(gate_up_read, i * KF + f + 1)
                        for half in range(2):
                            w = m.unit[2 * (f // 2) + half]
                            for k in range(KD):
                                last = mm(m.bank(2 + 2 * half + f % 2)[:, 0:CT], w[:, k, (f % 2) * P:(f % 2 + 1) * P],
                                          rowsT[:, k, :], start=(k == 0), stop=(k == KD - 1))
                        last.then_inc(gate_up_psum, 1)
                    transpose_rows(i * (16 * CH) + 32 * CH, i * 4 + 1, i * 4 + 4)
                    for d in range(KD + 1):
                        if d < KD:
                            w = m.unit[GU_UNITS + d // 2]
                            if d % 2 == 0:
                                pe.wait_ge(unit_loaded[GU_UNITS + d // 2], i * 16 + 16)
                            pe.wait_ge(down_read, i * KD + d + 1)
                            for k in range(KF):
                                if d == 0:
                                    pe.wait_ge(act_ready, i * KF + k + 1)
                                last = mm(m.bank(6 + d % 2)[:, 0:CT], w[:, k, (d % 2) * P:(d % 2 + 1) * P],
                                          act_T[:, k, :], start=(k == 0), stop=(k == KF - 1))
                            last.then_inc(down_psum, 1)
                        if d >= 1:
                            e = d - 1
                            pe.wait_ge(down_read, i * KD + e + 3)
                            if e == 0:
                                pe.wait_ge(rowsT_ready, i * 4 + 8)
                            if e == 4:
                                pe.wait_ge(y_read, i * 4 + 3)
                            for c in range(CH):
                                last = tr(m.bank(c)[:, (e % 4) * P:(e % 4 + 1) * P],
                                          yT[:, e % 2, c * P:(c + 1) * P], m.ident[:, :])
                            last.then_inc(yT_psum, 1)


def combine_and_embed(nc, m, p, ffn_post_g, w_ple_gate, b_ple_gate, w_ple_proj, ple_norm_g, out):
    with ExitStack() as ctx:
        sem = m.sem

        weights_loaded = sem("weights_loaded")
        rows_gathered = [sem(f"choices_gathered{b}") for b in range(2)]
        rows_used = sem("rows_used")
        y_ready = sem("y_ready")
        y_squares = sem("y_squares6")
        y_mean = sem("y_mean6")
        y_root = sem("y_root6")
        x2_ready = sem("x2_ready")
        inT_psum = sem("inT_psum")
        inT_act = sem("inT_act")
        inT_dve = sem("inT_dve")
        gate_psum = sem("gate_psum")
        gate_biased = sem("gate_biased")
        gate_done = sem("gate_done")
        gated = sem("gated")
        gated_squares = sem("gated_squares")
        gated_mean = sem("gated_mean")
        gated_root = sem("gated_root")
        out_ready = sem("out_ready")
        out_stored = sem("out_stored")
        block = ctx.enter_context(nc.Block())
        rg, wk = m.ring, m.work
        w_gate = rg[:, 0:8192].rearrange("p (k n) -> p k n", k=KD)
        w_proj = rg[:, 8192:10240].rearrange("p (k n) -> p k n", k=KP)
        p_sb = rg[:, 10240:12288].rearrange("p (t d) -> p t d", t=T)
        post_g, gate_b, norm_g = (rg[:, 12288 + i * D:12288 + (i + 1) * D] for i in range(3))
        inT = rg[:, 15360:15360 + 1280].rearrange("p (k s) -> p k s", k=KD + KP)
        gate_row = rg[:, 16640:17664]
        y_acc = rg[:, 17664:18688]
        choices = wk[:, 0:8192].rearrange("p (b k d) -> p b k d", b=2, k=TOPK)
        prod = wk[:, 8192:16384].rearrange("p (t d) -> p t d", t=T)
        ss = m.stat[:, 0:4]
        gs = m.stat[:, 8:16]

        @block.sync
        def _(sp):
            sp.dma_start(post_g, on_all(ffn_post_g)).then_inc(weights_loaded, 16)
            sp.dma_start(gate_b, on_all(b_ple_gate)).then_inc(weights_loaded, 16)
            sp.dma_start(norm_g, on_all(ple_norm_g)).then_inc(weights_loaded, 16)
            sp.dma_start(p_sb, p.rearrange("l b (t p) d -> p (l b t) d", p=P)).then_inc(weights_loaded, 16)
            sp.dma_start(w_gate, w_ple_gate.rearrange("l (k p) n -> p (l k) n", p=P)).then_inc(weights_loaded, 16)
            sp.dma_start(w_proj, w_ple_proj.rearrange("l (k p) n -> p (l k) n", p=P)).then_inc(weights_loaded, 16)
            out_t = out.rearrange("b (t p) d -> p (b t) d", p=P)
            for t in range(T):
                sp.wait_ge(out_ready, t + 1)
                sp.dma_start(out_t[:, t, :], m.x_sb[:, t, :]).then_inc(out_stored, 16)
            sp.wait_ge(out_stored, 16 * T)

        @block.gpsimd
        def _(pool):
            for t in range(T):
                if t >= 2:
                    pool.wait_ge(rows_used, t - 1)
                for k in range(TOPK):
                    pool.indirect_dma_start(choices[:, t % 2, k, :], None, m.y_rows,
                                            bass.IndirectOffsetOnAxis(m.slots[:, t, k:k + 1], 0)
                                            ).then_inc(rows_gathered[t % 2], 16)

        @block.scalar
        def _(act):
            s = nc.scalar
            step = Chain(m, act, m.act_step)
            for t in range(T):
                act.wait_ge(y_ready, t + 1)
                step(s.activation(m.junk[:, :], y_acc, ACT.Square, accum_out=ss[:, 0:1]), y_squares)
                act.wait_ge(y_mean, t + 1)
                step(s.activation(ss[:, 1:2], ss[:, 1:2], ACT.Sqrt), y_root)
                act.wait_ge(inT_psum, t + 1)
                step(s.activation(inT[:, 0:4, :], m.bank(0).rearrange("p (k s) -> p k s", k=4), ACT.Copy))
                step(s.activation(inT[:, KD:KD + KP, :], m.bank(7)[:, 0:KP * P].rearrange("p (k s) -> p k s", k=KP),
                                  ACT.Copy), inT_act)
                act.wait_ge(gate_biased, t + 1)
                step(s.activation(gate_row, gate_row, ACT.Sigmoid), gate_done)
                act.wait_ge(gated, t + 1)
                step(s.activation(m.junk[:, :], prod[:, t, :], ACT.Square, accum_out=gs[:, t:t + 1]), gated_squares)
            act.wait_ge(gated_mean, 1)
            step(s.activation(gs, gs, ACT.Sqrt), gated_root)

        @block.vector
        def _(dve):
            v = nc.vector
            step = Chain(m, dve, m.dve_step)
            dve.wait_ge(weights_loaded, 96)
            for t in range(T):
                dve.wait_ge(rows_gathered[t % 2], 16 * TOPK * (t // 2 + 1))
                step(v.tensor_scalar(y_acc, choices[:, t % 2, 0, :], m.gates[:, t, 0:1], None, ALU.mult))
                for k in range(1, TOPK):
                    step(v.scalar_tensor_tensor(y_acc, choices[:, t % 2, k, :], m.gates[:, t, k:k + 1], y_acc,
                                                ALU.mult, ALU.add), y_ready if k == TOPK - 1 else None)
                dve.wait_ge(y_squares, t + 1)
                step(v.tensor_scalar(ss[:, 1:2], ss[:, 0:1], 1.0 / D, EPS, ALU.mult, ALU.add), y_mean)
                dve.wait_ge(y_root, t + 1)
                step(v.reciprocal(ss[:, 2:3], ss[:, 1:2]))
                step(v.scalar_tensor_tensor(y_acc, y_acc, ss[:, 2:3], post_g, ALU.mult, ALU.mult), rows_used)
                step(v.tensor_tensor(m.x_sb[:, t, :], m.x_sb[:, t, :], y_acc, ALU.add), x2_ready)
                dve.wait_ge(inT_psum, t + 1)
                step(v.tensor_copy(inT[:, 4:8, :], m.bank(1).rearrange("p (k s) -> p k s", k=4)), inT_dve)
                dve.wait_ge(gate_psum, t + 1)
                step(v.tensor_tensor(gate_row, m.ps[:, 2:4, :].rearrange("p b c -> p (b c)"), gate_b, ALU.add),
                     gate_biased)
                dve.wait_ge(gate_done, t + 1)
                step(v.tensor_tensor(prod[:, t, :], m.ps[:, 4:6, :].rearrange("p b c -> p (b c)"), gate_row,
                                     ALU.mult), gated)
            dve.wait_ge(gated_squares, T)
            step(v.tensor_scalar(gs, gs, 1.0 / D, EPS, ALU.mult, ALU.add), gated_mean)
            dve.wait_ge(gated_root, 1)
            step(v.reciprocal(gs, gs))
            for t in range(T):
                step(v.scalar_tensor_tensor(prod[:, t, :], prod[:, t, :], gs[:, t:t + 1], norm_g, ALU.mult,
                                            ALU.mult))
                step(v.tensor_tensor(m.x_sb[:, t, :], m.x_sb[:, t, :], prod[:, t, :], ALU.add), out_ready)

        @block.tensor
        def _(pe):
            mm, tr = nc.tensor.matmul, nc.tensor.transpose
            pe.wait_ge(weights_loaded, 96)
            for t in range(T):
                pe.wait_ge(x2_ready, t + 1)
                if t >= 1:
                    pe.wait_ge(inT_act, t)
                    pe.wait_ge(inT_dve, t)
                    pe.wait_ge(gated, t)
                for k in range(KD):
                    tr(m.bank(k // 4)[:, (k % 4) * P:(k % 4 + 1) * P], m.x_sb[:, t, k * P:(k + 1) * P], m.ident[:, :])
                for k in range(KP):
                    last = tr(m.bank(7)[:, k * P:(k + 1) * P], p_sb[:, t, k * P:(k + 1) * P], m.ident[:, :])
                last.then_inc(inT_psum, 1)
                pe.wait_ge(inT_act, t + 1)
                pe.wait_ge(inT_dve, t + 1)
                for j in range(2):
                    for k in range(KP):
                        mm(m.bank(4 + j), inT[:, KD + k, :], w_proj[:, k, j * 512:(j + 1) * 512], start=(k == 0),
                           stop=(k == KP - 1))
                for j in range(2):
                    for k in range(KD):
                        last = mm(m.bank(2 + j), inT[:, k, :], w_gate[:, k, j * 512:(j + 1) * 512], start=(k == 0),
                                  stop=(k == KD - 1))
                last.then_inc(gate_psum, 1)


def decoder_layer(nc, x, p, positions, attn_pre_g, w_in, q_norm_g, w_uq, kv_norm_g, w_ukv, sg_norm_g, w_spatial,
                  b_spatial, mla_out_g, sg_out_g, w_out, attn_post_g, ffn_pre_g, w_router, b_router, w_gate_up,
                  b_gate_up, w_down, b_down, ffn_post_g, w_ple_gate, b_ple_gate, w_ple_proj, ple_norm_g, out):
    with ExitStack() as ctx:
        ctx.enter_context(nc.allow_non_contiguous_dma(reason="vectors of 1024 elements as columns"))
        m = Buffers(nc, ctx)
        input_projection(nc, m, x, positions, attn_pre_g, w_in, q_norm_g, w_uq, kv_norm_g, w_ukv, b_spatial,
                         mla_out_g, sg_out_g, b_router, b_gate_up, b_down)
        attention_operands(nc, m, w_spatial, sg_norm_g)
        w_out_loaded = ctx.enter_context(nc.semaphore("w_out_loaded"))
        w_out_scaled = ctx.enter_context(nc.semaphore("w_out_scaled"))
        attention(nc, m, w_out, w_out_loaded, w_out_scaled)
        output_and_router(nc, m, x, w_out_scaled, attn_post_g, ffn_pre_g, w_router)
        experts(nc, m, w_gate_up, w_down)
        combine_and_embed(nc, m, p, ffn_post_g, w_ple_gate, b_ple_gate, w_ple_proj, ple_norm_g, out)


_INS = ["x", "p", "positions", "attn_pre_g", "w_in", "q_norm_g", "w_uq", "kv_norm_g", "w_ukv", "sg_norm_g",
        "w_spatial", "b_spatial", "mla_out_g", "sg_out_g", "w_out", "attn_post_g", "ffn_pre_g", "w_router",
        "b_router", "w_gate_up", "b_gate_up", "w_down", "b_down", "ffn_post_g", "w_ple_gate", "b_ple_gate",
        "w_ple_proj", "ple_norm_g"]


def kernel(**inputs):
    import concourse.bacc as bacc
    from concourse.bass_utils import run_bass_kernel_spmd

    nc = bacc.Bacc("TRN2", target_bir_lowering=False, num_devices=1)
    arrays, args = {}, []
    for name in _INS:
        a = np.ascontiguousarray(inputs[name])
        arrays[f"in_{name}"] = a
        args.append(nc.dram_tensor(f"in_{name}", a.shape, mybir.dt.from_np(a.dtype), kind="ExternalInput").ap())
    out = nc.dram_tensor("out", (1, SEQ, D), F32, kind="ExternalOutput").ap()
    decoder_layer(nc, *args, out)
    r = run_bass_kernel_spmd(nc, [arrays], core_ids=[0])
    return r.results[0]["out"]
```

```python
from contextlib import ExitStack

import numpy as np

import concourse.bass as bass
from concourse import mybir

ALU = mybir.AluOpType
ACT = mybir.ActivationFunctionType
AX = mybir.AxisListType
F32 = mybir.dt.float32
F32R = mybir.dt.float32r
I32 = mybir.dt.int32
U32 = mybir.dt.uint32

P = 128
D = 1024
SEQ = 1024
T = SEQ // P
KD = D // P
H = 8
NOPE, ROPE, VH = 64, 32, 64
HR = ROPE // 2
QK = NOPE + ROPE
QL, KVL = 256, 128
QC = QL // P
A_COLS = QL + KVL + ROPE
SGW = 512
IN_COLS = A_COLS + 2 * SGW
HC = SGW // H
E = 32
TOPK = 4
F = 1024
KF = F // P
DP = 256
KP = DP // P
EPS = 1e-6
SCALE = float(QK) ** -0.5
LIMIT, ALPHA = 7.0, 1.702
THETA = 10000.0
NEG = -3.0e38
TWO_PI = 2 * np.pi
PI_A = 6.28125
PI_B = float(TWO_PI - PI_A)
ROUND = 1.5 * 2.0 ** 23
R_MAX = 3.1415925

CT = 320
CH = -(-CT // P)
MORE = TOPK * SEQ // (CT + 1)
MAX_ITEMS = E + MORE
TAB = MAX_ITEMS + 1
WIDTHS = (128, 136, 144, 160, 176, 200, 256, 320)
EMPTY = 1 << 20
N_UNITS = 12
GU_UNITS = 8
RAW = 6
Y_BANKS = (0, 1, 4)


class Chain:

    def __init__(self, m, eng, own):
        self.eng, self.own, self.count = eng, own, m.count

    def __call__(self, ins, signal=None):
        s = self.own if signal is None else signal
        self.count[s.name] = self.count.get(s.name, 0) + 1
        ins.then_inc(s, 1)
        self.eng.wait_ge(s, self.count[s.name])


class Buffers:

    def __init__(self, nc, ctx):
        def sb(name, shape, dt=F32):
            return ctx.enter_context(nc.sbuf_tensor(name, shape, dt))

        self.sem = lambda name: ctx.enter_context(nc.semaphore(name))
        self.count = {}
        self.pool_mark, self.sp_mark = self.sem("pool_mark"), self.sem("sp_mark")
        self.act_step, self.dve_step, self.pool_step = (self.sem(f"{e}_step") for e in ("act", "dve", "pool"))
        self.x_loaded = [self.sem(f"x_loaded{t}") for t in range(T)]
        self.h_rows = nc.dram_tensor("h_rows", [SEQ, D], F32).ap()
        self.choice_list = nc.dram_tensor("choice_list", [TAB * CT, 2], I32).ap()
        self.y_choices = nc.dram_tensor("y_choices", [SEQ * TOPK, D], F32).ap()
        self.ps = ctx.enter_context(nc.psum_tensor("ps", [P, 8, 512], F32))

        xa = sb("xa", [P, T * D])
        self.xa = xa
        self.x_sb = xa[:, :].rearrange("p (t d) -> p t d", t=T)
        self.za = xa[:, 0:T * A_COLS].rearrange("p (t c) -> p t c", t=T)
        self.qT = xa[0:QK, :].rearrange("p (h s) -> p h s", h=H)
        self.junk = sb("junk", [P, D])
        self.ident = sb("ident", [P, P])
        self.causal = sb("causal", [P, P])
        self.before = sb("before", [P, P])
        self.ones = sb("ones", [P, P])
        self.gains = sb("gains", [P, 20])
        self.stat = sb("stat", [P, 160])
        self.small = sb("small", [P, 64])
        self.cosb = sb("cosb", [P, T, HR])
        self.sinb = sb("sinb", [P, T, HR])
        self.rtmp = [sb(f"rtmp{i}", [P, T, HR]) for i in range(4)]
        self.invf = sb("invf", [P, HR])
        self.posi = sb("posi", [P, T], I32)
        self.posf = sb("posf", [P, T])
        self.small_row = sb("small_row", [P, 256])
        self.b_sp = sb("b_sp", [P, H])
        self.b_r = sb("b_r", [P, E])
        self.gates = sb("gates", [P, T, TOPK])
        self.slots = sb("slots", [P, T, TOPK], I32)
        self.choice_ids = sb("choice_ids", [P, T, TOPK, 2], I32)
        self.items = sb("items", [1, 2 * TAB + 1], I32)
        self.bias_cols = sb("bias_cols", [P, 2 * KF + KD, E])
        self.bias_now = sb("bias_now", [P, 2 * KF + KD])
        self.idx_next = sb("idx_next", [P, CH, 2], I32)
        self.idx_now = sb("idx_now", [P, CH, 2], I32)
        self.g_x, self.g_q, self.g_kv = self.gains[:, 0:8], self.gains[:, 8:10], self.gains[:, 10:11]
        self.g_mix = self.gains[:, 11:19]

    def open_early(self, nc, ctx):
        ring = ctx.enter_context(nc.sbuf_tensor("ring", [P, 24576], F32))
        work = ctx.enter_context(nc.sbuf_tensor("work", [P, 16384], F32))
        self.work = work
        self.ring = ring
        n_in = KD * IN_COLS
        self.w_in = ring[:, 0:n_in].rearrange("p (k n) -> p k n", k=KD)
        self.w_uq = ring[:, n_in:n_in + 1536].rearrange("p (k n) -> p k n", k=QC)
        self.w_ukv = ring[:, 13056:14080].rearrange("p (h n) -> p h n", h=H)
        self.cqT = ring[:, 14080:16128].rearrange("p (k s) -> p k s", k=QC)
        self.ckvT = ring[:, 16128:17152]
        self.krT = ring[0:QK, 17152:18176]
        self.v_sb = ring[:, 0:4096].rearrange("p (t n) -> p t n", t=T)
        self.probs = ring[:, 4096:6144].rearrange("p (b s) -> p b s", b=2)
        self.probsT = ring[:, 6144:8192].rearrange("p (b s) -> p b s", b=2)
        self.w_spT = ring[:, 8192:9216].rearrange("p (h s) -> p h s", h=H)
        self.w_sp = ring[:, 9216:10240].rearrange("p (h s) -> p h s", h=H)
        self.sg_g = ring[:, 10240:10752]
        self.w_out = ring[:, 12288:20480].rearrange("p (k n) -> p k n", k=KD)
        self.o_sb = ring[:, 20480:24576].rearrange("p (t c) -> p t c", t=T)
        self.post_g = ring[:, 0:1024]
        self.ffn_g = ring[:, 1024:2048]
        self.y_row = ring[:, 2048:4096].rearrange("p (b d) -> p b d", b=2)
        self.h_row = ring[:, 4096:6144].rearrange("p (b d) -> p b d", b=2)
        self.hT = ring[:, 6144:7168].rearrange("p (k s) -> p k s", k=KD)
        self.w_router = ring[:, 7168:7424].rearrange("p (k e) -> p k e", k=KD)
        self.logits = ring[:, 7424:7680].rearrange("p (t e) -> p t e", t=T)
        self.hot = ring[:, 7680:8704].rearrange("p (t k e) -> p t k e", t=T, k=TOPK)
        self.taken = ring[:, 8704:8960].rearrange("p (t e) -> p t e", t=T)
        self.place = ring[:, 8960:9216].rearrange("p (t e) -> p t e", t=T)
        self.scr = ring[:, 9216:12288]
        self.xT = work[:, 0:8192].rearrange("p (k s) -> p k s", k=KD)
        self.kT = work[0:QK, 0:8192].rearrange("p (h s) -> p h s", h=H)
        self.mixT = work[:, 0:8192].rearrange("p (k s) -> p k s", k=KD)
        self.u_sg = work[:, 8192:12288].rearrange("p (t c) -> p t c", t=T)
        self.v_sg = work[:, 12288:16384].rearrange("p (t c) -> p t c", t=T)

    def bank(self, i, rows=P):
        return self.ps[0:rows, i, :]


def columns(vector, k):
    return vector.rearrange("l (k p) -> p (l k)", k=k)


def on_all(vector):
    return vector.rearrange("l n -> (l n)").partition_broadcast(P)


def rope(v, step, x1, x2, cos, sin, tmp, signal=None):
    step(v.tensor_tensor(tmp[0], x1, cos, ALU.mult))
    step(v.tensor_tensor(tmp[1], x2, sin, ALU.mult))
    step(v.tensor_tensor(tmp[2], x2, cos, ALU.mult))
    step(v.tensor_tensor(tmp[3], x1, sin, ALU.mult))
    step(v.tensor_tensor(x1, tmp[0], tmp[1], ALU.subtract))
    step(v.tensor_tensor(x2, tmp[2], tmp[3], ALU.add), signal)


def input_projection(nc, m, x, positions, attn_pre_g, w_in, q_norm_g, w_uq, kv_norm_g, w_ukv, b_spatial, mla_out_g,
                     sg_out_g, b_router, b_gate_up, b_down):
    with ExitStack() as ctx:
        sem = m.sem

        x_loaded = m.x_loaded
        biases_loaded = sem("biases_loaded")
        small_loaded = sem("small_loaded")
        w_in_loaded = sem("w_in_loaded")
        w_mid_loaded = sem("w_mid_loaded")
        consts_ready = sem("consts_ready")
        w_in_scaled = sem("w_in_scaled")
        biasT_psum = sem("biasT_psum")
        biasT_copied = sem("biasT_copied")
        xT_psum = sem("xT_psum")
        xT_act = sem("xT_act")
        xT_dve = sem("xT_dve")
        squares_x = sem("squares_x")
        mean_x = sem("mean_x")
        root_x = sem("root_x")
        rstd_x = sem("rstd_x")
        angles = sem("angles")
        sines = sem("sines")
        z_psum = sem("z_psum")
        z_latent = sem("z_latent")
        z_gated = sem("z_gated")
        mean_latent = sem("mean_latent")
        root_latent = sem("root_latent")
        latent_ready = sem("latent_ready")
        latentT_psum = sem("latentT_psum")
        latentT_copied = sem("latentT_copied")
        block = ctx.enter_context(nc.Block())
        bgu_rows = m.work[0:E, 8192:8192 + 2 * F]
        bd_rows = m.work[0:E, 8192 + 2 * F:8192 + 2 * F + D]
        ssx = m.stat[:, 0:T]
        ms = m.stat[:, T:2 * T]
        lat = m.stat[:, 2 * T:4 * T]
        n_bias = 2 * KF + KD

        @block.sync
        def _(sp):
            x_t = x.rearrange("b (t p) d -> p (b t) d", p=P)
            for t in range(T):
                sp.dma_start(m.x_sb[:, t, :], x_t[:, t, :]).then_inc(x_loaded[t], 16)
                if t == 1:
                    sp.dma_start(bgu_rows, b_gate_up.rearrange("l e n -> (l e) n")).then_inc(biases_loaded, 16)
                    sp.dma_start(bd_rows, b_down.rearrange("l e n -> (l e) n")).then_inc(biases_loaded, 16)
            wi = w_in.rearrange("l (k p) n -> p (l k) n", p=P)
            for k in range(0, KD, 2):
                sp.dma_start(m.w_in[:, k:k + 2, :], wi[:, k:k + 2, :]).then_inc(w_in_loaded, 16)
            sp.dma_start(m.w_uq, w_uq.rearrange("l (k p) h c -> p (l k) (h c)", p=P)).then_inc(w_mid_loaded, 16)
            sp.dma_start(m.w_ukv, w_ukv.rearrange("l p h c -> (l p) h c")).then_inc(w_mid_loaded, 16)

        @block.gpsimd
        def _(pool):
            g = nc.gpsimd
            step = Chain(m, pool, m.pool_step)
            pool.dma_start(m.g_x, columns(attn_pre_g, KD)).then_inc(small_loaded, 16)
            pool.dma_start(m.posi[:, :], positions.rearrange("b (t p) -> p (b t)", p=P)).then_inc(small_loaded, 16)
            pool.dma_start(m.g_q, columns(q_norm_g, QC)).then_inc(small_loaded, 16)
            pool.dma_start(m.g_kv, columns(kv_norm_g, 1)).then_inc(small_loaded, 16)
            pool.dma_start(m.g_mix[:, 0:4], columns(mla_out_g, 4)).then_inc(small_loaded, 16)
            pool.dma_start(m.g_mix[:, 4:8], columns(sg_out_g, 4)).then_inc(small_loaded, 16)
            pool.dma_start(m.b_sp[:, :], b_spatial.rearrange("l h t -> t (l h)")).then_inc(small_loaded, 16)
            pool.dma_start(m.b_r[:, :], on_all(b_router)).then_inc(small_loaded, 16)
            step(g.memset(m.ident[:, :], 0.0))
            step(g.affine_select(out=m.ident[:, :], in_=m.ident[:, :], compare_op=ALU.not_equal, fill=1.0, base=0,
                                 pattern=[[-1, P]], channel_multiplier=1), consts_ready)
            inv = (np.float32(1.0) / np.power(np.float32(THETA), np.arange(0, ROPE, 2, dtype=np.float32)
                                              / np.float32(ROPE))).astype(np.float32)
            for i in range(HR):
                step(g.memset(m.invf[:, i:i + 1], float(inv[i])), consts_ready)
            step(g.memset(m.causal[:, :], 0.0))
            step(g.affine_select(out=m.causal[:, :], in_=m.causal[:, :], compare_op=ALU.is_ge, fill=NEG, base=0,
                                 pattern=[[-1, P]], channel_multiplier=1))
            step(g.memset(m.ones[:, :], 1.0))
            step(g.affine_select(out=m.before[:, :], in_=m.ones[:, :], compare_op=ALU.is_gt, fill=0.0, base=0,
                                 pattern=[[1, P]], channel_multiplier=-1))
            step(g.iota(m.choice_ids[:, :, :, 0], pattern=[[P, T], [0, TOPK]], base=0, channel_multiplier=1))
            step(g.iota(m.choice_ids[:, :, :, 1], pattern=[[P * TOPK, T], [1, TOPK]], base=0,
                        channel_multiplier=TOPK))
            step(g.memset(m.idx_next[:, :, :], EMPTY))
            pool.wait_ge(small_loaded, 8 * 16)
            pool.wait_ge(w_in_loaded, 4 * 16)
            for k in range(KD):
                step(g.tensor_scalar(m.w_in[:, k, :], m.w_in[:, k, :], m.g_x[:, k:k + 1], None, ALU.mult),
                     w_in_scaled)
            pool.wait_ge(w_mid_loaded, 2 * 16)
            for k in range(QC):
                step(g.tensor_scalar(m.w_uq[:, k, :], m.w_uq[:, k, :], m.g_q[:, k:k + 1], None, ALU.mult))
            step(g.tensor_scalar(m.w_ukv, m.w_ukv, m.g_kv, None, ALU.mult))

        @block.scalar
        def _(act):
            s = nc.scalar
            step = Chain(m, act, m.act_step)
            for t in range(T):
                act.wait_ge(x_loaded[t], 16)
                step(s.activation(m.junk[:, :], m.x_sb[:, t, :], ACT.Square, accum_out=ssx[:, t:t + 1]), squares_x)
                act.wait_ge(xT_psum, t + 1)
                step(s.activation(m.xT[:, 0:4, t * P:(t + 1) * P], m.bank(2 * (t % 2)).rearrange(
                    "p (k s) -> p k s", k=4), ACT.Copy), xT_act)
            act.wait_ge(mean_x, 1)
            step(s.activation(ms, ms, ACT.Sqrt), root_x)
            act.wait_ge(angles, 1)
            step(s.activation(m.sinb[:, :, :], m.rtmp[0][:, :, :], ACT.Sin))
            step(s.activation(m.cosb[:, :, :], m.rtmp[0][:, :, :], ACT.Sin, scale=0.5), sines)
            act.wait_ge(rstd_x, 1)
            act.wait_ge(biasT_psum, 2)
            for t in range(T):
                act.wait_ge(z_psum, t + 1)
                b = 3 * (t % 2)
                step(s.activation(m.u_sg[:, t, :], m.bank(b + 1), ACT.Gelu_apprx_tanh, scale=ms[:, t:t + 1]), z_gated)
                step(s.activation(m.v_sg[:, t, :], m.bank(b + 2), ACT.Gelu_apprx_tanh, scale=ms[:, t:t + 1]), z_gated)
            act.wait_ge(mean_latent, 1)
            step(s.activation(lat, lat, ACT.Sqrt), root_latent)

        @block.vector
        def _(dve):
            v = nc.vector
            step = Chain(m, dve, m.dve_step)
            for t in range(T):
                dve.wait_ge(xT_psum, t + 1)
                step(v.tensor_copy(m.xT[:, 4:8, t * P:(t + 1) * P], m.bank(2 * (t % 2) + 1).rearrange(
                    "p (k s) -> p k s", k=4)), xT_dve)
            dve.wait_ge(squares_x, T)
            step(v.tensor_scalar(ms, ssx, 1.0 / D, EPS, ALU.mult, ALU.add), mean_x)
            dve.wait_ge(small_loaded, 8 * 16)
            dve.wait_ge(consts_ready, 1 + HR)
            step(v.tensor_copy(m.posf[:, :], m.posi[:, :]))
            r0, r1 = m.rtmp[0][:, :, :], m.rtmp[1][:, :, :]
            wide = [P, T, HR]
            step(v.tensor_tensor(r0, m.posf[:, :].unsqueeze(2).broadcast_to(wide),
                                 m.invf[:, :].unsqueeze(1).broadcast_to(wide), ALU.mult))
            step(v.tensor_scalar(r1, r0, float(1.0 / TWO_PI), ROUND, ALU.mult, ALU.add))
            step(v.tensor_scalar(r1, r1, ROUND, None, ALU.subtract))
            step(v.scalar_tensor_tensor(r0, r1, -PI_A, r0, ALU.mult, ALU.add))
            step(v.scalar_tensor_tensor(r0, r1, -PI_B, r0, ALU.mult, ALU.add))
            step(v.tensor_scalar(r0, r0, R_MAX, -R_MAX, ALU.min, ALU.max), angles)
            dve.wait_ge(root_x, 1)
            step(v.reciprocal(ms, ms), rstd_x)
            for i in range(2):
                dve.wait_ge(biasT_psum, i + 1)
                n = min(16, n_bias - 16 * i)
                step(v.tensor_copy(m.bias_cols[:, 16 * i:16 * i + n, :], m.bank(6 + i)[:, 0:n * E].rearrange(
                    "p (c e) -> p c e", e=E)), biasT_copied)
            dve.wait_ge(sines, 1)
            step(v.tensor_tensor(m.cosb[:, :, :], m.cosb[:, :, :], m.cosb[:, :, :], ALU.mult))
            step(v.tensor_scalar(m.cosb[:, :, :], m.cosb[:, :, :], -2.0, 1.0, ALU.mult, ALU.add))
            dve.wait_ge(rstd_x, 1)
            for t in range(T):
                dve.wait_ge(z_psum, t + 1)
                step(v.tensor_scalar(m.za[:, t, :], m.bank(3 * (t % 2))[:, 0:A_COLS], ms[:, t:t + 1], None, ALU.mult),
                     z_latent)
                for a, b, c in ((0, QL, t), (QL, QL + KVL, T + t)):
                    step(v.tensor_tensor_reduce(out=m.small_row[:, 0:b - a], in0=m.za[:, t, a:b], in1=m.za[:, t, a:b],
                                                scale=1.0, scalar=0.0, op0=ALU.mult, op1=ALU.add,
                                                accum_out=lat[:, c:c + 1]))
            step(v.tensor_scalar(lat[:, 0:T], lat[:, 0:T], 1.0 / QL, EPS, ALU.mult, ALU.add))
            step(v.tensor_scalar(lat[:, T:2 * T], lat[:, T:2 * T], 1.0 / KVL, EPS, ALU.mult, ALU.add), mean_latent)
            rope(v, step, m.za[:, :, QL + KVL:QL + KVL + HR], m.za[:, :, QL + KVL + HR:A_COLS], m.cosb[:, :, :],
                 m.sinb[:, :, :], [r[:, :, :] for r in m.rtmp])
            dve.wait_ge(root_latent, 1)
            step(v.reciprocal(lat, lat))
            for t in range(T + 1):
                if t < T:
                    step(v.tensor_scalar(m.za[:, t, 0:QL], m.za[:, t, 0:QL], lat[:, t:t + 1], None, ALU.mult))
                    step(v.tensor_scalar(m.za[:, t, QL:QL + KVL], m.za[:, t, QL:QL + KVL], lat[:, T + t:T + t + 1],
                                         None, ALU.mult), latent_ready)
                if t >= 1:
                    dve.wait_ge(latentT_psum, t)
                    tok = slice((t - 1) * P, t * P)
                    b = m.bank(6 + (t - 1) % 2)
                    step(v.tensor_copy(m.cqT[:, :, tok], b[:, 0:QL].rearrange("p (k s) -> p k s", k=QC)))
                    step(v.tensor_copy(m.ckvT[:, tok], b[:, QL:QL + P]))
                    step(v.tensor_copy(m.krT[NOPE:QK, tok], b[NOPE:QK, QL + P:QL + 2 * P]), latentT_copied)

        @block.tensor
        def _(pe):
            mm, tr = nc.tensor.matmul, nc.tensor.transpose
            pe.wait_ge(consts_ready, 1)

            def transpose_biases(i):
                pe.wait_ge(biases_loaded, 32)
                for c in range(16 * i, min(16 * i + 16, n_bias)):
                    last = tr(m.bank(6 + i)[:, (c - 16 * i) * E:(c - 16 * i + 1) * E],
                              m.work[0:E, 8192 + c * P:8192 + (c + 1) * P], m.ident[0:E, 0:E])
                last.then_inc(biasT_psum, 1)

            for t in range(T):
                pe.wait_ge(x_loaded[t], 16)
                if t >= 2:
                    pe.wait_ge(xT_act, t - 1)
                    pe.wait_ge(xT_dve, t - 1)
                for k in range(KD):
                    last = tr(m.bank(2 * (t % 2) + k // 4)[:, (k % 4) * P:(k % 4 + 1) * P],
                              m.x_sb[:, t, k * P:(k + 1) * P], m.ident[:, :])
                last.then_inc(xT_psum, 1)
            for i in range(2):
                transpose_biases(i)
            pe.wait_ge(xT_act, T)
            pe.wait_ge(xT_dve, T)
            for t in range(T):
                if t >= 2:
                    pe.wait_ge(z_latent, t - 1)
                    pe.wait_ge(z_gated, 2 * (t - 1))
                for k in range(KD):
                    if t == 0:
                        pe.wait_ge(w_in_scaled, k + 1)
                    for j, (a, b) in enumerate(((0, A_COLS), (A_COLS, A_COLS + SGW), (A_COLS + SGW, IN_COLS))):
                        last = mm(m.bank(3 * (t % 2) + j)[:, 0:b - a], m.xT[:, k, t * P:(t + 1) * P],
                                  m.w_in[:, k, a:b], start=(k == 0), stop=(k == KD - 1))
                last.then_inc(z_psum, 1)
            pe.wait_ge(biasT_copied, 2)
            for t in range(T):
                pe.wait_ge(latent_ready, t + 1)
                if t >= 2:
                    pe.wait_ge(latentT_copied, t - 1)
                b = m.bank(6 + t % 2)
                for i in range(3):
                    tr(b[:, i * P:(i + 1) * P], m.za[:, t, i * P:(i + 1) * P], m.ident[:, :])
                tr(b[0:QK, 3 * P:4 * P], m.za[:, t, A_COLS - QK:A_COLS], m.ident[:, :]).then_inc(latentT_psum, 1)


def attention_operands(nc, m, w_spatial, sg_norm_g):
    with ExitStack() as ctx:
        sem = m.sem

        w_sp_loaded = sem("w_sp_loaded")
        kr_copied = sem("kr_copied")
        w_spT_psum = sem("w_spT_psum")
        w_spT_copied = sem("w_spT_copied")
        w_spT_masked = sem("w_spT_masked")
        v_squares = sem("v_squares")
        v_mean = sem("v_mean")
        v_root = sem("v_root")
        v_normed = sem("v_normed")
        q_psum = sem("q_psum")
        q_copied = sem("q_copied")
        q_roped = sem("q_roped")
        qT_psum = sem("qT_psum")
        qT_act = sem("qT_act")
        qT_dve = sem("qT_dve")
        kv_psum = sem("kv_psum")
        kv_act = sem("kv_act")
        kv_dve = sem("kv_dve")
        sg_psum = sem("sg_psum")
        sg_gated = sem("sg_gated")
        block = ctx.enter_context(nc.Block())
        q_row = m.ring[:, 20480:20480 + 2 * H * QK].rearrange("p (b h c) -> p b h c", b=2, h=H)
        squares = m.ring[:, 4096:8192]
        sgs = m.stat[:, 32:32 + T * H]
        half = H // 2
        kv_jobs = [("k", h, s) for h in range(H) for s in range(2)] + [("v", t, 0) for t in range(T)]

        @block.sync
        def _(sp):
            sp.dma_start(m.w_sp, w_spatial.rearrange("l h t s -> t (l h) s")).then_inc(w_sp_loaded, 16)
            sp.dma_start(m.sg_g, on_all(sg_norm_g.rearrange("l h c -> l (h c)"))).then_inc(w_sp_loaded, 16)

        @block.gpsimd
        def _(pool):
            g = nc.gpsimd
            step = Chain(m, pool, m.pool_step)
            for h in range(H):
                step(g.tensor_copy(m.kT[NOPE:QK, h, :], m.krT[NOPE:QK, :]), kr_copied)
            for i in range(2):
                pool.wait_ge(w_spT_copied, i + 1)
                part = m.w_spT[:, 4 * i:4 * i + 4, :]
                step(g.affine_select(out=part, in_=part, compare_op=ALU.is_ge, fill=0.0, base=0,
                                     pattern=[[0, 4], [1, P]], channel_multiplier=-1), w_spT_masked)

        @block.scalar
        def _(act):
            s = nc.scalar
            step = Chain(m, act, m.act_step)
            step(s.activation(squares, m.v_sg.rearrange("p t c -> p (t c)"), ACT.Square), v_squares)
            for i in range(2):
                act.wait_ge(w_spT_psum, i + 1)
                step(s.activation(m.w_spT[:, 4 * i:4 * i + 4, :], m.bank(6 + i).rearrange("p (h s) -> p h s", h=4),
                                  ACT.Copy), w_spT_copied)
            act.wait_ge(v_mean, 1)
            step(s.activation(sgs, sgs, ACT.Sqrt), v_root)
            for t in range(T + 1):
                if t < T:
                    act.wait_ge(q_psum, t + 1)
                    if t >= 2:
                        act.wait_ge(qT_psum, t - 1)
                    for i in range(2):
                        step(s.activation(q_row[:, t % 2, half * i:half * i + half, :],
                                          m.bank(2 * (t % 2) + i)[:, 0:half * QK].rearrange(
                                              "p (h c) -> p h c", h=half), ACT.Copy), q_copied)
                if t >= 1:
                    act.wait_ge(qT_psum, t)
                    step(s.activation(m.qT[:, 0:half, (t - 1) * P:t * P], m.bank(4, QK).rearrange(
                        "p (h s) -> p h s", h=half), ACT.Copy), qT_act)
            for n, (kind, i, j) in enumerate(kv_jobs):
                if n % 2 == 0:
                    act.wait_ge(kv_psum, n + 1)
                    if kind == "k":
                        step(s.activation(m.kT[0:NOPE, i, j * 512:(j + 1) * 512], m.bank(6, NOPE), ACT.Copy), kv_act)
                    else:
                        step(s.activation(m.v_sb[:, i, :], m.bank(6), ACT.Copy), kv_act)

        @block.vector
        def _(dve):
            v = nc.vector
            step = Chain(m, dve, m.dve_step)
            dve.wait_ge(v_squares, 1)
            step(v.tensor_reduce(out=sgs, in_=squares.rearrange("p (g c) -> p g c", c=HC), op=ALU.add, axis=AX.X))
            step(v.tensor_scalar(sgs, sgs, 1.0 / HC, EPS, ALU.mult, ALU.add), v_mean)
            dve.wait_ge(v_root, 1)
            step(v.reciprocal(sgs, sgs))
            grouped = m.v_sg.rearrange("p t (h c) -> p (t h) c", h=H)
            step(v.tensor_tensor(grouped, grouped, sgs.unsqueeze(2).broadcast_to([P, T * H, HC]), ALU.mult))
            dve.wait_ge(w_sp_loaded, 32)
            step(v.tensor_tensor(m.v_sg, m.v_sg, m.sg_g.unsqueeze(1).broadcast_to([P, T, SGW]), ALU.mult), v_normed)
            for t in range(T + 1):
                if t < T:
                    dve.wait_ge(q_copied, 2 * (t + 1))
                    q = q_row[:, t % 2, :, :]
                    turn = [P, H, HR]
                    rope(v, step, q[:, :, NOPE:NOPE + HR], q[:, :, NOPE + HR:QK],
                         m.cosb[:, t, :].unsqueeze(1).broadcast_to(turn),
                         m.sinb[:, t, :].unsqueeze(1).broadcast_to(turn), [r[:, :, :] for r in m.rtmp], q_roped)
                if t >= 1:
                    dve.wait_ge(qT_psum, t)
                    step(v.tensor_copy(m.qT[:, half:H, (t - 1) * P:t * P], m.bank(5, QK).rearrange(
                        "p (h s) -> p h s", h=half)), qT_dve)
            for n, (kind, i, j) in enumerate(kv_jobs):
                if n % 2 == 1:
                    dve.wait_ge(kv_psum, n + 1)
                    if kind == "k":
                        step(v.tensor_copy(m.kT[0:NOPE, i, j * 512:(j + 1) * 512], m.bank(7, NOPE)), kv_dve)
                    else:
                        step(v.tensor_copy(m.v_sb[:, i, :], m.bank(7)), kv_dve)
            for h in range(H):
                dve.wait_ge(sg_psum, h + 1)
                u = m.u_sg[:, :, h * HC:(h + 1) * HC]
                step(v.scalar_tensor_tensor(u, m.bank(h % 4).rearrange("p (t c) -> p t c", t=T), m.b_sp[:, h:h + 1],
                                            u, ALU.add, ALU.mult), sg_gated)

        @block.tensor
        def _(pe):
            mm, tr = nc.tensor.matmul, nc.tensor.transpose
            pe.wait_ge(w_sp_loaded, 32)
            for i in range(2):
                for h in range(4):
                    last = tr(m.bank(6 + i)[:, h * P:(h + 1) * P], m.w_sp[:, 4 * i + h, :], m.ident[:, :])
                last.then_inc(w_spT_psum, 1)
            for t in range(T + 1):
                if t < T:
                    if t >= 2:
                        pe.wait_ge(q_copied, 2 * (t - 1))
                    for i in range(2):
                        for k in range(QC):
                            last = mm(m.bank(2 * (t % 2) + i)[:, 0:half * QK], m.cqT[:, k, t * P:(t + 1) * P],
                                      m.w_uq[:, k, i * half * QK:(i + 1) * half * QK], start=(k == 0),
                                      stop=(k == QC - 1))
                    last.then_inc(q_psum, 1)
                if t >= 1:
                    pe.wait_ge(q_roped, t)
                    if t >= 2:
                        pe.wait_ge(qT_act, t - 1)
                        pe.wait_ge(qT_dve, t - 1)
                    for h in range(H):
                        last = tr(m.bank(4 + h // half, QK)[:, (h % half) * P:(h % half + 1) * P],
                                  q_row[:, (t - 1) % 2, h, :], m.ident[:, :])
                    last.then_inc(qT_psum, 1)
            pe.wait_ge(w_spT_copied, 2)
            for n, (kind, i, j) in enumerate(kv_jobs):
                if n >= 2:
                    pe.wait_ge(kv_act if n % 2 == 0 else kv_dve, n // 2)
                if kind == "k":
                    last = mm(m.bank(6 + n % 2, NOPE), m.w_ukv[:, i, 0:NOPE], m.ckvT[:, j * 512:(j + 1) * 512],
                              start=True, stop=True)
                else:
                    last = mm(m.bank(6 + n % 2), m.ckvT[:, i * P:(i + 1) * P], m.w_ukv[:, :, NOPE:NOPE + VH],
                              start=True, stop=True)
                last.then_inc(kv_psum, 1)
            pe.wait_ge(v_normed, 1)
            pe.wait_ge(w_spT_masked, 2)
            for h in range(H):
                if h >= 4:
                    pe.wait_ge(sg_gated, h - 3)
                mm(m.bank(h % 4), m.w_spT[:, h, :], m.v_sg[:, :, h * HC:(h + 1) * HC], start=True,
                   stop=True).then_inc(sg_psum, 1)


def attention(nc, m, w_out, w_out_loaded, w_out_scaled):
    with ExitStack() as ctx:
        sem = m.sem

        empty_ready = sem("empty_ready")
        cleared = sem("cleared")
        scores_psum = sem("scores_psum")
        max_ready = sem("max_ready")
        probs_ready = sem("probs_ready")
        pT_psum = sem("pT_psum")
        pT_act = sem("pT_act")
        pT_dve = sem("pT_dve")
        o_psum = sem("o_psum")
        o_ready = sem("o_ready")
        block = ctx.enter_context(nc.Block())
        jobs = [(h, i) for h in range(H) for i in range(T)]
        N = len(jobs)
        empty = m.junk[:, 0:TAB * CT * 2 // P].bitcast(I32)
        nmax, rsum, rinv = m.stat[:, 96:100], m.stat[:, 100:104], m.stat[:, 104:108]

        def wide(n):
            return sum(i >= 4 for _, i in jobs[:n])

        @block.sync
        def _(sp):
            wo = w_out.rearrange("l (k p) n -> p (l k) n", p=P)
            for k in range(0, KD, 4):
                sp.dma_start(m.w_out[:, k:k + 4, :], wo[:, k:k + 4, :]).then_inc(w_out_loaded, 16)
            sp.wait_ge(empty_ready, 1)
            sp.dma_start(m.choice_list.rearrange("a o -> (a o)").rearrange("(p c) -> p c", p=P), empty).then_inc(cleared, 16)
            sp.wait_ge(cleared, 16)

        @block.gpsimd
        def _(pool):
            g = nc.gpsimd
            step = Chain(m, pool, m.pool_step)
            step(g.memset(empty, EMPTY), empty_ready)
            pool.wait_ge(w_out_loaded, 32)
            for k in range(KD):
                step(g.tensor_scalar(m.w_out[:, k, :], m.w_out[:, k, :], m.g_mix[:, k:k + 1], None, ALU.mult),
                     w_out_scaled)

        @block.scalar
        def _(act):
            s = nc.scalar
            step = Chain(m, act, m.act_step)
            for n in range(N + 1):
                if n < N:
                    w = (jobs[n][1] + 1) * P
                    act.wait_ge(max_ready, n + 1)
                    if n >= 2:
                        act.wait_ge(pT_psum, n - 1)
                    if n >= 4:
                        act.wait_ge(o_ready, n - 3)
                    step(s.activation(m.probs[:, n % 2, 0:w], m.ps[:, 2 * (n % 2):2 * (n % 2) + 2, :].rearrange(
                        "p b c -> p (b c)")[:, 0:w], ACT.Exp, bias=nmax[:, n % 4:n % 4 + 1], scale=SCALE,
                        accum_out=rsum[:, n % 4:n % 4 + 1]), probs_ready)
                if n >= 1:
                    l = n - 1
                    w = min(4, jobs[l][1] + 1) * P
                    act.wait_ge(pT_psum, l + 1)
                    if l >= 2:
                        act.wait_ge(o_psum, l - 1)
                    step(s.activation(m.probsT[:, l % 2, 0:w], m.bank(4)[:, 0:w], ACT.Copy), pT_act)

        @block.vector
        def _(dve):
            v = nc.vector
            step = Chain(m, dve, m.dve_step)
            for n in range(N + 2):
                if n < N:
                    i = jobs[n][1]
                    w = (i + 1) * P
                    s = m.ps[:, 2 * (n % 2):2 * (n % 2) + 2, :].rearrange("p b c -> p (b c)")
                    dve.wait_ge(scores_psum, n + 1)
                    if n >= 4:
                        dve.wait_ge(probs_ready, n - 3)
                    step(v.tensor_tensor(s[:, w - P:w], s[:, w - P:w], m.causal[:, :], ALU.add))
                    step(v.reduce_max(nmax[:, n % 4:n % 4 + 1], s[:, 0:w], AX.X))
                    step(v.tensor_scalar(nmax[:, n % 4:n % 4 + 1], nmax[:, n % 4:n % 4 + 1], -SCALE, None, ALU.mult),
                         max_ready)
                l = n - 1
                if 0 <= l < N and jobs[l][1] >= 4:
                    w = (jobs[l][1] - 3) * P
                    dve.wait_ge(pT_psum, l + 1)
                    if l >= 2:
                        dve.wait_ge(o_psum, l - 1)
                    step(v.tensor_copy(m.probsT[:, l % 2, 512:512 + w], m.bank(5)[:, 0:w]), pT_dve)
                l = n - 2
                if l >= 0:
                    h, i = jobs[l]
                    dve.wait_ge(probs_ready, l + 1)
                    step(v.reciprocal(rinv[:, l % 4:l % 4 + 1], rsum[:, l % 4:l % 4 + 1]))
                    dve.wait_ge(o_psum, l + 1)
                    step(v.tensor_scalar(m.o_sb[:, i, h * VH:(h + 1) * VH], m.bank(6 + l % 2)[:, 0:VH],
                                         rinv[:, l % 4:l % 4 + 1], None, ALU.mult), o_ready)

        @block.tensor
        def _(pe):
            mm, tr = nc.tensor.matmul, nc.tensor.transpose
            for n in range(-1, N + 1):
                if n + 1 < N:
                    l = n + 1
                    h, i = jobs[l]
                    if l >= 2:
                        pe.wait_ge(probs_ready, l - 1)
                    for b in range(i // 4 + 1):
                        w = min(512, (i + 1) * P - 512 * b)
                        last = mm(m.bank(2 * (l % 2) + b)[:, 0:w], m.qT[:, h, i * P:(i + 1) * P],
                                  m.kT[:, h, 512 * b:512 * b + w], start=True, stop=True)
                    last.then_inc(scores_psum, 1)
                if 0 <= n < N:
                    i = jobs[n][1]
                    pe.wait_ge(probs_ready, n + 1)
                    if n >= 1:
                        pe.wait_ge(pT_act, n)
                    if wide(n):
                        pe.wait_ge(pT_dve, wide(n))
                    for j in range(i + 1):
                        last = tr(m.bank(4 + j // 4)[:, (j % 4) * P:(j % 4 + 1) * P],
                                  m.probs[:, n % 2, j * P:(j + 1) * P], m.ident[:, :])
                    last.then_inc(pT_psum, 1)
                if n >= 1:
                    l = n - 1
                    h, i = jobs[l]
                    pe.wait_ge(pT_act, l + 1)
                    if wide(l + 1):
                        pe.wait_ge(pT_dve, wide(l + 1))
                    if l >= 2:
                        pe.wait_ge(o_ready, l - 1)
                    for j in range(i + 1):
                        last = mm(m.bank(6 + l % 2)[:, 0:VH], m.probsT[:, l % 2, j * P:(j + 1) * P],
                                  m.v_sb[:, j, h * VH:(h + 1) * VH], start=(j == 0), stop=(j == i))
                    last.then_inc(o_psum, 1)


def output_and_router(nc, m, x, w_out_scaled, attn_post_g, ffn_pre_g, w_router):
    with ExitStack() as ctx:
        sem = m.sem

        gains_loaded = sem("gains_loaded")
        iotas_ready = sem("iotas_ready")
        mix_squares = sem("mix_squares")
        mix_mean = sem("mix_mean")
        mix_root = sem("mix_root")
        mix_normed = sem("mix_normed")
        mixT_psum = sem("mixT_psum")
        mixT_act = sem("mixT_act")
        mixT_dve = sem("mixT_dve")
        y_psum = sem("y_psum")
        y_squares = sem("y_squares")
        y_mean = sem("y_mean")
        y_root = sem("y_root")
        y_scaled = sem("y_scaled")
        x1_ready = sem("x1_ready")
        x1_squares = sem("x1_squares")
        x1_mean = sem("x1_mean")
        x1_root = sem("x1_root")
        h_ready = sem("h_ready")
        h_stored = [sem(f"h_stored{b}") for b in range(2)]
        hT_psum = sem("hT_psum")
        hT_act = sem("hT_act")
        hT_dve = sem("hT_dve")
        logits_psum = sem("logits_psum")
        logits_ready = sem("logits_ready")
        tops_ready = sem("tops_ready")
        exps_ready = sem("exps_ready")
        taken_ready = sem("taken_ready")
        ranks_psum = sem("ranks_psum")
        slots_ready = sem("slots_ready")
        list_written = sem("list_written")
        block = ctx.enter_context(nc.Block())
        mix_s = m.stat[:, 0:2 * T]
        ys, xs = m.stat[:, 16:20], m.stat[:, 20:24]
        top8 = m.scr[:, 0:64].rearrange("p (t k) -> p t k", t=T)
        idx8 = m.scr[:, 64:128].bitcast(U32).rearrange("p (t k) -> p t k", t=T)
        idxf = m.scr[:, 128:160].rearrange("p (t k) -> p t k", t=T)
        shifted = m.scr[:, 160:192].rearrange("p (t k) -> p t k", t=T)
        gate_sum = m.scr[:, 192:200]
        slotf = m.scr[:, 200:232].rearrange("p (t k) -> p t k", t=T)
        expert_no = m.scr[:, 256:288]
        first_slot = m.scr[:, 288:320]
        picked = m.scr[:, 1024:2048].rearrange("p (t k e) -> p t k e", t=T, k=TOPK)
        cnt, more, ends, jump = (m.scr[:, 320 + i * E:320 + (i + 1) * E] for i in range(4))
        number = m.scr[:, 448:448 + MORE + 1]
        tab = m.scr[0:1, 512:512 + 2 * TAB + 1]
        table3 = [m.scr[0:1, 2048 + i * 448:2048 + i * 448 + (MORE + 1) * E].rearrange("p (j e) -> p j e", e=E)
                  for i in range(2)]
        of_item = [m.scr[0:1, 640 + i * 16:640 + i * 16 + MORE + 1] for i in range(3)]

        @block.sync
        def _(sp):
            sp.dma_start(m.post_g, on_all(attn_post_g)).then_inc(gains_loaded, 16)
            sp.dma_start(m.ffn_g, on_all(ffn_pre_g)).then_inc(gains_loaded, 16)
            x_t = x.rearrange("b (t p) d -> p (b t) d", p=P)
            for t in range(T):
                sp.dma_start(m.x_sb[:, t, :], x_t[:, t, :]).then_inc(m.x_loaded[t], 16)
            sp.dma_start(m.w_router, w_router.rearrange("l (k p) e -> p (l k) e", p=P)).then_inc(gains_loaded, 16)
            h_t = m.h_rows.rearrange("(t p) d -> p t d", p=P)
            for t in range(T):
                sp.wait_ge(h_ready, t + 1)
                sp.dma_start(h_t[:, t, :], m.h_row[:, t % 2, :]).then_inc(h_stored[t % 2], 16)
            for b in range(2):
                sp.wait_ge(h_stored[b], 16 * (T // 2))

        @block.gpsimd
        def _(pool):
            g = nc.gpsimd
            step = Chain(m, pool, m.pool_step)
            exact = dict(allow_small_or_imprecise_dtypes=True)
            step(g.iota(expert_no, pattern=[[1, E]], base=0, channel_multiplier=0, **exact))
            step(g.iota(first_slot, pattern=[[CT, E]], base=0, channel_multiplier=0, **exact))
            step(g.iota(number, pattern=[[1, MORE + 1]], base=0, channel_multiplier=0, **exact), iotas_ready)
            pool.wait_ge(slots_ready, 1)
            for t in range(T):
                for k in range(TOPK):
                    pool.indirect_dma_start(m.choice_list, bass.IndirectOffsetOnAxis(m.slots[:, t, k:k + 1], 0),
                                            m.choice_ids[:, t, k, :], None).then_inc(list_written, 16)
            pool.wait_ge(list_written, 16 * T * TOPK)

        @block.scalar
        def _(act):
            s = nc.scalar
            step = Chain(m, act, m.act_step)
            for t in range(T):
                step(s.activation(m.junk[:, 0:512], m.o_sb[:, t, :], ACT.Square, accum_out=mix_s[:, t:t + 1]),
                     mix_squares)
                step(s.activation(m.junk[:, 512:1024], m.u_sg[:, t, :], ACT.Square,
                                  accum_out=mix_s[:, T + t:T + t + 1]), mix_squares)
            act.wait_ge(mix_mean, 1)
            step(s.activation(mix_s, mix_s, ACT.Sqrt), mix_root)
            for t in range(T):
                act.wait_ge(mixT_psum, t + 1)
                step(s.activation(m.mixT[:, 0:4, t * P:(t + 1) * P], m.bank(0).rearrange("p (k s) -> p k s", k=4),
                                  ACT.Copy), mixT_act)
            for t in range(T + 1):
                if t < T:
                    act.wait_ge(y_psum, t + 1)
                    b = 2 + 2 * (t % 2)
                    step(s.activation(m.junk[:, :], m.ps[:, b:b + 2, :].rearrange("p b c -> p (b c)"), ACT.Square,
                                      accum_out=ys[:, 0:1]), y_squares)
                    act.wait_ge(y_mean, t + 1)
                    step(s.activation(ys[:, 1:2], ys[:, 1:2], ACT.Sqrt), y_root)
                    act.wait_ge(x1_ready, t + 1)
                    step(s.activation(m.junk[:, :], m.x_sb[:, t, :], ACT.Square, accum_out=xs[:, 0:1]), x1_squares)
                    act.wait_ge(x1_mean, t + 1)
                    step(s.activation(xs[:, 1:2], xs[:, 1:2], ACT.Sqrt), x1_root)
                    act.wait_ge(hT_psum, t + 1)
                    if t >= 1:
                        act.wait_ge(logits_psum, t)
                    step(s.activation(m.hT[:, 0:4, :], m.bank(6).rearrange("p (k s) -> p k s", k=4), ACT.Copy),
                         hT_act)
            act.wait_ge(tops_ready, 1)
            step(s.activation(shifted, shifted, ACT.Exp), exps_ready)

        @block.vector
        def _(dve):
            v = nc.vector
            step = Chain(m, dve, m.dve_step)
            dve.wait_ge(mix_squares, 2 * T)
            step(v.tensor_scalar(mix_s, mix_s, 1.0 / SGW, EPS, ALU.mult, ALU.add), mix_mean)
            dve.wait_ge(mix_root, 1)
            step(v.reciprocal(mix_s, mix_s))
            for t in range(T + 1):
                if t < T:
                    step(v.tensor_scalar(m.o_sb[:, t, :], m.o_sb[:, t, :], mix_s[:, t:t + 1], None, ALU.mult))
                    step(v.tensor_scalar(m.u_sg[:, t, :], m.u_sg[:, t, :], mix_s[:, T + t:T + t + 1], None, ALU.mult),
                         mix_normed)
                if t >= 1:
                    dve.wait_ge(mixT_psum, t)
                    step(v.tensor_copy(m.mixT[:, 4:8, (t - 1) * P:t * P], m.bank(1).rearrange(
                        "p (k s) -> p k s", k=4)), mixT_dve)
            dve.wait_ge(gains_loaded, 48)
            for t in range(T):
                b = 2 + 2 * (t % 2)
                dve.wait_ge(y_squares, t + 1)
                step(v.tensor_scalar(ys[:, 1:2], ys[:, 0:1], 1.0 / D, EPS, ALU.mult, ALU.add), y_mean)
                dve.wait_ge(y_root, t + 1)
                step(v.reciprocal(ys[:, 2:3], ys[:, 1:2]))
                y = m.y_row[:, 0, :]
                step(v.scalar_tensor_tensor(y, m.ps[:, b:b + 2, :].rearrange("p b c -> p (b c)"), ys[:, 2:3],
                                            m.post_g, ALU.mult, ALU.mult), y_scaled)
                dve.wait_ge(m.x_loaded[t], 32)
                step(v.tensor_tensor(m.x_sb[:, t, :], m.x_sb[:, t, :], y, ALU.add), x1_ready)
                dve.wait_ge(x1_squares, t + 1)
                step(v.tensor_scalar(xs[:, 1:2], xs[:, 0:1], 1.0 / D, EPS, ALU.mult, ALU.add), x1_mean)
                dve.wait_ge(x1_root, t + 1)
                step(v.reciprocal(xs[:, 2:3], xs[:, 1:2]))
                if t >= 2:
                    dve.wait_ge(h_stored[t % 2], 16 * (t // 2))
                step(v.scalar_tensor_tensor(m.h_row[:, t % 2, :], m.x_sb[:, t, :], xs[:, 2:3], m.ffn_g, ALU.mult,
                                            ALU.mult), h_ready)
                dve.wait_ge(hT_psum, t + 1)
                if t >= 1:
                    dve.wait_ge(logits_psum, t)
                step(v.tensor_copy(m.hT[:, 4:8, :], m.bank(7).rearrange("p (k s) -> p k s", k=4)), hT_dve)
                dve.wait_ge(logits_psum, t + 1)
                step(v.tensor_tensor(m.logits[:, t, :], m.bank(0)[:, 0:E], m.b_r[:, :], ALU.add), logits_ready)
                step(v.max(top8[:, t, :], m.logits[:, t, :]))
                step(v.max_index(idx8[:, t, :], top8[:, t, :], m.logits[:, t, :]))
            step(v.tensor_tensor(shifted, top8[:, :, 0:TOPK], top8[:, :, 0:1].broadcast_to([P, T, TOPK]),
                                 ALU.subtract), tops_ready)
            step(v.tensor_copy(idxf, idx8[:, :, 0:TOPK]))
            dve.wait_ge(exps_ready, 1)
            step(v.tensor_reduce(out=gate_sum, in_=shifted, op=ALU.add, axis=AX.X))
            step(v.reciprocal(gate_sum, gate_sum))
            step(v.tensor_tensor(m.gates[:, :, :], shifted, gate_sum.unsqueeze(2).broadcast_to([P, T, TOPK]),
                                 ALU.mult))
            dve.wait_ge(iotas_ready, 1)
            for t in range(T):
                step(v.tensor_tensor(m.hot[:, t, :, :], expert_no.unsqueeze(1).broadcast_to([P, TOPK, E]),
                                     idxf[:, t, :].unsqueeze(2).broadcast_to([P, TOPK, E]), ALU.is_equal))
            step(v.tensor_tensor(m.taken, m.hot[:, :, 0, :], m.hot[:, :, 1, :], ALU.add))
            step(v.tensor_tensor(m.taken, m.taken, m.hot[:, :, 2, :], ALU.add))
            step(v.tensor_tensor(m.taken, m.taken, m.hot[:, :, 3, :], ALU.add), taken_ready)
            dve.wait_ge(ranks_psum, 2)
            step(v.tensor_copy(cnt, m.bank(3)[:, 0:E]))
            step(v.tensor_scalar(more, cnt, float(CT), None, ALU.is_gt))
            for c in range(2, SEQ // CT):
                step(v.scalar_tensor_tensor(more, cnt, float(c * CT), more, ALU.is_gt, ALU.add))
            step(v.tensor_tensor_scan(ends, m.ones[:, 0:E], more, 0.0, ALU.mult, ALU.add))
            step(v.tensor_tensor(jump, ends, more, ALU.subtract))
            step(v.tensor_scalar(jump, jump, float(E - 1), float(CT), ALU.add, ALU.mult))
            step(v.tensor_tensor(jump, jump, first_slot, ALU.subtract))
            ranks = m.bank(2)[:, 0:T * E].rearrange("p (t e) -> p t e", t=T)
            step(v.scalar_tensor_tensor(m.place, ranks, float(CT), jump.unsqueeze(1).broadcast_to([P, T, E]),
                                        ALU.is_ge, ALU.mult))
            step(v.tensor_tensor(m.place, m.place, ranks, ALU.add))
            step(v.tensor_tensor(m.place, m.place, first_slot.unsqueeze(1).broadcast_to([P, T, E]), ALU.add))
            for t in range(T):
                step(v.tensor_tensor(picked[:, t, :, :], m.hot[:, t, :, :],
                                     m.place[:, t, :].unsqueeze(1).broadcast_to([P, TOPK, E]), ALU.mult))
            step(v.tensor_reduce(out=slotf, in_=picked, op=ALU.add, axis=AX.X))
            step(v.tensor_copy(m.slots[:, :, :], slotf), slots_ready)
            over = [1, MORE + 1, E]
            passed, picks = table3
            chunk, left, valid = of_item
            experts, classes = tab[:, 0:TAB], tab[:, TAB:2 * TAB]
            step(v.tensor_tensor(passed, ends[0:1, :].unsqueeze(1).broadcast_to(over),
                                 number[0:1, :].unsqueeze(2).broadcast_to(over), ALU.is_le))
            step(v.tensor_copy(experts[:, 0:E], expert_no[0:1, :]))
            step(v.tensor_reduce(out=experts[:, E:TAB], in_=passed, op=ALU.add, axis=AX.X))
            step(v.tensor_scalar(experts[:, E:TAB], experts[:, E:TAB], float(E - 1), None, ALU.min))
            step(v.tensor_tensor(picks, passed, more[0:1, :].unsqueeze(1).broadcast_to(over), ALU.mult))
            step(v.tensor_reduce(out=chunk, in_=picks, op=ALU.add, axis=AX.X))
            step(v.tensor_tensor(chunk, number[0:1, :], chunk, ALU.subtract))
            step(v.tensor_scalar(chunk, chunk, -float(CT), -float(CT), ALU.mult, ALU.add))
            step(v.tensor_tensor(picks, expert_no[0:1, :].unsqueeze(1).broadcast_to(over),
                                 experts[:, E:TAB].unsqueeze(2).broadcast_to(over), ALU.is_equal))
            step(v.tensor_tensor(picks, picks, cnt[0:1, :].unsqueeze(1).broadcast_to(over), ALU.mult))
            step(v.tensor_reduce(out=left, in_=picks, op=ALU.add, axis=AX.X))
            step(v.tensor_tensor(left, left, chunk, ALU.add))
            for place, count in ((classes[:, 0:E], cnt[0:1, :]), (classes[:, E:TAB], left)):
                step(v.tensor_scalar(place, count, float(WIDTHS[0]), 1.0, ALU.is_gt, ALU.add))
                for w in WIDTHS[1:-1]:
                    step(v.scalar_tensor_tensor(place, count, float(w), place, ALU.is_gt, ALU.add))
            step(v.tensor_scalar(valid, number[0:1, :], ends[0:1, E - 1:E], None, ALU.is_lt))
            step(v.tensor_tensor(classes[:, E:TAB], classes[:, E:TAB], valid, ALU.mult))
            step(v.tensor_scalar(tab[:, 2 * TAB:2 * TAB + 1], ends[0:1, E - 1:E], float(E), None, ALU.add))
            step(v.tensor_copy(m.items[:, :], tab))

        @block.tensor
        def _(pe):
            mm, tr = nc.tensor.matmul, nc.tensor.transpose
            for t in range(T):
                pe.wait_ge(mix_normed, t + 1)
                if t >= 1:
                    pe.wait_ge(mixT_act, t)
                    pe.wait_ge(mixT_dve, t)
                for k in range(KD):
                    src = m.o_sb if k < 4 else m.u_sg
                    last = tr(m.bank(k // 4)[:, (k % 4) * P:(k % 4 + 1) * P],
                              src[:, t, (k % 4) * P:(k % 4 + 1) * P], m.ident[:, :])
                last.then_inc(mixT_psum, 1)
            pe.wait_ge(mixT_act, T)
            pe.wait_ge(mixT_dve, T)
            pe.wait_ge(w_out_scaled, KD)
            pe.wait_ge(gains_loaded, 48)
            for t in range(T + 1):
                if t < T:
                    if t >= 2:
                        pe.wait_ge(y_scaled, t - 1)
                    for k in range(KD):
                        for j in range(2):
                            last = mm(m.bank(2 + 2 * (t % 2) + j), m.mixT[:, k, t * P:(t + 1) * P],
                                      m.w_out[:, k, j * 512:(j + 1) * 512], start=(k == 0), stop=(k == KD - 1))
                    last.then_inc(y_psum, 1)
                if t >= 1:
                    pe.wait_ge(h_ready, t)
                    if t >= 2:
                        pe.wait_ge(hT_act, t - 1)
                        pe.wait_ge(hT_dve, t - 1)
                    for k in range(KD):
                        last = tr(m.bank(6 + k // 4)[:, (k % 4) * P:(k % 4 + 1) * P],
                                  m.h_row[:, (t - 1) % 2, k * P:(k + 1) * P], m.ident[:, :])
                    last.then_inc(hT_psum, 1)
                    pe.wait_ge(hT_act, t)
                    pe.wait_ge(hT_dve, t)
                    if t >= 2:
                        pe.wait_ge(logits_ready, t - 1)
                    for k in range(KD):
                        last = mm(m.bank(0)[:, 0:E], m.hT[:, k, :], m.w_router[:, k, :], start=(k == 0),
                                  stop=(k == KD - 1))
                    last.then_inc(logits_psum, 1)
            pe.wait_ge(taken_ready, 1)
            for t in range(T):
                for j in range(t + 1):
                    last = mm(m.bank(2)[:, t * E:(t + 1) * E], m.ones[:, :] if j < t else m.before[:, :],
                              m.taken[:, j, :], start=(j == 0), stop=(j == t))
            last.then_inc(ranks_psum, 1)
            for j in range(T):
                last = mm(m.bank(3)[:, 0:E], m.ones[:, :], m.taken[:, j, :], start=(j == 0), stop=(j == T - 1))
            last.then_inc(ranks_psum, 1)


def experts(nc, m, w_gate_up, w_down):
    with ExitStack() as ctx:
        sem = m.sem

        def sb(name, shape, dt=F32):
            return ctx.enter_context(nc.sbuf_tensor(name, shape, dt))

        unit_loaded = [sem(f"unit_loaded{r}") for r in range(RAW)]
        cleared = sem("rows_cleared")
        index_loaded = sem("index_loaded")
        index_taken = sem("index_taken")
        rows_gathered = sem("rows_gathered")
        rowsT_psum = sem("rowsT_psum")
        rowsT_ready = sem("rowsT_ready")
        bias_ready = sem("bias_ready")
        gate_psum = sem("gate_psum_moe")
        up_psum = sem("up_psum")
        gate_read = sem("gate_read")
        up_read = sem("up_read")
        up_clamped = sem("up_clamped")
        sigmoid_ready = sem("sigmoid_ready")
        silu_ready = sem("silu_ready")
        act_ready = sem("act_ready")
        down_psum = sem("down_psum")
        down_read = sem("down_read")
        yT_psum = sem("yT_psum")
        y_read = sem("y_read")
        y_stored = sem("y_stored")
        y_free = sem("y_free")

        raw = [sb(f"raw{r}", [P, KD, 256]) for r in range(RAW)]
        rows = sb("rows", [P, CH, D])
        rowsT = sb("rowsT", [P, KD, CT])
        gate = sb("gate", [P, 2, CT])
        up = sb("up", [P, 2, CT])
        sig = sb("sig", [P, 2, CT])
        act_f = sb("act_f", [P, KF, CT])
        yT = sb("yT", [P, 3, CT])
        y_out = sb("y_out", [P, CH, D])
        block = ctx.enter_context(nc.Block())

        def class_of(eng, i):
            return eng.value_load(m.items[0:1, bass.ds(i + TAB, 1)], min_val=0, max_val=len(WIDTHS))

        def unit_used(eng, i, u):
            if u >= GU_UNITS:
                eng.wait_ge(down_psum, i * KD + 2 * (u - GU_UNITS) + 3)
            else:
                eng.wait_ge(gate_psum if u % 2 == 0 else up_psum, i * KF + u - u % 2 + 2)

        @block.sync
        def _(sp):
            def load_unit(u, expert):
                if u < GU_UNITS:
                    src = w_gate_up.rearrange("l e (k p) n -> (l e) p k n", p=P)
                    c = (u // 2) * 256 + (u % 2) * F
                else:
                    src = w_down.rearrange("l e (k p) n -> (l e) p k n", p=P)
                    c = (u - GU_UNITS) * 256
                src = src[bass.ds(expert, 1), :, :, c:c + 256].rearrange("e p k n -> (e p) k n")
                sp.dma_start(raw[u % RAW][:, :, :], src).then_inc(unit_loaded[u % RAW], 16)

            for u in range(RAW):
                load_unit(u, 0)
            with sp.Fori(0, MAX_ITEMS) as i:
                with sp.If(class_of(sp, i) > 0):
                    this = sp.value_load(m.items[0:1, bass.ds(i, 1)], min_val=0, max_val=E - 1)
                    after = sp.value_load(m.items[0:1, bass.ds(i + 1, 1)], min_val=0, max_val=E - 1)
                    for u in range(RAW, N_UNITS + RAW):
                        unit_used(sp, i, u - RAW)
                        load_unit(u % N_UNITS, this if u < N_UNITS else after)
            n_items = sp.value_load(m.items[0:1, 2 * TAB:2 * TAB + 1], min_val=E, max_val=MAX_ITEMS)
            for r in range(RAW):
                sp.wait_ge(unit_loaded[r], n_items * (16 * N_UNITS // RAW) + 16)
            sp.sem_inc(m.sp_mark, 1)

        @block.gpsimd
        def _(pool):
            def load_index(item):
                whole = CT // P
                pool.dma_start(m.idx_next[:, 0:whole, :], m.choice_list[bass.ds(item * CT, whole * P), :].rearrange(
                    "(c p) o -> p c o", p=P)).then_inc(index_loaded, 16)
                pool.dma_start(m.idx_next[0:CT - whole * P, whole, :],
                               m.choice_list[bass.ds(item * CT + whole * P, CT - whole * P), :]
                               ).then_inc(index_loaded, 16)

            def gather():
                for c in range(CH):
                    pool.indirect_dma_start(rows[:, c, :], None, m.h_rows,
                                            bass.IndirectOffsetOnAxis(m.idx_next[:, c, 0:1], 0),
                                            bounds_check=SEQ - 1, oob_is_err=False).then_inc(rows_gathered, 16)

            load_index(0)
            pool.wait_ge(cleared, 2)
            pool.wait_ge(index_loaded, 32)
            gather()
            pool.sem_inc(y_free, 1)
            with pool.Fori(0, MAX_ITEMS) as i:
                with pool.If(class_of(pool, i) > 0):
                    pool.wait_ge(rows_gathered, i * (16 * CH) + 16 * CH)
                    pool.sem_inc(m.pool_mark, 1)
                    nc.gpsimd.tensor_copy(m.idx_now[:, :, :], m.idx_next[:, :, :]).then_inc(index_taken, 1)
                    pool.wait_ge(index_taken, i + 1)
                    load_index(i + 1)
                    pool.wait_ge(rowsT_psum, i * KD + KD)
                    pool.wait_ge(index_loaded, i * 32 + 64)
                    pool.sem_inc(m.pool_mark, 1)
                    gather()
                    pool.wait_ge(y_read, i * 2 + 3)
                    pool.sem_inc(m.pool_mark, 1)
                    for c in range(CH):
                        pool.indirect_dma_start(m.y_choices, bass.IndirectOffsetOnAxis(m.idx_now[:, c, 1:2], 0),
                                                y_out[:, c, :], None, bounds_check=SEQ * TOPK - 1,
                                                oob_is_err=False).then_inc(y_stored, 16)
                    pool.wait_ge(y_stored, i * (16 * CH) + 16 * CH)
                    pool.sem_inc(y_free, 1)

        @block.scalar
        def _(act):
            s = nc.scalar

            def rows_out(base, k):
                act.wait_ge(rowsT_psum, base + (k + 1))
                s.activation(rowsT[:, k, :], m.bank(2 + k % 2)[:, 0:CT], ACT.Copy).then_inc(rowsT_ready, 1)

            def y_part(i, part, n):
                act.wait_ge(yT_psum, i * KD + 4 * part + 4)
                if part == 0:
                    act.wait_ge(y_free, i + 1)
                for c in range(-(-n // P)):
                    r = min(P, n - c * P)
                    last = s.activation(y_out[0:r, c, part * 512:(part + 1) * 512],
                                        m.bank(Y_BANKS[c], r), ACT.Copy)
                last.then_inc(y_read, 1)

            act.sem_inc(y_read, 1)
            for k in range(KD):
                rows_out(0, k)
            with act.Fori(0, MAX_ITEMS) as i:
                cls = class_of(act, i)
                for w, n in enumerate(WIDTHS):
                    with act.If(cls == w + 1):
                        for pair in range(KF // 2):
                            act.wait_ge(gate_read, i * KF + 2 * pair + 4)
                            if pair >= 1:
                                act.wait_ge(silu_ready, i * (KF // 2) + pair)
                            s.activation(sig[:, :, 0:n], gate[:, :, 0:n], ACT.Sigmoid,
                                         scale=ALPHA).then_inc(sigmoid_ready, 1)
                        for k in range(KD):
                            rows_out(i * KD + KD, k)
                            if k == 5:
                                y_part(i, 0, n)
                        y_part(i, 1, n)

        @block.vector
        def _(dve):
            v = nc.vector

            def down_out(i, d, n):
                dve.wait_ge(down_psum, i * KD + d + 2)
                v.tensor_scalar(yT[:, d % 3, 0:n], m.bank(6 + d % 2)[:, 0:n],
                                m.bias_now[:, 2 * KF + d:2 * KF + d + 1], None, ALU.add).then_inc(down_read, 1)

            v.memset(rows[:, :, :], 0.0).then_inc(cleared, 1)
            v.memset(y_out[:, :, :], 0.0).then_inc(cleared, 1)
            dve.sem_inc(gate_read, 2)
            dve.sem_inc(up_read, 2)
            dve.sem_inc(down_read, 2)
            half = KF // 2
            with dve.Fori(0, MAX_ITEMS) as i:
                cls = class_of(dve, i)
                for w, n in enumerate(WIDTHS):
                    with dve.If(cls == w + 1):
                        expert = dve.value_load(m.items[0:1, bass.ds(i, 1)], min_val=0, max_val=E - 1)
                        dve.wait_ge(down_read, i * KD + 2)
                        v.tensor_copy(m.bias_now[:, :], m.bias_cols[:, :, bass.ds(expert, 1)].rearrange(
                            "p c e -> p (c e)")).then_inc(bias_ready, 1)
                        dve.wait_ge(bias_ready, i + 1)
                        for pair in range(half):
                            for c in range(2):
                                f = 2 * pair + c
                                dve.wait_ge(gate_psum, i * KF + f + 1)
                                v.tensor_scalar(gate[:, c, 0:n], m.bank(2 + c)[:, 0:n], m.bias_now[:, f:f + 1],
                                                LIMIT, ALU.add, ALU.min).then_inc(gate_read, 1)
                            for c in range(2):
                                f = 2 * pair + c
                                dve.wait_ge(up_psum, i * KF + f + 1)
                                v.tensor_scalar(up[:, c, 0:n], m.bank(4 + c)[:, 0:n],
                                                m.bias_now[:, KF + f:KF + f + 1], LIMIT, ALU.add,
                                                ALU.min).then_inc(up_read, 1)
                            dve.wait_ge(up_read, i * KF + 2 * pair + 4)
                            v.tensor_scalar(up[:, :, 0:n], up[:, :, 0:n], -LIMIT, 1.0, ALU.max,
                                            ALU.add).then_inc(up_clamped, 1)
                            dve.wait_ge(sigmoid_ready, i * half + pair + 1)
                            v.tensor_tensor(gate[:, :, 0:n], gate[:, :, 0:n], sig[:, :, 0:n],
                                            ALU.mult).then_inc(silu_ready, 1)
                            dve.wait_ge(up_clamped, i * half + pair + 1)
                            dve.wait_ge(silu_ready, i * half + pair + 1)
                            v.tensor_tensor(act_f[:, 2 * pair:2 * pair + 2, 0:n], gate[:, :, 0:n], up[:, :, 0:n],
                                            ALU.mult).then_inc(act_ready, 1)
                            dve.wait_ge(act_ready, i * half + pair + 1)
                        for d in range(KD):
                            down_out(i, d, n)

        @block.tensor
        def _(pe):
            tr = nc.tensor.transpose

            def product(bank, u, c, x, ks, n):
                for k in ks:
                    last = nc.tensor.matmul(bank[:, 0:n], raw[u % RAW][:, k, c * P:(c + 1) * P], x[:, k, 0:n],
                                            start=(k == 0), stop=(k == KD - 1))
                return last

            def unit_here(i, u):
                pe.wait_ge(unit_loaded[u % RAW], i * (16 * N_UNITS // RAW) + 16 * (u // RAW + 1))

            def transpose_rows(k):
                for c in range(CH):
                    r = min(P, CT - c * P)
                    last = tr(m.bank(2 + k % 2)[:, c * P:c * P + r], rows[0:r, c, k * P:(k + 1) * P],
                              m.ident[0:r, 0:r])
                last.then_inc(rowsT_psum, 1)

            def transpose_out(i, e, n):
                pe.wait_ge(down_read, i * KD + e + 3)
                if e % 4 == 0:
                    pe.wait_ge(y_read, i * 2 + e // 4 + 1)
                for c in range(-(-n // P)):
                    r = min(P, n - c * P)
                    last = tr(m.bank(Y_BANKS[c], r)[:, (e % 4) * P:(e % 4 + 1) * P], yT[:, e % 3, c * P:c * P + r],
                              m.ident[:, :])
                last.then_inc(yT_psum, 1)

            pe.sem_inc(down_psum, 1)
            pe.wait_ge(rows_gathered, 16 * CH)
            for k in range(KD):
                if k >= 2:
                    pe.wait_ge(rowsT_ready, k - 1)
                transpose_rows(k)
            with pe.Fori(0, MAX_ITEMS) as i:
                cls = class_of(pe, i)
                for w, n in enumerate(WIDTHS):
                    with pe.If(cls == w + 1):
                        pe.wait_ge(rowsT_ready, i * KD + KD)
                        for u in range(GU_UNITS):
                            unit_here(i, u)
                            if u == 1:
                                pe.wait_ge(y_read, i * 2 + 1)
                            read, done = (gate_read, gate_psum) if u % 2 == 0 else (up_read, up_psum)
                            for c in range(2):
                                pe.wait_ge(read, i * KF + u - u % 2 + c + 1)
                                product(m.bank(2 + 2 * (u % 2) + c), u, c, rowsT, range(KD),
                                        n).then_inc(done, 1)
                        unit_here(i, GU_UNITS)
                        for c in range(2):
                            pe.wait_ge(down_read, i * KD + c + 1)
                            for pair in range(KF // 2 - 1):
                                if c == 0:
                                    pe.wait_ge(act_ready, i * (KF // 2) + pair + 1)
                                product(m.bank(6 + c), GU_UNITS, c, act_f, (2 * pair, 2 * pair + 1), n)
                        pe.wait_ge(act_ready, i * (KF // 2) + KF // 2)
                        for c in range(2):
                            product(m.bank(6 + c), GU_UNITS, c, act_f, (KF - 2, KF - 1),
                                    n).then_inc(down_psum, 1)
                        pe.wait_ge(rows_gathered, i * (16 * CH) + 32 * CH)
                        pe.wait_ge(gate_read, i * KF + KF + 2)
                        for k in range(2):
                            transpose_rows(k)
                        for d in range(2, KD):
                            u = GU_UNITS + d // 2
                            if d % 2 == 0:
                                unit_here(i, u)
                            pe.wait_ge(down_read, i * KD + d + 1)
                            product(m.bank(6 + d % 2), u, d % 2, act_f, range(KF), n).then_inc(down_psum, 1)
                            transpose_out(i, d - 2, n)
                            pe.wait_ge(rowsT_ready, i * KD + KD + d - 1)
                            transpose_rows(d)
                        for e in (KD - 2, KD - 1):
                            transpose_out(i, e, n)


def combine_and_embed(nc, m, p, ffn_post_g, w_ple_gate, b_ple_gate, w_ple_proj, ple_norm_g, out):
    with ExitStack() as ctx:
        sem = m.sem

        weights_loaded = sem("weights_loaded")
        rows_gathered = [sem(f"choices_gathered{b}") for b in range(2)]
        rows_used = sem("rows_used")
        y_ready = sem("y_ready")
        y_squares = sem("y_squares6")
        y_mean = sem("y_mean6")
        y_root = sem("y_root6")
        x2_ready = sem("x2_ready")
        inT_psum = sem("inT_psum")
        inT_act = sem("inT_act")
        inT_dve = sem("inT_dve")
        gate_psum = sem("gate_psum")
        gate_biased = sem("gate_biased")
        gate_done = sem("gate_done")
        gated = sem("gated")
        gated_squares = sem("gated_squares")
        gated_mean = sem("gated_mean")
        gated_root = sem("gated_root")
        out_ready = sem("out_ready")
        out_stored = sem("out_stored")
        block = ctx.enter_context(nc.Block())
        rg, wk = (ctx.enter_context(nc.sbuf_tensor(n, [P, c], F32)) for n, c in (("late", 18688), ("late_rows", 16384)))
        w_gate = rg[:, 0:8192].rearrange("p (k n) -> p k n", k=KD)
        w_proj = rg[:, 8192:10240].rearrange("p (k n) -> p k n", k=KP)
        p_sb = rg[:, 10240:12288].rearrange("p (t d) -> p t d", t=T)
        post_g, gate_b, norm_g = (rg[:, 12288 + i * D:12288 + (i + 1) * D] for i in range(3))
        inT = rg[:, 15360:15360 + 1280].rearrange("p (k s) -> p k s", k=KD + KP)
        gate_row = rg[:, 16640:17664]
        y_acc = rg[:, 17664:18688]
        choices = wk[:, 0:8192].rearrange("p (b k d) -> p b k d", b=2, k=TOPK)
        prod = wk[:, 8192:16384].rearrange("p (t d) -> p t d", t=T)
        ss = m.stat[:, 0:4]
        gs = m.stat[:, 8:16]

        @block.sync
        def _(sp):
            sp.dma_start(post_g, on_all(ffn_post_g)).then_inc(weights_loaded, 16)
            sp.dma_start(gate_b, on_all(b_ple_gate)).then_inc(weights_loaded, 16)
            sp.dma_start(norm_g, on_all(ple_norm_g)).then_inc(weights_loaded, 16)
            sp.dma_start(p_sb, p.rearrange("l b (t p) d -> p (l b t) d", p=P)).then_inc(weights_loaded, 16)
            sp.dma_start(w_gate, w_ple_gate.rearrange("l (k p) n -> p (l k) n", p=P)).then_inc(weights_loaded, 16)
            sp.dma_start(w_proj, w_ple_proj.rearrange("l (k p) n -> p (l k) n", p=P)).then_inc(weights_loaded, 16)
            out_t = out.rearrange("b (t p) d -> p (b t) d", p=P)
            y_t = m.y_choices.rearrange("(t p k) d -> p t (k d)", p=P, k=TOPK)
            for t in range(T):
                if t >= 2:
                    sp.wait_ge(rows_used, t - 1)
                sp.dma_start(choices[:, t % 2, :, :].rearrange("p k d -> p (k d)"), y_t[:, t, :]
                             ).then_inc(rows_gathered[t % 2], 16)
            for t in range(T):
                sp.wait_ge(out_ready, t + 1)
                sp.dma_start(out_t[:, t, :], m.x_sb[:, t, :]).then_inc(out_stored, 16)
            sp.wait_ge(out_stored, 16 * T)

        @block.scalar
        def _(act):
            s = nc.scalar
            step = Chain(m, act, m.act_step)
            for t in range(T):
                act.wait_ge(y_ready, t + 1)
                step(s.activation(m.junk[:, :], y_acc, ACT.Square, accum_out=ss[:, 0:1]), y_squares)
                act.wait_ge(y_mean, t + 1)
                step(s.activation(ss[:, 1:2], ss[:, 1:2], ACT.Sqrt), y_root)
                act.wait_ge(inT_psum, t + 1)
                step(s.activation(inT[:, 0:4, :], m.bank(0).rearrange("p (k s) -> p k s", k=4), ACT.Copy))
                step(s.activation(inT[:, KD:KD + KP, :], m.bank(7)[:, 0:KP * P].rearrange("p (k s) -> p k s", k=KP),
                                  ACT.Copy), inT_act)
                act.wait_ge(gate_biased, t + 1)
                step(s.activation(gate_row, gate_row, ACT.Sigmoid), gate_done)
                act.wait_ge(gated, t + 1)
                step(s.activation(m.junk[:, :], prod[:, t, :], ACT.Square, accum_out=gs[:, t:t + 1]), gated_squares)
            act.wait_ge(gated_mean, 1)
            step(s.activation(gs, gs, ACT.Sqrt), gated_root)

        @block.vector
        def _(dve):
            v = nc.vector
            step = Chain(m, dve, m.dve_step)
            dve.wait_ge(weights_loaded, 96)
            for t in range(T):
                dve.wait_ge(rows_gathered[t % 2], 16 * (t // 2 + 1))
                step(v.tensor_scalar(y_acc, choices[:, t % 2, 0, :], m.gates[:, t, 0:1], None, ALU.mult))
                for k in range(1, TOPK):
                    step(v.scalar_tensor_tensor(y_acc, choices[:, t % 2, k, :], m.gates[:, t, k:k + 1], y_acc,
                                                ALU.mult, ALU.add), y_ready if k == TOPK - 1 else None)
                dve.wait_ge(y_squares, t + 1)
                step(v.tensor_scalar(ss[:, 1:2], ss[:, 0:1], 1.0 / D, EPS, ALU.mult, ALU.add), y_mean)
                dve.wait_ge(y_root, t + 1)
                step(v.reciprocal(ss[:, 2:3], ss[:, 1:2]))
                step(v.scalar_tensor_tensor(y_acc, y_acc, ss[:, 2:3], post_g, ALU.mult, ALU.mult), rows_used)
                step(v.tensor_tensor(m.x_sb[:, t, :], m.x_sb[:, t, :], y_acc, ALU.add), x2_ready)
                dve.wait_ge(inT_psum, t + 1)
                step(v.tensor_copy(inT[:, 4:8, :], m.bank(1).rearrange("p (k s) -> p k s", k=4)), inT_dve)
                dve.wait_ge(gate_psum, t + 1)
                step(v.tensor_tensor(gate_row, m.ps[:, 2:4, :].rearrange("p b c -> p (b c)"), gate_b, ALU.add),
                     gate_biased)
                dve.wait_ge(gate_done, t + 1)
                step(v.tensor_tensor(prod[:, t, :], m.ps[:, 4:6, :].rearrange("p b c -> p (b c)"), gate_row,
                                     ALU.mult), gated)
            dve.wait_ge(gated_squares, T)
            step(v.tensor_scalar(gs, gs, 1.0 / D, EPS, ALU.mult, ALU.add), gated_mean)
            dve.wait_ge(gated_root, 1)
            step(v.reciprocal(gs, gs))
            for t in range(T):
                step(v.scalar_tensor_tensor(prod[:, t, :], prod[:, t, :], gs[:, t:t + 1], norm_g, ALU.mult,
                                            ALU.mult))
                step(v.tensor_tensor(m.x_sb[:, t, :], m.x_sb[:, t, :], prod[:, t, :], ALU.add), out_ready)

        @block.tensor
        def _(pe):
            mm, tr = nc.tensor.matmul, nc.tensor.transpose
            pe.wait_ge(weights_loaded, 96)
            for t in range(T):
                pe.wait_ge(x2_ready, t + 1)
                if t >= 1:
                    pe.wait_ge(inT_act, t)
                    pe.wait_ge(inT_dve, t)
                    pe.wait_ge(gated, t)
                for k in range(KD):
                    tr(m.bank(k // 4)[:, (k % 4) * P:(k % 4 + 1) * P], m.x_sb[:, t, k * P:(k + 1) * P], m.ident[:, :])
                for k in range(KP):
                    last = tr(m.bank(7)[:, k * P:(k + 1) * P], p_sb[:, t, k * P:(k + 1) * P], m.ident[:, :])
                last.then_inc(inT_psum, 1)
                pe.wait_ge(inT_act, t + 1)
                pe.wait_ge(inT_dve, t + 1)
                for j in range(2):
                    for k in range(KP):
                        mm(m.bank(4 + j), inT[:, KD + k, :], w_proj[:, k, j * 512:(j + 1) * 512], start=(k == 0),
                           stop=(k == KP - 1))
                for j in range(2):
                    for k in range(KD):
                        last = mm(m.bank(2 + j), inT[:, k, :], w_gate[:, k, j * 512:(j + 1) * 512], start=(k == 0),
                                  stop=(k == KD - 1))
                last.then_inc(gate_psum, 1)


def decoder_layer(nc, x, p, positions, attn_pre_g, w_in, q_norm_g, w_uq, kv_norm_g, w_ukv, sg_norm_g, w_spatial,
                  b_spatial, mla_out_g, sg_out_g, w_out, attn_post_g, ffn_pre_g, w_router, b_router, w_gate_up,
                  b_gate_up, w_down, b_down, ffn_post_g, w_ple_gate, b_ple_gate, w_ple_proj, ple_norm_g, out):
    with ExitStack() as ctx:
        ctx.enter_context(nc.allow_non_contiguous_dma(reason="vectors of 1024 elements as columns"))
        m = Buffers(nc, ctx)
        with ExitStack() as early:
            m.open_early(nc, early)
            input_projection(nc, m, x, positions, attn_pre_g, w_in, q_norm_g, w_uq, kv_norm_g, w_ukv, b_spatial,
                             mla_out_g, sg_out_g, b_router, b_gate_up, b_down)
            attention_operands(nc, m, w_spatial, sg_norm_g)
            w_out_loaded, w_out_scaled = m.sem("w_out_loaded"), m.sem("w_out_scaled")
            attention(nc, m, w_out, w_out_loaded, w_out_scaled)
            output_and_router(nc, m, x, w_out_scaled, attn_post_g, ffn_pre_g, w_router)
        experts(nc, m, w_gate_up, w_down)
        combine_and_embed(nc, m, p, ffn_post_g, w_ple_gate, b_ple_gate, w_ple_proj, ple_norm_g, out)


_INS = ["x", "p", "positions", "attn_pre_g", "w_in", "q_norm_g", "w_uq", "kv_norm_g", "w_ukv", "sg_norm_g",
        "w_spatial", "b_spatial", "mla_out_g", "sg_out_g", "w_out", "attn_post_g", "ffn_pre_g", "w_router",
        "b_router", "w_gate_up", "b_gate_up", "w_down", "b_down", "ffn_post_g", "w_ple_gate", "b_ple_gate",
        "w_ple_proj", "ple_norm_g"]


def kernel(**inputs):
    import concourse.bacc as bacc
    from concourse.bass_utils import run_bass_kernel_spmd

    nc = bacc.Bacc("TRN2", target_bir_lowering=False, num_devices=1)
    arrays, args = {}, []
    for name in _INS:
        a = np.ascontiguousarray(inputs[name])
        arrays[f"in_{name}"] = a
        args.append(nc.dram_tensor(f"in_{name}", a.shape, mybir.dt.from_np(a.dtype), kind="ExternalInput").ap())
    out = nc.dram_tensor("out", (1, SEQ, D), F32, kind="ExternalOutput").ap()
    decoder_layer(nc, *args, out)
    r = run_bass_kernel_spmd(nc, [arrays], core_ids=[0])
    return r.results[0]["out"]
```

```python
from contextlib import ExitStack

import numpy as np

import concourse.bass as bass
from concourse import mybir

ALU = mybir.AluOpType
ACT = mybir.ActivationFunctionType
AX = mybir.AxisListType
F32 = mybir.dt.float32
I32 = mybir.dt.int32
U32 = mybir.dt.uint32

P = 128
D = 1024
SEQ = 1024
T = SEQ // P
KD = D // P
H = 8
NOPE, ROPE, VH = 64, 32, 64
HR = ROPE // 2
QK = NOPE + ROPE
QL, KVL = 256, 128
QC = QL // P
A_COLS = QL + KVL + ROPE
SGW = 512
IN_COLS = A_COLS + 2 * SGW
HC = SGW // H
E = 32
TOPK = 4
F = 1024
KF = F // P
DP = 256
KP = DP // P
EPS = 1e-6
SCALE = float(QK) ** -0.5
LIMIT, ALPHA = 7.0, 1.702
TILE_ORDER = (0, 2, 4, 6, 7, 5, 3, 1)
THETA = 10000.0
NEG = -3.0e38
TWO_PI = 2 * np.pi
PI_A = 6.28125
PI_B = float(TWO_PI - PI_A)
ROUND = 1.5 * 2.0 ** 23
R_MAX = 3.1415925

CT = 320
CH = -(-CT // P)
REGION = -(-SEQ // CT) * CT
GROUP = 4
MORE = -(-(TOPK * SEQ // (CT + 1)) // GROUP) * GROUP
MAX_ITEMS = E + MORE
TAB = MAX_ITEMS + 1
WIDTHS = (128, 136, 144, 160, 176, 200, 256, 320)
EMPTY = 1 << 20
N_UNITS = 12
GU_UNITS = 8
RAW = 6
Y_BANKS = (0, 1, 4)


class Chain:

    def __init__(self, m, eng, own):
        self.eng, self.own, self.count = eng, own, m.count

    def __call__(self, ins, signal=None):
        s = self.own if signal is None else signal
        self.count[s.name] = self.count.get(s.name, 0) + 1
        ins.then_inc(s, 1)
        self.eng.wait_ge(s, self.count[s.name])


class Buffers:

    def __init__(self, nc, ctx):
        def sb(name, shape, dt=F32):
            return ctx.enter_context(nc.sbuf_tensor(name, shape, dt))

        self.sem = lambda name: ctx.enter_context(nc.semaphore(name))
        self.count = {}
        self.mark = self.sem("mark")
        self.act_step, self.dve_step, self.pool_step = (self.sem(f"{e}_step") for e in ("act", "dve", "pool"))
        self.x_loaded = [self.sem(f"x_loaded{t}") for t in range(T)]
        self.list_written = self.sem("list_written")
        self.mix_squares = self.sem("mix_squares")
        self.h_rows = nc.dram_tensor("h_rows", [SEQ, D], F32).ap()
        self.choice_list = nc.dram_tensor("choice_list", [E * REGION, 2], I32).ap()
        self.y_choices = nc.dram_tensor("y_choices", [SEQ * TOPK, D], F32).ap()
        self.ps = ctx.enter_context(nc.psum_tensor("ps", [P, 8, 512], F32))

        xa = sb("xa", [P, T * D])
        self.xa = xa
        self.x_sb = xa[:, :].rearrange("p (t d) -> p t d", t=T)
        self.za = xa[:, 0:T * A_COLS].rearrange("p (t c) -> p t c", t=T)
        self.qT = xa[0:QK, :].rearrange("p (h s) -> p h s", h=H)
        self.junk = sb("junk", [P, D])
        self.ident = sb("ident", [P, P])
        self.causal = sb("causal", [P, P])
        self.before = sb("before", [P, P])
        self.ones = sb("ones", [P, P])
        self.gains = sb("gains", [P, 20])
        self.stat = sb("stat", [P, 160])
        self.eps = sb("eps", [P, 1])
        self.cosb = sb("cosb", [P, T, HR])
        self.sinb = sb("sinb", [P, T, HR])
        self.rtmp = [sb(f"rtmp{i}", [P, T, HR]) for i in range(4)]
        self.invf = sb("invf", [P, HR])
        self.posi = sb("posi", [P, T], I32)
        self.posf = sb("posf", [P, T])
        self.small_row = sb("small_row", [P, 256])
        self.b_sp = sb("b_sp", [P, H])
        self.b_r = sb("b_r", [P, E])
        self.gates = sb("gates", [P, T, TOPK])
        self.slots = sb("slots", [P, T, TOPK], I32)
        self.choice_ids = sb("choice_ids", [P, T, TOPK, 2], I32)
        self.items = sb("items", [1, 3 * TAB + 1], I32)
        self.bias_cols = sb("bias_cols", [P, 2 * KF + KD, E])
        self.bias_now = sb("bias_now", [P, 2 * KF + KD])
        self.idx_next = sb("idx_next", [P, CH, 2], I32)
        self.idx_now = sb("idx_now", [P, CH, 2], I32)
        self.mix_s = self.stat[:, 128:128 + 2 * T]
        self.g_x, self.g_q, self.g_kv = self.gains[:, 0:8], self.gains[:, 8:10], self.gains[:, 10:11]
        self.g_mix = self.gains[:, 11:19]

    def open_early(self, nc, ctx):
        ring = ctx.enter_context(nc.sbuf_tensor("ring", [P, 24576], F32))
        work = ctx.enter_context(nc.sbuf_tensor("work", [P, 16384], F32))
        self.work = work
        self.ring = ring
        n_in = KD * IN_COLS
        self.w_in = ring[:, 0:n_in].rearrange("p (k n) -> p k n", k=KD)
        self.w_uq = ring[:, n_in:n_in + 1536].rearrange("p (k n) -> p k n", k=QC)
        self.w_ukv = ring[:, 13056:14080].rearrange("p (h n) -> p h n", h=H)
        self.cqT = ring[:, 14080:16128].rearrange("p (k s) -> p k s", k=QC)
        self.ckvT = ring[:, 16128:17152]
        self.krT = ring[0:QK, 17152:18176]
        self.v_sb = ring[:, 0:4096].rearrange("p (t n) -> p t n", t=T)
        self.probs = ring[:, 4096:6144].rearrange("p (b s) -> p b s", b=2)
        self.probsT = ring[:, 6144:8192].rearrange("p (b s) -> p b s", b=2)
        self.w_spT = ring[:, 8192:9216].rearrange("p (h s) -> p h s", h=H)
        self.w_sp = ring[:, 9216:10240].rearrange("p (h s) -> p h s", h=H)
        self.sg_g = ring[:, 18176:18688]
        self.w_out = ring[:, 12288:20480].rearrange("p (k n) -> p k n", k=KD)
        self.o_sb = ring[:, 20480:24576].rearrange("p (t c) -> p t c", t=T)
        self.post_g = ring[:, 0:1024]
        self.ffn_g = ring[:, 1024:2048]
        self.y_row = ring[:, 2048:4096].rearrange("p (b d) -> p b d", b=2)
        self.h_row = ring[:, 4096:6144].rearrange("p (b d) -> p b d", b=2)
        self.hT = ring[:, 6144:7168].rearrange("p (k s) -> p k s", k=KD)
        self.w_router = ring[:, 7168:7424].rearrange("p (k e) -> p k e", k=KD)
        self.logits = ring[:, 7424:7680].rearrange("p (t e) -> p t e", t=T)
        self.hot = ring[:, 7680:8704].rearrange("p (t k e) -> p t k e", t=T, k=TOPK)
        self.taken = ring[:, 8704:8960].rearrange("p (t e) -> p t e", t=T)
        self.place = ring[:, 8960:9216].rearrange("p (t e) -> p t e", t=T)
        self.scr = ring[:, 9216:12288]
        self.xT = work[:, 0:8192].rearrange("p (k s) -> p k s", k=KD)
        self.kT = work[0:QK, 0:8192].rearrange("p (h s) -> p h s", h=H)
        self.mixT = work[:, 0:8192].rearrange("p (k s) -> p k s", k=KD)
        self.u_sg = work[:, 8192:12288].rearrange("p (t c) -> p t c", t=T)
        self.v_sg = work[:, 12288:16384].rearrange("p (t c) -> p t c", t=T)

    def bank(self, i, rows=P):
        return self.ps[0:rows, i, :]


def columns(vector, k):
    return vector.rearrange("l (k p) -> p (l k)", k=k)


def on_all(vector):
    return vector.rearrange("l n -> (l n)").partition_broadcast(P)


def rope(v, step, x1, x2, cos, sin, tmp, signal=None):
    step(v.tensor_tensor(tmp[0], x1, cos, ALU.mult))
    step(v.tensor_tensor(tmp[1], x2, sin, ALU.mult))
    step(v.tensor_tensor(tmp[2], x2, cos, ALU.mult))
    step(v.tensor_tensor(tmp[3], x1, sin, ALU.mult))
    step(v.tensor_tensor(x1, tmp[0], tmp[1], ALU.subtract))
    step(v.tensor_tensor(x2, tmp[2], tmp[3], ALU.add), signal)


def input_projection(nc, m, x, positions, attn_pre_g, w_in, q_norm_g, w_uq, kv_norm_g, w_ukv, sg_norm_g, b_spatial,
                     mla_out_g, sg_out_g, b_router, b_gate_up, b_down):
    with ExitStack() as ctx:
        sem = m.sem

        x_loaded = m.x_loaded
        biases_loaded = sem("biases_loaded")
        gain_loaded = sem("gain_loaded")
        small_loaded = sem("small_loaded")
        w_in_loaded = [sem(f"w_in_loaded{k}") for k in range(KD // 2)]
        w_mid_loaded = sem("w_mid_loaded")
        consts_ready = sem("consts_ready")
        w_in_act = sem("w_in_act")
        w_in_dve = sem("w_in_dve")
        biasT_psum = sem("biasT_psum")
        biasT_copied = sem("biasT_copied")
        xT_psum = sem("xT_psum")
        xT_act = sem("xT_act")
        xT_dve = sem("xT_dve")
        root_x = sem("root_x")
        rstd_x = sem("rstd_x")
        angles = sem("angles")
        sines = sem("sines")
        z_psum = sem("z_psum")
        z_latent = sem("z_latent")
        z_gated = sem("z_gated")
        root_latent = sem("root_latent")
        latent_ready = sem("latent_ready")
        v_root = sem("v_root")
        v_gelu_squares = sem("v_gelu_squares")
        v_squared = sem("v_squared")
        latent_squares = sem("latent_squares")
        latentT_psum = sem("latentT_psum")
        latentT_copied = sem("latentT_copied")
        block = ctx.enter_context(nc.Block())
        bgu_rows = m.work[0:E, 8192:8192 + 2 * F]
        bd_rows = m.work[0:E, 8192 + 2 * F:8192 + 2 * F + D]
        ms = m.stat[:, T:2 * T]
        lat = m.stat[:, 2 * T:4 * T].rearrange("p (t c) -> p t c", t=T)
        sgs = m.stat[:, 32:32 + T * H].rearrange("p (t h) -> p t h", t=T)
        v_squares = m.ring[:, 18688:18688 + SGW]
        eps = m.eps[:, :]
        n_bias = 2 * KF + KD

        @block.sync
        def _(sp):
            x_t = x.rearrange("b (t p) d -> p (b t) d", p=P)
            wi = w_in.rearrange("l (k p) n -> p (l k) n", p=P)
            for t in range(T):
                sp.dma_start(m.x_sb[:, t, :], x_t[:, t, :]).then_inc(x_loaded[t], 16)
                if t == 1:
                    sp.dma_start(bgu_rows, b_gate_up.rearrange("l e n -> (l e) n")).then_inc(biases_loaded, 16)
                    sp.dma_start(bd_rows, b_down.rearrange("l e n -> (l e) n")).then_inc(biases_loaded, 16)
                    for k in range(0, KD, 2):
                        sp.dma_start(m.w_in[:, k:k + 2, :], wi[:, k:k + 2, :]).then_inc(w_in_loaded[k // 2], 16)
            sp.dma_start(m.sg_g, on_all(sg_norm_g.rearrange("l h c -> l (h c)"))).then_inc(w_mid_loaded, 16)
            sp.dma_start(m.w_uq, w_uq.rearrange("l (k p) h c -> p (l k) (h c)", p=P)).then_inc(w_mid_loaded, 16)
            sp.dma_start(m.w_ukv, w_ukv.rearrange("l p h c -> (l p) h c")).then_inc(w_mid_loaded, 16)

        @block.gpsimd
        def _(pool):
            g = nc.gpsimd
            step = Chain(m, pool, m.pool_step)
            pool.dma_start(m.g_x, columns(attn_pre_g, KD)).then_inc(gain_loaded, 16)
            pool.dma_start(m.posi[:, :], positions.rearrange("b (t p) -> p (b t)", p=P)).then_inc(small_loaded, 16)
            pool.dma_start(m.g_q, columns(q_norm_g, QC)).then_inc(small_loaded, 16)
            pool.dma_start(m.g_kv, columns(kv_norm_g, 1)).then_inc(small_loaded, 16)
            pool.dma_start(m.g_mix[:, 0:4], columns(mla_out_g, 4)).then_inc(small_loaded, 16)
            pool.dma_start(m.g_mix[:, 4:8], columns(sg_out_g, 4)).then_inc(small_loaded, 16)
            pool.dma_start(m.b_sp[:, :], b_spatial.rearrange("l h t -> t (l h)")).then_inc(small_loaded, 16)
            pool.dma_start(m.b_r[:, :], on_all(b_router)).then_inc(small_loaded, 16)
            step(g.memset(m.eps[:, :], EPS))
            step(g.memset(m.ident[:, :], 0.0))
            step(g.affine_select(out=m.ident[:, :], in_=m.ident[:, :], compare_op=ALU.not_equal, fill=1.0, base=0,
                                 pattern=[[-1, P]], channel_multiplier=1), consts_ready)
            inv = (np.float32(1.0) / np.power(np.float32(THETA), np.arange(0, ROPE, 2, dtype=np.float32)
                                              / np.float32(ROPE))).astype(np.float32)
            for i in range(HR):
                step(g.memset(m.invf[:, i:i + 1], float(inv[i])), consts_ready)
            step(g.memset(m.causal[:, :], 0.0))
            step(g.affine_select(out=m.causal[:, :], in_=m.causal[:, :], compare_op=ALU.is_ge, fill=NEG, base=0,
                                 pattern=[[-1, P]], channel_multiplier=1))
            step(g.memset(m.ones[:, :], 1.0))
            step(g.affine_select(out=m.before[:, :], in_=m.ones[:, :], compare_op=ALU.is_gt, fill=0.0, base=0,
                                 pattern=[[1, P]], channel_multiplier=-1))
            step(g.iota(m.choice_ids[:, :, :, 0], pattern=[[P, T], [0, TOPK]], base=0, channel_multiplier=1))
            step(g.iota(m.choice_ids[:, :, :, 1], pattern=[[P * TOPK, T], [1, TOPK]], base=0,
                        channel_multiplier=TOPK))
            step(g.memset(m.idx_next[:, :, :], EMPTY))
            pool.wait_ge(small_loaded, 7 * 16)
            pool.wait_ge(w_mid_loaded, 3 * 16)
            for k in range(QC):
                step(g.tensor_scalar(m.w_uq[:, k, :], m.w_uq[:, k, :], m.g_q[:, k:k + 1], None, ALU.mult))
            step(g.tensor_scalar(m.w_ukv, m.w_ukv, m.g_kv, None, ALU.mult))

        @block.scalar
        def _(act):
            s = nc.scalar
            step = Chain(m, act, m.act_step)

            def prepare_x(t):
                act.wait_ge(x_loaded[t], 16)
                step(s.activation(m.junk[:, :], m.x_sb[:, t, :], ACT.Square, accum_out=ms[:, t:t + 1]))
                step(s.activation(ms[:, t:t + 1], ms[:, t:t + 1], ACT.Sqrt, scale=1.0 / D, bias=eps), root_x)
                act.wait_ge(xT_psum, t + 1)
                step(s.activation(m.xT[:, 0:4, t * P:(t + 1) * P], m.bank(6).rearrange(
                    "p (k s) -> p k s", k=4), ACT.Copy), xT_act)

            act.wait_ge(consts_ready, 1)
            prepare_x(0)
            act.wait_ge(gain_loaded, 16)
            for k in range(1, KD, 2):
                act.wait_ge(w_in_loaded[k // 2], 16)
                step(s.activation(m.w_in[:, k, :], m.w_in[:, k, :], ACT.Copy, scale=m.g_x[:, k:k + 1]), w_in_act)
            act.wait_ge(angles, 1)
            step(s.activation(m.sinb[:, :, :], m.rtmp[0][:, :, :], ACT.Sin))
            step(s.activation(m.cosb[:, :, :], m.rtmp[0][:, :, :], ACT.Sin, scale=0.5), sines)
            act.wait_ge(biasT_psum, 2)
            for t in range(T):
                if t + 1 < T:
                    prepare_x(t + 1)
                act.wait_ge(rstd_x, t + 1)
                act.wait_ge(z_psum, t + 1)
                b = 3 * (t % 2)
                step(s.activation(m.v_sg[:, t, :], m.bank(b + 2), ACT.Gelu_apprx_tanh, scale=ms[:, t:t + 1]), z_gated)
                step(s.activation(m.u_sg[:, t, :], m.bank(b + 1), ACT.Gelu_apprx_tanh, scale=ms[:, t:t + 1]), z_gated)
                if t >= 1:
                    act.wait_ge(v_squared, t)
                step(s.activation(v_squares, m.v_sg[:, t, :], ACT.Square), v_gelu_squares)
                act.wait_ge(latent_squares, t + 1)
                step(s.activation(lat[:, t, 0:1], lat[:, t, 0:1], ACT.Sqrt, scale=1.0 / QL, bias=eps))
                step(s.activation(lat[:, t, 1:2], lat[:, t, 1:2], ACT.Sqrt, scale=1.0 / KVL, bias=eps), root_latent)
                act.wait_ge(v_squared, t + 1)
                step(s.activation(sgs[:, t, :], sgs[:, t, :], ACT.Sqrt, scale=1.0 / HC, bias=eps), v_root)

        @block.vector
        def _(dve):
            v = nc.vector
            step = Chain(m, dve, m.dve_step)

            def prepare_x(t):
                dve.wait_ge(root_x, t + 1)
                step(v.reciprocal(ms[:, t:t + 1], ms[:, t:t + 1]), rstd_x)
                dve.wait_ge(xT_psum, t + 1)
                step(v.tensor_copy(m.xT[:, 4:8, t * P:(t + 1) * P], m.bank(7).rearrange(
                    "p (k s) -> p k s", k=4)), xT_dve)

            prepare_x(0)
            for i in range(2):
                dve.wait_ge(biasT_psum, i + 1)
                n = min(16, n_bias - 16 * i)
                step(v.tensor_copy(m.bias_cols[:, 16 * i:16 * i + n, :], m.bank(6 + i)[:, 0:n * E].rearrange(
                    "p (c e) -> p c e", e=E)), biasT_copied)
            dve.wait_ge(gain_loaded, 16)
            for k in range(0, KD, 2):
                dve.wait_ge(w_in_loaded[k // 2], 16)
                step(v.tensor_scalar(m.w_in[:, k, :], m.w_in[:, k, :], m.g_x[:, k:k + 1], None, ALU.mult), w_in_dve)
            dve.wait_ge(small_loaded, 7 * 16)
            dve.wait_ge(consts_ready, 1 + HR)
            step(v.tensor_copy(m.posf[:, :], m.posi[:, :]))
            r0, r1 = m.rtmp[0][:, :, :], m.rtmp[1][:, :, :]
            wide = [P, T, HR]
            step(v.tensor_tensor(r0, m.posf[:, :].unsqueeze(2).broadcast_to(wide),
                                 m.invf[:, :].unsqueeze(1).broadcast_to(wide), ALU.mult))
            step(v.tensor_scalar(r1, r0, float(1.0 / TWO_PI), ROUND, ALU.mult, ALU.add))
            step(v.tensor_scalar(r1, r1, ROUND, None, ALU.subtract))
            step(v.scalar_tensor_tensor(r0, r1, -PI_A, r0, ALU.mult, ALU.add))
            step(v.scalar_tensor_tensor(r0, r1, -PI_B, r0, ALU.mult, ALU.add))
            step(v.tensor_scalar(r0, r0, R_MAX, -R_MAX, ALU.min, ALU.max), angles)
            dve.wait_ge(sines, 1)
            step(v.tensor_tensor(m.cosb[:, :, :], m.cosb[:, :, :], m.cosb[:, :, :], ALU.mult))
            step(v.tensor_scalar(m.cosb[:, :, :], m.cosb[:, :, :], -2.0, 1.0, ALU.mult, ALU.add))
            dve.wait_ge(w_mid_loaded, 3 * 16)

            def latentT_copy(t):
                dve.wait_ge(latentT_psum, t + 1)
                tok = slice(t * P, (t + 1) * P)
                b = m.bank(6)
                step(v.tensor_copy(m.cqT[:, :, tok], b[:, 0:QL].rearrange("p (k s) -> p k s", k=QC)))
                step(v.tensor_copy(m.ckvT[:, tok], b[:, QL:QL + P]))
                step(v.tensor_copy(m.krT[NOPE:QK, tok], b[NOPE:QK, QL + P:QL + 2 * P]), latentT_copied)

            for t in range(T):
                if t + 1 < T:
                    prepare_x(t + 1)
                dve.wait_ge(z_psum, t + 1)
                step(v.tensor_scalar(m.za[:, t, :], m.bank(3 * (t % 2))[:, 0:A_COLS], ms[:, t:t + 1], None, ALU.mult),
                     z_latent)
                for a, b, c in ((0, QL, 0), (QL, QL + KVL, 1)):
                    step(v.tensor_tensor_reduce(out=m.small_row[:, 0:b - a], in0=m.za[:, t, a:b], in1=m.za[:, t, a:b],
                                                scale=1.0, scalar=0.0, op0=ALU.mult, op1=ALU.add,
                                                accum_out=lat[:, t, c:c + 1]), latent_squares if c else None)
                rope(v, step, m.za[:, t, QL + KVL:QL + KVL + HR], m.za[:, t, QL + KVL + HR:A_COLS], m.cosb[:, t, :],
                     m.sinb[:, t, :], [r[:, t, :] for r in m.rtmp])
                dve.wait_ge(v_gelu_squares, t + 1)
                step(v.tensor_reduce(out=sgs[:, t, :], in_=v_squares.rearrange("p (h c) -> p h c", h=H), op=ALU.add,
                                     axis=AX.X), v_squared)
                dve.wait_ge(root_latent, t + 1)
                step(v.reciprocal(lat[:, t, :], lat[:, t, :]))
                step(v.tensor_scalar(m.za[:, t, 0:QL], m.za[:, t, 0:QL], lat[:, t, 0:1], None, ALU.mult))
                step(v.tensor_scalar(m.za[:, t, QL:QL + KVL], m.za[:, t, QL:QL + KVL], lat[:, t, 1:2], None,
                                     ALU.mult), latent_ready)
                dve.wait_ge(v_root, t + 1)
                step(v.reciprocal(sgs[:, t, :], sgs[:, t, :]))
                grouped = m.v_sg[:, t, :].rearrange("p (h c) -> p h c", h=H)
                step(v.tensor_tensor(grouped, grouped, sgs[:, t, :].unsqueeze(2).broadcast_to([P, H, HC]), ALU.mult))
                step(v.tensor_tensor(m.v_sg[:, t, :], m.v_sg[:, t, :], m.sg_g, ALU.mult))
                if t >= 1:
                    latentT_copy(t - 1)
            latentT_copy(T - 1)

        @block.tensor
        def _(pe):
            mm, tr = nc.tensor.matmul, nc.tensor.transpose
            pe.wait_ge(consts_ready, 1)

            def transpose_biases(i):
                pe.wait_ge(biases_loaded, 32)
                for c in range(16 * i, min(16 * i + 16, n_bias)):
                    last = tr(m.bank(6 + i)[:, (c - 16 * i) * E:(c - 16 * i + 1) * E],
                              m.work[0:E, 8192 + c * P:8192 + (c + 1) * P], m.ident[0:E, 0:E])
                last.then_inc(biasT_psum, 1)

            def transpose_x(t):
                pe.wait_ge(x_loaded[t], 16)
                if t == 1:
                    pe.wait_ge(biasT_copied, 2)
                if t >= 3:
                    pe.wait_ge(latentT_copied, t - 2)
                for k in range(KD):
                    last = tr(m.bank(6 + k // 4)[:, (k % 4) * P:(k % 4 + 1) * P],
                              m.x_sb[:, t, k * P:(k + 1) * P], m.ident[:, :])
                last.then_inc(xT_psum, 1)

            transpose_x(0)
            pe.wait_ge(xT_act, 1)
            pe.wait_ge(xT_dve, 1)
            for i in range(2):
                transpose_biases(i)

            def transpose_latents(t):
                pe.wait_ge(latent_ready, t + 1)
                pe.wait_ge(xT_act, min(t + 3, T))
                if t >= 1:
                    pe.wait_ge(latentT_copied, t)
                b = m.bank(6)
                for i in range(3):
                    tr(b[:, i * P:(i + 1) * P], m.za[:, t, i * P:(i + 1) * P], m.ident[:, :])
                tr(b[0:QK, 3 * P:4 * P], m.za[:, t, A_COLS - QK:A_COLS], m.ident[:, :]).then_inc(latentT_psum, 1)

            for t in range(T):
                if t >= 2:
                    pe.wait_ge(z_latent, t - 1)
                    pe.wait_ge(z_gated, 2 * (t - 1))
                pe.wait_ge(xT_act, t + 1)
                pe.wait_ge(xT_dve, t + 1)
                for k in range(KD):
                    if t == 0:
                        pe.wait_ge(w_in_act if k % 2 else w_in_dve, k // 2 + 1)
                    if k == KD // 2 and t + 1 < T:
                        transpose_x(t + 1)
                    if t >= 1 and k == KD - 1:
                        transpose_latents(t - 1)
                    for j, (a, b) in enumerate(((0, A_COLS), (A_COLS, A_COLS + SGW), (A_COLS + SGW, IN_COLS))):
                        last = mm(m.bank(3 * (t % 2) + j)[:, 0:b - a], m.xT[:, k, t * P:(t + 1) * P],
                                  m.w_in[:, k, a:b], start=(k == 0), stop=(k == KD - 1))
                last.then_inc(z_psum, 1)
            transpose_latents(T - 1)


def attention_operands(nc, m, w_spatial):
    with ExitStack() as ctx:
        sem = m.sem

        w_sp_loaded = sem("w_sp_loaded")
        w_spT_psum = sem("w_spT_psum")
        w_spT_copied = sem("w_spT_copied")
        w_spT_masked = sem("w_spT_masked")
        q_psum = sem("q_psum")
        q_copied = sem("q_copied")
        q_roped = sem("q_roped")
        qT_psum = sem("qT_psum")
        qT_act = sem("qT_act")
        qT_dve = sem("qT_dve")
        kv_psum = sem("kv_psum")
        kv_act = sem("kv_act")
        kv_dve = sem("kv_dve")
        sg_psum = sem("sg_psum")
        sg_gated = sem("sg_gated")
        block = ctx.enter_context(nc.Block())
        q_row = m.ring[:, 20480:20480 + 2 * H * QK].rearrange("p (b h c) -> p b h c", b=2, h=H)
        half = H // 2
        kv_jobs = [("k", h, s) for h in range(H) for s in range(2)] + [("v", t, 0) for t in range(T)]

        @block.sync
        def _(sp):
            sp.dma_start(m.w_sp, w_spatial.rearrange("l h t s -> t (l h) s")).then_inc(w_sp_loaded, 16)

        @block.gpsimd
        def _(pool):
            g = nc.gpsimd
            step = Chain(m, pool, m.pool_step)
            for h in range(H):
                step(g.tensor_copy(m.kT[NOPE:QK, h, :], m.krT[NOPE:QK, :]))
            for i in range(2):
                pool.wait_ge(w_spT_copied, i + 1)
                part = m.w_spT[:, 4 * i:4 * i + 4, :]
                step(g.affine_select(out=part, in_=part, compare_op=ALU.is_ge, fill=0.0, base=0,
                                     pattern=[[0, 4], [1, P]], channel_multiplier=-1), w_spT_masked)

        @block.scalar
        def _(act):
            s = nc.scalar
            step = Chain(m, act, m.act_step)
            for i in range(2):
                act.wait_ge(w_spT_psum, i + 1)
                step(s.activation(m.w_spT[:, 4 * i:4 * i + 4, :], m.bank(6 + i).rearrange("p (h s) -> p h s", h=4),
                                  ACT.Copy), w_spT_copied)
            for t in range(T + 1):
                if t < T:
                    act.wait_ge(q_psum, t + 1)
                    if t >= 2:
                        act.wait_ge(qT_psum, t - 1)
                    for i in range(2):
                        step(s.activation(q_row[:, t % 2, half * i:half * i + half, :],
                                          m.bank(2 * (t % 2) + i)[:, 0:half * QK].rearrange(
                                              "p (h c) -> p h c", h=half), ACT.Copy), q_copied)
                if t >= 1:
                    act.wait_ge(qT_psum, t)
                    step(s.activation(m.qT[:, 0:half, (t - 1) * P:t * P], m.bank(4, QK).rearrange(
                        "p (h s) -> p h s", h=half), ACT.Copy), qT_act)
            for n, (kind, i, j) in enumerate(kv_jobs):
                if n % 2 == 0:
                    act.wait_ge(kv_psum, n + 1)
                    if kind == "k":
                        step(s.activation(m.kT[0:NOPE, i, j * 512:(j + 1) * 512], m.bank(6, NOPE), ACT.Copy), kv_act)
                    else:
                        step(s.activation(m.v_sb[:, i, :], m.bank(6), ACT.Copy), kv_act)

        @block.vector
        def _(dve):
            v = nc.vector
            step = Chain(m, dve, m.dve_step)
            for t in range(T + 1):
                if t < T:
                    dve.wait_ge(q_copied, 2 * (t + 1))
                    q = q_row[:, t % 2, :, :]
                    turn = [P, H, HR]
                    rope(v, step, q[:, :, NOPE:NOPE + HR], q[:, :, NOPE + HR:QK],
                         m.cosb[:, t, :].unsqueeze(1).broadcast_to(turn),
                         m.sinb[:, t, :].unsqueeze(1).broadcast_to(turn), [r[:, :, :] for r in m.rtmp], q_roped)
                if t >= 1:
                    dve.wait_ge(qT_psum, t)
                    step(v.tensor_copy(m.qT[:, half:H, (t - 1) * P:t * P], m.bank(5, QK).rearrange(
                        "p (h s) -> p h s", h=half)), qT_dve)
            for n, (kind, i, j) in enumerate(kv_jobs):
                if n % 2 == 1:
                    dve.wait_ge(kv_psum, n + 1)
                    if kind == "k":
                        step(v.tensor_copy(m.kT[0:NOPE, i, j * 512:(j + 1) * 512], m.bank(7, NOPE)), kv_dve)
                    else:
                        step(v.tensor_copy(m.v_sb[:, i, :], m.bank(7)), kv_dve)
            for h in range(H):
                dve.wait_ge(sg_psum, h + 1)
                u = m.u_sg[:, :, h * HC:(h + 1) * HC]
                step(v.scalar_tensor_tensor(u, m.bank(h % 4).rearrange("p (t c) -> p t c", t=T), m.b_sp[:, h:h + 1],
                                            u, ALU.add, ALU.mult), sg_gated)

        @block.tensor
        def _(pe):
            mm, tr = nc.tensor.matmul, nc.tensor.transpose
            pe.wait_ge(w_sp_loaded, 16)
            for i in range(2):
                for h in range(4):
                    last = tr(m.bank(6 + i)[:, h * P:(h + 1) * P], m.w_sp[:, 4 * i + h, :], m.ident[:, :])
                last.then_inc(w_spT_psum, 1)
            for t in range(T + 1):
                if t < T:
                    if t >= 2:
                        pe.wait_ge(q_copied, 2 * (t - 1))
                    for i in range(2):
                        for k in range(QC):
                            last = mm(m.bank(2 * (t % 2) + i)[:, 0:half * QK], m.cqT[:, k, t * P:(t + 1) * P],
                                      m.w_uq[:, k, i * half * QK:(i + 1) * half * QK], start=(k == 0),
                                      stop=(k == QC - 1))
                    last.then_inc(q_psum, 1)
                if t >= 1:
                    pe.wait_ge(q_roped, t)
                    if t >= 2:
                        pe.wait_ge(qT_act, t - 1)
                        pe.wait_ge(qT_dve, t - 1)
                    for h in range(H):
                        last = tr(m.bank(4 + h // half, QK)[:, (h % half) * P:(h % half + 1) * P],
                                  q_row[:, (t - 1) % 2, h, :], m.ident[:, :])
                    last.then_inc(qT_psum, 1)
            pe.wait_ge(w_spT_copied, 2)
            for n, (kind, i, j) in enumerate(kv_jobs):
                if n >= 2:
                    pe.wait_ge(kv_act if n % 2 == 0 else kv_dve, n // 2)
                if kind == "k":
                    last = mm(m.bank(6 + n % 2, NOPE), m.w_ukv[:, i, 0:NOPE], m.ckvT[:, j * 512:(j + 1) * 512],
                              start=True, stop=True)
                else:
                    last = mm(m.bank(6 + n % 2), m.ckvT[:, i * P:(i + 1) * P], m.w_ukv[:, :, NOPE:NOPE + VH],
                              start=True, stop=True)
                last.then_inc(kv_psum, 1)
            pe.wait_ge(w_spT_masked, 2)
            for h in range(H):
                if h >= 4:
                    pe.wait_ge(sg_gated, h - 3)
                mm(m.bank(h % 4), m.w_spT[:, h, :], m.v_sg[:, :, h * HC:(h + 1) * HC], start=True,
                   stop=True).then_inc(sg_psum, 1)


def attention(nc, m, w_out, w_out_loaded, w_out_scaled):
    with ExitStack() as ctx:
        sem = m.sem

        empty_ready = sem("empty_ready")
        cleared = sem("cleared")
        scores_psum = sem("scores_psum")
        max_ready = sem("max_ready")
        probs_ready = sem("probs_ready")
        pT_psum = sem("pT_psum")
        pT_act = sem("pT_act")
        pT_dve = sem("pT_dve")
        o_psum = sem("o_psum")
        o_ready = sem("o_ready")
        block = ctx.enter_context(nc.Block())
        jobs = [(h, i) for h in range(H) for i in TILE_ORDER]
        N = len(jobs)
        empty = m.junk[:, 0:E * REGION * 2 // P].bitcast(I32)
        squares = m.scr[:, 2560:3072]
        nmax, rsum, rinv = m.stat[:, 96:100], m.stat[:, 100:104], m.stat[:, 104:108]

        def wide(n):
            return sum(i >= 4 for _, i in jobs[:n])

        @block.sync
        def _(sp):
            wo = w_out.rearrange("l (k p) n -> p (l k) n", p=P)
            for k in range(0, KD, 4):
                sp.dma_start(m.w_out[:, k:k + 4, :], wo[:, k:k + 4, :]).then_inc(w_out_loaded, 16)
            sp.wait_ge(empty_ready, 1)
            sp.dma_start(m.choice_list.rearrange("(p c) o -> p (c o)", p=P), empty).then_inc(cleared, 16)
            sp.wait_ge(cleared, 16)

        @block.gpsimd
        def _(pool):
            g = nc.gpsimd
            step = Chain(m, pool, m.pool_step)
            step(g.memset(empty, EMPTY), empty_ready)
            pool.wait_ge(w_out_loaded, 32)
            for k in range(KD):
                step(g.tensor_scalar(m.w_out[:, k, :], m.w_out[:, k, :], m.g_mix[:, k:k + 1], None, ALU.mult),
                     w_out_scaled)

        @block.scalar
        def _(act):
            s = nc.scalar
            step = Chain(m, act, m.act_step)

            def mix_square(row, c):
                step(s.activation(squares, row, ACT.Square, accum_out=m.mix_s[:, c:c + 1]), m.mix_squares)

            for n in range(N + 1):
                if n < N:
                    w = (jobs[n][1] + 1) * P
                    act.wait_ge(max_ready, n + 1)
                    if n >= 2:
                        act.wait_ge(pT_psum, n - 1)
                    if n >= 4:
                        act.wait_ge(o_ready, n - 3)
                    step(s.activation(m.probs[:, n % 2, 0:w], m.ps[:, 2 * (n % 2):2 * (n % 2) + 2, :].rearrange(
                        "p b c -> p (b c)")[:, 0:w], ACT.Exp, bias=nmax[:, n % 4:n % 4 + 1], scale=SCALE,
                        accum_out=rsum[:, n % 4:n % 4 + 1]), probs_ready)
                if n >= 1:
                    l = n - 1
                    w = min(4, jobs[l][1] + 1) * P
                    act.wait_ge(pT_psum, l + 1)
                    if l >= 2:
                        act.wait_ge(o_psum, l - 1)
                    step(s.activation(m.probsT[:, l % 2, 0:w], m.bank(4)[:, 0:w], ACT.Copy), pT_act)
                if n % T == T // 2:
                    mix_square(m.u_sg[:, n // T, :], T + n // T)
                if n - 2 >= N - T:
                    act.wait_ge(o_ready, n - 1)
                    mix_square(m.o_sb[:, jobs[n - 2][1], :], jobs[n - 2][1])
            act.wait_ge(o_ready, N)
            mix_square(m.o_sb[:, jobs[N - 1][1], :], jobs[N - 1][1])

        @block.vector
        def _(dve):
            v = nc.vector
            step = Chain(m, dve, m.dve_step)
            for n in range(N + 2):
                if n < N:
                    i = jobs[n][1]
                    w = (i + 1) * P
                    s = m.ps[:, 2 * (n % 2):2 * (n % 2) + 2, :].rearrange("p b c -> p (b c)")
                    dve.wait_ge(scores_psum, n + 1)
                    if n >= 4:
                        dve.wait_ge(probs_ready, n - 3)
                    step(v.tensor_tensor(s[:, w - P:w], s[:, w - P:w], m.causal[:, :], ALU.add))
                    step(v.reduce_max(nmax[:, n % 4:n % 4 + 1], s[:, 0:w], AX.X))
                    step(v.tensor_scalar(nmax[:, n % 4:n % 4 + 1], nmax[:, n % 4:n % 4 + 1], -SCALE, None, ALU.mult),
                         max_ready)
                l = n - 1
                if 0 <= l < N and jobs[l][1] >= 4:
                    w = (jobs[l][1] - 3) * P
                    dve.wait_ge(pT_psum, l + 1)
                    if l >= 2:
                        dve.wait_ge(o_psum, l - 1)
                    step(v.tensor_copy(m.probsT[:, l % 2, 512:512 + w], m.bank(5)[:, 0:w]), pT_dve)
                l = n - 2
                if l >= 0:
                    h, i = jobs[l]
                    dve.wait_ge(probs_ready, l + 1)
                    step(v.reciprocal(rinv[:, l % 4:l % 4 + 1], rsum[:, l % 4:l % 4 + 1]))
                    dve.wait_ge(o_psum, l + 1)
                    step(v.tensor_scalar(m.o_sb[:, i, h * VH:(h + 1) * VH], m.bank(6 + l % 2)[:, 0:VH],
                                         rinv[:, l % 4:l % 4 + 1], None, ALU.mult), o_ready)

        @block.tensor
        def _(pe):
            mm, tr = nc.tensor.matmul, nc.tensor.transpose
            for n in range(-1, N + 1):
                if n + 1 < N:
                    l = n + 1
                    h, i = jobs[l]
                    if l >= 2:
                        pe.wait_ge(probs_ready, l - 1)
                    for b in range(i // 4 + 1):
                        w = min(512, (i + 1) * P - 512 * b)
                        last = mm(m.bank(2 * (l % 2) + b)[:, 0:w], m.qT[:, h, i * P:(i + 1) * P],
                                  m.kT[:, h, 512 * b:512 * b + w], start=True, stop=True)
                    last.then_inc(scores_psum, 1)
                if 0 <= n < N:
                    i = jobs[n][1]
                    pe.wait_ge(probs_ready, n + 1)
                    if n >= 1:
                        pe.wait_ge(pT_act, n)
                    if wide(n):
                        pe.wait_ge(pT_dve, wide(n))
                    for j in range(i + 1):
                        last = tr(m.bank(4 + j // 4)[:, (j % 4) * P:(j % 4 + 1) * P],
                                  m.probs[:, n % 2, j * P:(j + 1) * P], m.ident[:, :])
                    last.then_inc(pT_psum, 1)
                if n >= 1:
                    l = n - 1
                    h, i = jobs[l]
                    pe.wait_ge(pT_act, l + 1)
                    if wide(l + 1):
                        pe.wait_ge(pT_dve, wide(l + 1))
                    if l >= 2:
                        pe.wait_ge(o_ready, l - 1)
                    for j in range(i + 1):
                        last = mm(m.bank(6 + l % 2)[:, 0:VH], m.probsT[:, l % 2, j * P:(j + 1) * P],
                                  m.v_sb[:, j, h * VH:(h + 1) * VH], start=(j == 0), stop=(j == i))
                    last.then_inc(o_psum, 1)


def output_and_router(nc, m, x, w_out_scaled, attn_post_g, ffn_pre_g, w_router):
    with ExitStack() as ctx:
        sem = m.sem

        gains_loaded = sem("gains_loaded")
        iotas_ready = sem("iotas_ready")
        mix_root = sem("mix_root")
        mix_normed = sem("mix_normed")
        mixT_psum = sem("mixT_psum")
        mixT_act = sem("mixT_act")
        mixT_dve = sem("mixT_dve")
        y_psum = sem("y_psum")
        y_root = sem("y_root")
        y_scaled = sem("y_scaled")
        x1_ready = sem("x1_ready")
        x1_root = sem("x1_root")
        h_ready = sem("h_ready")
        h_stored = [sem(f"h_stored{b}") for b in range(2)]
        hT_psum = sem("hT_psum")
        hT_act = sem("hT_act")
        hT_dve = sem("hT_dve")
        logits_psum = sem("logits_psum")
        logits_ready = sem("logits_ready")
        tops_ready = sem("tops_ready")
        exps_ready = sem("exps_ready")
        taken_ready = sem("taken_ready")
        ranks_psum = sem("ranks_psum")
        ranks_read = sem("ranks_read")
        slots_ready = sem("slots_ready")
        list_written = m.list_written
        counts_psum = sem("counts_psum")
        block = ctx.enter_context(nc.Block())
        mix_s = m.mix_s
        eps = m.eps[:, :]
        ys, xs = m.stat[:, 16:20], m.stat[:, 20:24]
        top8 = m.scr[:, 0:64].rearrange("p (t k) -> p t k", t=T)
        idx8 = m.scr[:, 64:128].bitcast(U32).rearrange("p (t k) -> p t k", t=T)
        idxf = m.scr[:, 128:160].rearrange("p (t k) -> p t k", t=T)
        shifted = m.scr[:, 160:192].rearrange("p (t k) -> p t k", t=T)
        gate_sum = m.scr[:, 192:200]
        slotf = m.scr[:, 200:232].rearrange("p (t k) -> p t k", t=T)
        expert_no = m.scr[:, 256:288]
        first_slot = m.scr[:, 288:320]
        picked = m.scr[:, 1024:2048].rearrange("p (t k e) -> p t k e", t=T, k=TOPK)
        cnt, more, ends = (m.scr[:, 320 + i * E:320 + (i + 1) * E] for i in range(3))
        number = m.scr[:, 448:448 + MORE + 1]
        tab = m.scr[0:1, 512:512 + 3 * TAB + 1]
        table3 = [m.scr[0:1, 2048 + i * 448:2048 + i * 448 + (MORE + 1) * E].rearrange("p (j e) -> p j e", e=E)
                  for i in range(2)]
        of_item = [m.scr[0:1, 704 + i * 16:704 + i * 16 + MORE + 1] for i in range(3)]

        def dispatch(dve, v, step, t):
            dve.wait_ge(ranks_psum, t + 1)
            step(v.tensor_tensor(m.place[:, t, :], m.bank(7)[:, E:2 * E], first_slot, ALU.add), ranks_read)
            step(v.tensor_tensor(picked[:, t, :, :], m.hot[:, t, :, :],
                                 m.place[:, t, :].unsqueeze(1).broadcast_to([P, TOPK, E]), ALU.mult))
            step(v.tensor_reduce(out=slotf[:, t, :], in_=picked[:, t, :, :], op=ALU.add, axis=AX.X))
            step(v.tensor_copy(m.slots[:, t, :], slotf[:, t, :]), slots_ready)

        @block.sync
        def _(sp):
            sp.dma_start(m.post_g, on_all(attn_post_g)).then_inc(gains_loaded, 16)
            sp.dma_start(m.ffn_g, on_all(ffn_pre_g)).then_inc(gains_loaded, 16)
            sp.dma_start(m.w_router, w_router.rearrange("l (k p) e -> p (l k) e", p=P)).then_inc(gains_loaded, 16)
            x_t = x.rearrange("b (t p) d -> p (b t) d", p=P)
            for t in range(T):
                sp.dma_start(m.x_sb[:, t, :], x_t[:, t, :]).then_inc(m.x_loaded[t], 16)
            h_t = m.h_rows.rearrange("(t p) d -> p t d", p=P)
            for t in range(T):
                sp.wait_ge(h_ready, t + 1)
                sp.dma_start(h_t[:, t, :], m.h_row[:, t % 2, :]).then_inc(h_stored[t % 2], 16)
            for b in range(2):
                sp.wait_ge(h_stored[b], 16 * (T // 2))

        @block.gpsimd
        def _(pool):
            g = nc.gpsimd
            step = Chain(m, pool, m.pool_step)
            exact = dict(allow_small_or_imprecise_dtypes=True)
            step(g.iota(expert_no, pattern=[[1, E]], base=0, channel_multiplier=0, **exact))
            step(g.iota(first_slot, pattern=[[REGION, E]], base=0, channel_multiplier=0, **exact))
            step(g.iota(number, pattern=[[1, MORE + 1]], base=0, channel_multiplier=0, **exact), iotas_ready)
            for t in range(T):
                pool.wait_ge(slots_ready, t + 1)
                for k in range(TOPK):
                    pool.indirect_dma_start(m.choice_list, bass.IndirectOffsetOnAxis(m.slots[:, t, k:k + 1], 0),
                                            m.choice_ids[:, t, k, :], None).then_inc(list_written, 16)

        @block.scalar
        def _(act):
            s = nc.scalar
            step = Chain(m, act, m.act_step)
            step(s.activation(mix_s, mix_s, ACT.Sqrt, scale=1.0 / SGW, bias=eps), mix_root)

            def mixT_half(t):
                act.wait_ge(mixT_psum, t + 1)
                step(s.activation(m.mixT[:, 0:4, t * P:(t + 1) * P], m.bank(0).rearrange("p (k s) -> p k s", k=4),
                                  ACT.Copy), mixT_act)

            mixT_half(0)
            mixT_half(1)
            for t in range(T):
                act.wait_ge(y_psum, t + 1)
                b = 2 + 2 * (t % 2)
                step(s.activation(m.junk[:, :], m.ps[:, b:b + 2, :].rearrange("p b c -> p (b c)"), ACT.Square,
                                  accum_out=ys[:, 0:1]))
                step(s.activation(ys[:, 1:2], ys[:, 0:1], ACT.Sqrt, scale=1.0 / D, bias=eps), y_root)
                act.wait_ge(x1_ready, t + 1)
                step(s.activation(m.junk[:, :], m.x_sb[:, t, :], ACT.Square, accum_out=xs[:, 0:1]))
                step(s.activation(xs[:, 1:2], xs[:, 0:1], ACT.Sqrt, scale=1.0 / D, bias=eps), x1_root)
                if t + 2 < T:
                    mixT_half(t + 2)
                act.wait_ge(hT_psum, t + 1)
                if t >= 1:
                    act.wait_ge(logits_psum, t)
                step(s.activation(m.hT[:, 0:4, :], m.bank(6).rearrange("p (k s) -> p k s", k=4), ACT.Copy), hT_act)
            act.wait_ge(tops_ready, 1)
            step(s.activation(shifted, shifted, ACT.Exp), exps_ready)

        @block.vector
        def _(dve):
            v = nc.vector
            step = Chain(m, dve, m.dve_step)
            dve.wait_ge(mix_root, 1)
            step(v.reciprocal(mix_s, mix_s))

            def mix_norm(t):
                step(v.tensor_scalar(m.o_sb[:, t, :], m.o_sb[:, t, :], mix_s[:, t:t + 1], None, ALU.mult))
                step(v.tensor_scalar(m.u_sg[:, t, :], m.u_sg[:, t, :], mix_s[:, T + t:T + t + 1], None, ALU.mult),
                     mix_normed)

            def mixT_half(t):
                dve.wait_ge(mixT_psum, t + 1)
                step(v.tensor_copy(m.mixT[:, 4:8, t * P:(t + 1) * P], m.bank(1).rearrange("p (k s) -> p k s", k=4)),
                     mixT_dve)

            mix_norm(0)
            mix_norm(1)
            mixT_half(0)
            mixT_half(1)
            mix_norm(2)
            dve.wait_ge(gains_loaded, 48)
            dve.wait_ge(iotas_ready, 1)
            for t in range(T):
                b = 2 + 2 * (t % 2)
                dve.wait_ge(y_root, t + 1)
                step(v.reciprocal(ys[:, 2:3], ys[:, 1:2]))
                y = m.y_row[:, 0, :]
                step(v.scalar_tensor_tensor(y, m.ps[:, b:b + 2, :].rearrange("p b c -> p (b c)"), ys[:, 2:3],
                                            m.post_g, ALU.mult, ALU.mult), y_scaled)
                dve.wait_ge(m.x_loaded[t], 32)
                step(v.tensor_tensor(m.x_sb[:, t, :], m.x_sb[:, t, :], y, ALU.add), x1_ready)
                dve.wait_ge(x1_root, t + 1)
                step(v.reciprocal(xs[:, 2:3], xs[:, 1:2]))
                if t >= 2:
                    dve.wait_ge(h_stored[t % 2], 16 * (t // 2))
                step(v.scalar_tensor_tensor(m.h_row[:, t % 2, :], m.x_sb[:, t, :], xs[:, 2:3], m.ffn_g, ALU.mult,
                                            ALU.mult), h_ready)
                if t + 2 < T:
                    mixT_half(t + 2)
                if t + 3 < T:
                    mix_norm(t + 3)
                dve.wait_ge(hT_psum, t + 1)
                if t >= 1:
                    dve.wait_ge(logits_psum, t)
                step(v.tensor_copy(m.hT[:, 4:8, :], m.bank(7).rearrange("p (k s) -> p k s", k=4)), hT_dve)
                dve.wait_ge(logits_psum, t + 1)
                step(v.tensor_tensor(m.logits[:, t, :], m.bank(7)[:, 0:E], m.b_r[:, :], ALU.add), logits_ready)
                step(v.max(top8[:, t, :], m.logits[:, t, :]))
                step(v.max_index(idx8[:, t, :], top8[:, t, :], m.logits[:, t, :]))
                step(v.tensor_copy(idxf[:, t, :], idx8[:, t, 0:TOPK]))
                step(v.tensor_tensor(m.hot[:, t, :, :], expert_no.unsqueeze(1).broadcast_to([P, TOPK, E]),
                                     idxf[:, t, :].unsqueeze(2).broadcast_to([P, TOPK, E]), ALU.is_equal))
                step(v.tensor_reduce(out=m.taken[:, t, :], in_=m.hot[:, t, :, :].rearrange("p k e -> p e k"),
                                     op=ALU.add, axis=AX.X), taken_ready)
                if t >= 1:
                    dispatch(dve, v, step, t - 1)
            dispatch(dve, v, step, T - 1)
            step(v.tensor_tensor(shifted, top8[:, :, 0:TOPK], top8[:, :, 0:1].broadcast_to([P, T, TOPK]),
                                 ALU.subtract), tops_ready)
            dve.wait_ge(exps_ready, 1)
            step(v.tensor_reduce(out=gate_sum, in_=shifted, op=ALU.add, axis=AX.X))
            step(v.reciprocal(gate_sum, gate_sum))
            step(v.tensor_tensor(m.gates[:, :, :], shifted, gate_sum.unsqueeze(2).broadcast_to([P, T, TOPK]),
                                 ALU.mult))
            dve.wait_ge(counts_psum, 1)
            step(v.tensor_copy(cnt, m.bank(3)[:, 0:E]))
            step(v.tensor_scalar(more, cnt, float(CT), None, ALU.is_gt))
            for c in range(2, REGION // CT):
                step(v.scalar_tensor_tensor(more, cnt, float(c * CT), more, ALU.is_gt, ALU.add))
            step(v.tensor_tensor_scan(ends, m.ones[:, 0:E], more, 0.0, ALU.mult, ALU.add))
            over = [1, MORE + 1, E]
            passed, picks = table3
            chunk, left, valid = of_item
            experts, classes, firsts = (tab[:, i * TAB:(i + 1) * TAB] for i in range(3))
            step(v.tensor_tensor(passed, ends[0:1, :].unsqueeze(1).broadcast_to(over),
                                 number[0:1, :].unsqueeze(2).broadcast_to(over), ALU.is_le))
            step(v.tensor_copy(experts[:, 0:E], expert_no[0:1, :]))
            step(v.tensor_copy(firsts[:, 0:E], first_slot[0:1, :]))
            step(v.tensor_reduce(out=experts[:, E:TAB], in_=passed, op=ALU.add, axis=AX.X))
            step(v.tensor_scalar(experts[:, E:TAB], experts[:, E:TAB], float(E - 1), None, ALU.min))
            step(v.tensor_tensor(picks, passed, more[0:1, :].unsqueeze(1).broadcast_to(over), ALU.mult))
            step(v.tensor_reduce(out=chunk, in_=picks, op=ALU.add, axis=AX.X))
            step(v.tensor_tensor(chunk, number[0:1, :], chunk, ALU.subtract))
            step(v.tensor_scalar(chunk, chunk, -float(CT), -float(CT), ALU.mult, ALU.add))
            step(v.scalar_tensor_tensor(firsts[:, E:TAB], experts[:, E:TAB], float(REGION), chunk, ALU.mult,
                                        ALU.subtract))
            step(v.tensor_tensor(picks, expert_no[0:1, :].unsqueeze(1).broadcast_to(over),
                                 experts[:, E:TAB].unsqueeze(2).broadcast_to(over), ALU.is_equal))
            step(v.tensor_tensor(picks, picks, cnt[0:1, :].unsqueeze(1).broadcast_to(over), ALU.mult))
            step(v.tensor_reduce(out=left, in_=picks, op=ALU.add, axis=AX.X))
            step(v.tensor_tensor(left, left, chunk, ALU.add))
            for place, count in ((classes[:, 0:E], cnt[0:1, :]), (classes[:, E:TAB], left)):
                step(v.tensor_scalar(place, count, float(WIDTHS[0]), 1.0, ALU.is_gt, ALU.add))
                for w in WIDTHS[1:-1]:
                    step(v.scalar_tensor_tensor(place, count, float(w), place, ALU.is_gt, ALU.add))
            step(v.tensor_scalar(valid, number[0:1, :], ends[0:1, E - 1:E], None, ALU.is_lt))
            step(v.tensor_tensor(classes[:, E:TAB], classes[:, E:TAB], valid, ALU.mult))
            step(v.tensor_tensor(firsts[:, E:TAB], firsts[:, E:TAB], valid, ALU.mult))
            step(v.tensor_scalar(tab[:, 3 * TAB:3 * TAB + 1], ends[0:1, E - 1:E], float(E), None, ALU.add))
            step(v.tensor_copy(m.items[:, :], tab))

        @block.tensor
        def _(pe):
            mm, tr = nc.tensor.matmul, nc.tensor.transpose

            def transpose_mix(t):
                pe.wait_ge(mix_normed, t + 1)
                if t >= 1:
                    pe.wait_ge(mixT_act, t)
                    pe.wait_ge(mixT_dve, t)
                for k in range(KD):
                    src = m.o_sb if k < 4 else m.u_sg
                    last = tr(m.bank(k // 4)[:, (k % 4) * P:(k % 4 + 1) * P],
                              src[:, t, (k % 4) * P:(k % 4 + 1) * P], m.ident[:, :])
                last.then_inc(mixT_psum, 1)
            def transpose_h(t):
                pe.wait_ge(h_ready, t + 1)
                if t >= 1:
                    pe.wait_ge(hT_act, t)
                    pe.wait_ge(logits_ready, t)
                if t >= 2:
                    pe.wait_ge(ranks_read, t - 1)
                for k in range(KD):
                    last = tr(m.bank(6 + k // 4)[:, (k % 4) * P:(k % 4 + 1) * P],
                              m.h_row[:, t % 2, k * P:(k + 1) * P], m.ident[:, :])
                last.then_inc(hT_psum, 1)

            def logits(t):
                if t == 0:
                    pe.wait_ge(gains_loaded, 48)
                pe.wait_ge(hT_act, t + 1)
                pe.wait_ge(hT_dve, t + 1)
                if t >= 1:
                    ranks(t - 1)
                for k in range(KD):
                    last = mm(m.bank(7)[:, 0:E], m.hT[:, k, :], m.w_router[:, k, :], start=(k == 0),
                              stop=(k == KD - 1))
                last.then_inc(logits_psum, 1)

            def ranks(t):
                pe.wait_ge(taken_ready, t + 1)
                for j in range(t + 1):
                    last = mm(m.bank(7)[:, E:2 * E], m.ones[:, :] if j < t else m.before[:, :],
                              m.taken[:, j, :], start=(j == 0), stop=(j == t))
                last.then_inc(ranks_psum, 1)

            transpose_mix(0)
            pe.wait_ge(w_out_scaled, KD)
            for t in range(T):
                if t >= 2:
                    pe.wait_ge(y_scaled, t - 1)
                pe.wait_ge(mixT_act, t + 1)
                pe.wait_ge(mixT_dve, t + 1)
                for j in range(2):
                    for k in range(KD):
                        if j == 1 and k == 0 and t + 1 < T:
                            transpose_mix(t + 1)
                        if j == 1 and k == KD // 2 + 1 and t >= 1:
                            transpose_h(t - 1)
                        last = mm(m.bank(2 + 2 * (t % 2) + j), m.mixT[:, k, t * P:(t + 1) * P],
                                  m.w_out[:, k, j * 512:(j + 1) * 512], start=(k == 0), stop=(k == KD - 1))
                last.then_inc(y_psum, 1)
                if t >= 1:
                    logits(t - 1)
            transpose_h(T - 1)
            logits(T - 1)
            pe.wait_ge(ranks_read, T - 1)
            ranks(T - 1)
            for j in range(T):
                last = mm(m.bank(3)[:, 0:E], m.ones[:, :], m.taken[:, j, :], start=(j == 0), stop=(j == T - 1))
            last.then_inc(counts_psum, 1)


def by_width(eng, cls, widths=WIDTHS, w=1):
    if len(widths) == 1:
        yield widths[0]
    else:
        with eng.If(cls == w):
            yield widths[0]
        with eng.Else():
            yield from by_width(eng, cls, widths[1:], w + 1)


def experts(nc, m, late, w_gate_up, w_down, p, w_ple_gate, w_ple_proj):
    with ExitStack() as ctx:
        sem = m.sem

        def sb(name, shape, dt=F32):
            return ctx.enter_context(nc.sbuf_tensor(name, shape, dt))

        unit_loaded = [sem(f"unit_loaded{r}") for r in range(RAW)]
        cleared = sem("rows_cleared")
        index_loaded = sem("index_loaded")
        index_taken = sem("index_taken")
        rows_gathered = sem("rows_gathered")
        rowsT_psum = sem("rowsT_psum")
        rowsT_ready = sem("rowsT_ready")
        bias_ready = sem("bias_ready")
        gate_psum = sem("gate_psum_moe")
        up_psum = sem("up_psum")
        gate_read = sem("gate_read")
        up_read = sem("up_read")
        up_clamped = sem("up_clamped")
        sigmoid_ready = sem("sigmoid_ready")
        silu_ready = sem("silu_ready")
        act_ready = sem("act_ready")
        down_psum = sem("down_psum")
        down_read = sem("down_read")
        yT_psum = sem("yT_psum")
        y_read = sem("y_read")
        y_stored = sem("y_stored")
        y_free = sem("y_free")

        raw = [sb(f"raw{r}", [P, KD, 256]) for r in range(RAW)]
        rows = sb("rows", [P, CH, D])
        rowsT = sb("rowsT", [P, KD, CT])
        gate = sb("gate", [P, 2, CT])
        up = sb("up", [P, 2, CT])
        sig = sb("sig", [P, 2, CT])
        act_f = sb("act_f", [P, KF, CT])
        yT = sb("yT", [P, 3, CT])
        y_out = sb("y_out", [P, CH, D])
        block = ctx.enter_context(nc.Block())

        def class_of(eng, i):
            return eng.value_load(m.items[0:1, bass.ds(i + TAB, 1)], min_val=0, max_val=len(WIDTHS))

        def unit_used(eng, i, u):
            if u >= GU_UNITS:
                eng.wait_ge(down_psum, i * KD + 2 * (u - GU_UNITS) + 3)
            else:
                eng.wait_ge(gate_psum if u % 2 == 0 else up_psum, i * KF + u - u % 2 + 2)

        def items(eng, first=0):
            with eng.Fori(0, (MAX_ITEMS - first) // GROUP) as g:
                with eng.If(class_of(eng, g * GROUP + first) > 0):
                    with eng.Fori(0, GROUP) as j:
                        i = g * GROUP + (j + first)
                        cls = class_of(eng, i)
                        with eng.If(cls > 0):
                            yield i, cls
                    eng.sem_inc(m.mark, 1)

        @block.sync
        def _(sp):
            def load_unit(u, expert):
                if u < GU_UNITS:
                    src = w_gate_up.rearrange("l e (k p) n -> (l e) p k n", p=P)
                    c = (u // 2) * 256 + (u % 2) * F
                else:
                    src = w_down.rearrange("l e (k p) n -> (l e) p k n", p=P)
                    c = (u - GU_UNITS) * 256
                src = src[bass.ds(expert, 1), :, :, c:c + 256].rearrange("e p k n -> (e p) k n")
                sp.dma_start(raw[u % RAW][:, :, :], src).then_inc(unit_loaded[u % RAW], 16)

            sp.wait_ge(rows_gathered, 16 * CH)
            for u in range(RAW):
                load_unit(u, 0)

            def load_item(i):
                this = sp.value_load(m.items[0:1, bass.ds(i, 1)], min_val=0, max_val=E - 1)
                after = sp.value_load(m.items[0:1, bass.ds(i + 1, 1)], min_val=0, max_val=E - 1)
                for u in range(RAW, N_UNITS + RAW):
                    unit_used(sp, i, u - RAW)
                    load_unit(u % N_UNITS, this if u < N_UNITS else after)

            with sp.Fori(0, KD) as i:
                load_item(i)
                sp.dma_start(late.w_gate[:, bass.ds(i, 1), :], w_ple_gate.rearrange(
                    "l (k p) n -> p (l k) n", p=P)[:, bass.ds(i, 1), :]).then_inc(late.loaded, 16)
                sp.dma_start(late.p_sb[:, bass.ds(i, 1), :], p.rearrange(
                    "l b (t p) d -> p (l b t) d", p=P)[:, bass.ds(i, 1), :]).then_inc(late.loaded, 16)
            sp.dma_start(late.w_proj, w_ple_proj.rearrange("l (k p) n -> p (l k) n", p=P)).then_inc(late.loaded, 16)
            for i, _ in items(sp, KD):
                load_item(i)
            n_items = sp.value_load(m.items[0:1, 3 * TAB:3 * TAB + 1], min_val=E, max_val=MAX_ITEMS)
            for r in range(RAW):
                sp.wait_ge(unit_loaded[r], n_items * (16 * N_UNITS // RAW) + 16)
            sp.sem_inc(m.mark, 1)

        @block.gpsimd
        def _(pool):
            def load_index(item):
                whole = CT // P
                first = pool.value_load(m.items[0:1, bass.ds(item + 2 * TAB, 1)], min_val=0, max_val=E * REGION - CT)
                pool.dma_start(m.idx_next[:, 0:whole, :], m.choice_list[bass.ds(first, whole * P), :].rearrange(
                    "(c p) o -> p c o", p=P)).then_inc(index_loaded, 16)
                pool.dma_start(m.idx_next[0:CT - whole * P, whole, :],
                               m.choice_list[bass.ds(first + whole * P, CT - whole * P), :]
                               ).then_inc(index_loaded, 16)

            def gather():
                for c in range(CH):
                    pool.indirect_dma_start(rows[:, c, :], None, m.h_rows,
                                            bass.IndirectOffsetOnAxis(m.idx_next[:, c, 0:1], 0),
                                            bounds_check=SEQ - 1, oob_is_err=False).then_inc(rows_gathered, 16)

            pool.wait_ge(m.list_written, 16 * T * TOPK)
            load_index(0)
            pool.wait_ge(cleared, 1)
            pool.wait_ge(index_loaded, 32)
            gather()
            pool.sem_inc(y_free, 1)
            for i, _ in items(pool):
                pool.wait_ge(rows_gathered, i * (16 * CH) + 16 * CH)
                pool.sem_inc(m.mark, 1)
                nc.gpsimd.tensor_copy(m.idx_now[:, :, :], m.idx_next[:, :, :]).then_inc(index_taken, 1)
                pool.wait_ge(index_taken, i + 1)
                load_index(i + 1)
                pool.wait_ge(rowsT_psum, i * KD + KD)
                pool.wait_ge(index_loaded, i * 32 + 64)
                pool.sem_inc(m.mark, 1)
                gather()
                pool.wait_ge(y_read, i * 2 + 3)
                pool.sem_inc(m.mark, 1)
                for c in range(CH):
                    pool.indirect_dma_start(m.y_choices, bass.IndirectOffsetOnAxis(m.idx_now[:, c, 1:2], 0),
                                            y_out[:, c, :], None, bounds_check=SEQ * TOPK - 1,
                                            oob_is_err=False).then_inc(y_stored, 16)
                pool.wait_ge(y_stored, i * (16 * CH) + 16 * CH)
                pool.sem_inc(y_free, 1)

        @block.scalar
        def _(act):
            s = nc.scalar

            def rows_out(base, k):
                act.wait_ge(rowsT_psum, base + (k + 1))
                s.activation(rowsT[:, k, :], m.bank(2 + k % 2)[:, 0:CT], ACT.Copy).then_inc(rowsT_ready, 1)

            def y_part(i, part, n):
                act.wait_ge(yT_psum, i * KD + 4 * part + 4)
                if part == 0:
                    act.wait_ge(y_free, i + 1)
                for c in range(-(-n // P)):
                    r = min(P, n - c * P)
                    last = s.activation(y_out[0:r, c, part * 512:(part + 1) * 512],
                                        m.bank(Y_BANKS[c], r), ACT.Copy)
                last.then_inc(y_read, 1)

            act.sem_inc(y_read, 1)
            act.wait_ge(cleared, 2)
            for k in range(KD):
                rows_out(0, k)
            for i, cls in items(act):
                for n in by_width(act, cls):
                    for pair in range(KF // 2):
                        act.wait_ge(gate_read, i * KF + 2 * pair + 4)
                        if pair >= 1:
                            act.wait_ge(silu_ready, i * (KF // 2) + pair)
                        s.activation(sig[:, :, 0:n], gate[:, :, 0:n], ACT.Sigmoid,
                                     scale=ALPHA).then_inc(sigmoid_ready, 1)
                    for k in range(KD):
                        rows_out(i * KD + KD, k)
                        if k == 5:
                            y_part(i, 0, n)
                    y_part(i, 1, n)

        @block.vector
        def _(dve):
            v = nc.vector

            def down_out(i, d, n):
                dve.wait_ge(down_psum, i * KD + d + 2)
                v.tensor_scalar(yT[:, d % 3, 0:n], m.bank(6 + d % 2)[:, 0:n],
                                m.bias_now[:, 2 * KF + d:2 * KF + d + 1], None, ALU.add).then_inc(down_read, 1)

            v.memset(rows[:, :, :], 0.0).then_inc(cleared, 1)
            v.memset(y_out[:, :, :], 0.0).then_inc(cleared, 1)
            dve.sem_inc(gate_read, 2)
            dve.sem_inc(up_read, 2)
            dve.sem_inc(down_read, 2)
            half = KF // 2
            for i, cls in items(dve):
                for n in by_width(dve, cls):
                    expert = dve.value_load(m.items[0:1, bass.ds(i, 1)], min_val=0, max_val=E - 1)
                    dve.wait_ge(down_read, i * KD + 2)
                    v.tensor_copy(m.bias_now[:, :], m.bias_cols[:, :, bass.ds(expert, 1)].rearrange(
                        "p c e -> p (c e)")).then_inc(bias_ready, 1)
                    dve.wait_ge(bias_ready, i + 1)
                    for pair in range(half):
                        for c in range(2):
                            f = 2 * pair + c
                            dve.wait_ge(gate_psum, i * KF + f + 1)
                            v.tensor_scalar(gate[:, c, 0:n], m.bank(2 + c)[:, 0:n], m.bias_now[:, f:f + 1],
                                            LIMIT, ALU.add, ALU.min).then_inc(gate_read, 1)
                        for c in range(2):
                            f = 2 * pair + c
                            dve.wait_ge(up_psum, i * KF + f + 1)
                            v.tensor_scalar(up[:, c, 0:n], m.bank(4 + c)[:, 0:n],
                                            m.bias_now[:, KF + f:KF + f + 1], LIMIT, ALU.add,
                                            ALU.min).then_inc(up_read, 1)
                        dve.wait_ge(up_read, i * KF + 2 * pair + 4)
                        v.tensor_scalar(up[:, :, 0:n], up[:, :, 0:n], -LIMIT, 1.0, ALU.max,
                                        ALU.add).then_inc(up_clamped, 1)
                        dve.wait_ge(sigmoid_ready, i * half + pair + 1)
                        v.tensor_tensor(gate[:, :, 0:n], gate[:, :, 0:n], sig[:, :, 0:n],
                                        ALU.mult).then_inc(silu_ready, 1)
                        dve.wait_ge(up_clamped, i * half + pair + 1)
                        dve.wait_ge(silu_ready, i * half + pair + 1)
                        v.tensor_tensor(act_f[:, 2 * pair:2 * pair + 2, 0:n], gate[:, :, 0:n], up[:, :, 0:n],
                                        ALU.mult).then_inc(act_ready, 1)
                        dve.wait_ge(act_ready, i * half + pair + 1)
                    for d in range(KD):
                        down_out(i, d, n)

        @block.tensor
        def _(pe):
            tr = nc.tensor.transpose

            def product(bank, u, c, x, ks, n):
                for k in ks:
                    last = nc.tensor.matmul(bank[:, 0:n], raw[u % RAW][:, k, c * P:(c + 1) * P], x[:, k, 0:n],
                                            start=(k == 0), stop=(k == KD - 1))
                return last

            def unit_here(i, u):
                pe.wait_ge(unit_loaded[u % RAW], i * (16 * N_UNITS // RAW) + 16 * (u // RAW + 1))

            def transpose_rows(k):
                for c in range(CH):
                    r = min(P, CT - c * P)
                    last = tr(m.bank(2 + k % 2)[:, c * P:c * P + r], rows[0:r, c, k * P:(k + 1) * P],
                              m.ident[0:r, 0:r])
                last.then_inc(rowsT_psum, 1)

            def transpose_out(i, e, n):
                pe.wait_ge(down_read, i * KD + e + 3)
                if e % 4 == 0:
                    pe.wait_ge(y_read, i * 2 + e // 4 + 1)
                for c in range(-(-n // P)):
                    r = min(P, n - c * P)
                    last = tr(m.bank(Y_BANKS[c], r)[:, (e % 4) * P:(e % 4 + 1) * P], yT[:, e % 3, c * P:c * P + r],
                              m.ident[:, :])
                last.then_inc(yT_psum, 1)

            pe.sem_inc(down_psum, 1)
            pe.wait_ge(rows_gathered, 16 * CH)
            for k in range(KD):
                if k >= 2:
                    pe.wait_ge(rowsT_ready, k - 1)
                transpose_rows(k)
            class_reg = pe.alloc_register("width_class")
            pe.reg_load(class_reg, m.items[0:1, TAB:TAB + 1])
            with pe.Fori(0, MAX_ITEMS) as i:
                cls = pe.snap(class_reg)
                with pe.If(cls > 0):
                    for n in by_width(pe, cls):
                        pe.wait_ge(rowsT_ready, i * KD + KD)
                        for u in range(GU_UNITS):
                            unit_here(i, u)
                            if u == 1:
                                pe.wait_ge(y_read, i * 2 + 1)
                            read, done = (gate_read, gate_psum) if u % 2 == 0 else (up_read, up_psum)
                            for c in range(2):
                                pe.wait_ge(read, i * KF + u - u % 2 + c + 1)
                                product(m.bank(2 + 2 * (u % 2) + c), u, c, rowsT, range(KD),
                                        n).then_inc(done, 1)
                        unit_here(i, GU_UNITS)
                        for c in range(2):
                            pe.wait_ge(down_read, i * KD + c + 1)
                            for pair in range(KF // 2 - 1):
                                if c == 0:
                                    pe.wait_ge(act_ready, i * (KF // 2) + pair + 1)
                                product(m.bank(6 + c), GU_UNITS, c, act_f, (2 * pair, 2 * pair + 1), n)
                        pe.wait_ge(act_ready, i * (KF // 2) + KF // 2)
                        for c in range(2):
                            product(m.bank(6 + c), GU_UNITS, c, act_f, (KF - 2, KF - 1),
                                    n).then_inc(down_psum, 1)
                        pe.wait_ge(rows_gathered, i * (16 * CH) + 32 * CH)
                        pe.wait_ge(gate_read, i * KF + KF + 2)
                        for k in range(2):
                            transpose_rows(k)
                        for d in range(2, KD):
                            u = GU_UNITS + d // 2
                            if d % 2 == 0:
                                unit_here(i, u)
                            pe.wait_ge(down_read, i * KD + d + 1)
                            product(m.bank(6 + d % 2), u, d % 2, act_f, range(KF), n).then_inc(down_psum, 1)
                            transpose_out(i, d - 2, n)
                            if d == KD - 1:
                                pe.reg_load(class_reg, m.items[0:1, bass.ds(i + (TAB + 1), 1)])
                            pe.wait_ge(rowsT_ready, i * KD + KD + d - 1)
                            transpose_rows(d)
                        for e in (KD - 2, KD - 1):
                            transpose_out(i, e, n)


class LateWeights:

    def __init__(self, nc, ctx, m):
        both = ctx.enter_context(nc.sbuf_tensor("late_weights", [P, KD * D + KP * D + T * DP], F32))
        self.loaded = m.sem("late_loaded")
        self.w_gate = both[:, 0:KD * D].rearrange("p (k n) -> p k n", k=KD)
        self.w_proj = both[:, KD * D:(KD + KP) * D].rearrange("p (k n) -> p k n", k=KP)
        self.p_sb = both[:, (KD + KP) * D:].rearrange("p (t d) -> p t d", t=T)


def combine_and_embed(nc, m, late, ffn_post_g, b_ple_gate, ple_norm_g, out):
    with ExitStack() as ctx:
        sem = m.sem

        def sb(name, shape):
            return ctx.enter_context(nc.sbuf_tensor(name, shape, F32))

        gains_loaded = sem("late_gains_loaded")
        choices_loaded = [sem(f"choices_loaded{b}") for b in range(2)]
        first_ready = sem("first_ready")
        y_ready = sem("y_ready")
        y_root = sem("y_root6")
        x2_ready = sem("x2_ready")
        pT_psum = sem("pT_psum6")
        pT_ready = sem("pT_ready")
        proj_psum = sem("proj_psum")
        proj_ready = sem("proj_ready")
        inT_psum = sem("inT_psum")
        inT_act = sem("inT_act")
        inT_dve = sem("inT_dve")
        gate_psum = sem("gate_psum")
        gate_biased = sem("gate_biased")
        gate_done = sem("gate_done")
        gated = sem("gated")
        gated_root = sem("gated_root")
        embedding_ready = sem("embedding_ready")
        out_ready = sem("out_ready")
        out_stored = sem("out_stored")
        post_g, gate_b, norm_g = (sb(n, [P, D]) for n in ("post_g_row", "gate_b_row", "norm_g_row"))
        inT = sb("inT", [P, 2, KD, P])
        pT = sb("pT", [P, 2, KP, P])
        y_acc = sb("y_acc", [P, 2, D])
        gate_row = sb("gate_row", [P, D])
        choices = sb("choices", [P, 2, TOPK, D])
        prod = sb("prod", [P, T, D])
        block = ctx.enter_context(nc.Block())
        eps = m.eps[:, :]
        ys, gs = m.stat[:, 0:T], m.stat[:, T:2 * T]

        def pair(b):
            return m.ps[:, b:b + 2, :].rearrange("p b c -> p (b c)")

        @block.sync
        def _(sp):
            out_t = out.rearrange("b (t p) d -> p (b t) d", p=P)
            y_t = m.y_choices.rearrange("(t p k) d -> p t (k d)", p=P, k=TOPK)
            for t in range(T):
                if t >= 2:
                    sp.wait_ge(y_ready, t - 1)
                sp.dma_start(choices[:, t % 2, :, :].rearrange("p k d -> p (k d)"), y_t[:, t, :]
                             ).then_inc(choices_loaded[t % 2], 16)
                if t == 0:
                    sp.dma_start(post_g[:, :], on_all(ffn_post_g)).then_inc(gains_loaded, 16)
                    sp.dma_start(gate_b[:, :], on_all(b_ple_gate)).then_inc(gains_loaded, 16)
                    sp.dma_start(norm_g[:, :], on_all(ple_norm_g)).then_inc(gains_loaded, 16)
            for t in range(T):
                sp.wait_ge(out_ready, t + 1)
                sp.dma_start(out_t[:, t, :], m.x_sb[:, t, :]).then_inc(out_stored, 16)
            sp.wait_ge(out_stored, 16 * T)

        @block.gpsimd
        def _(pool):
            g = nc.gpsimd
            step = Chain(m, pool, m.pool_step)
            for t in range(T):
                pool.wait_ge(embedding_ready, t + 1)
                step(g.tensor_tensor(m.x_sb[:, t, :], m.x_sb[:, t, :], prod[:, t, :], ALU.add), out_ready)

        @block.scalar
        def _(act):
            s = nc.scalar
            step = Chain(m, act, m.act_step)

            def first_choice(t):
                act.wait_ge(choices_loaded[t % 2], 16 * (t // 2 + 1))
                if t >= 2:
                    act.wait_ge(x2_ready, t - 1)
                step(s.activation(y_acc[:, t % 2, :], choices[:, t % 2, 0, :], ACT.Copy,
                                  scale=m.gates[:, t, 0:1]), first_ready)

            def y_rms(t):
                act.wait_ge(y_ready, t + 1)
                step(s.activation(m.junk[:, :], y_acc[:, t % 2, :], ACT.Square, accum_out=ys[:, t:t + 1]))
                step(s.activation(ys[:, t:t + 1], ys[:, t:t + 1], ACT.Sqrt, scale=1.0 / D, bias=eps), y_root)

            def inT_half(t):
                act.wait_ge(inT_psum, t + 1)
                step(s.activation(inT[:, t % 2, 0:4, :], m.bank(4).rearrange("p (k s) -> p k s", k=4), ACT.Copy),
                     inT_act)

            def proj(t):
                act.wait_ge(pT_psum, t + 1)
                step(s.activation(pT[:, t % 2, :, :], m.bank(6 + t % 2)[:, 0:KP * P].rearrange(
                    "p (k s) -> p k s", k=KP), ACT.Copy), pT_ready)
                if t >= 1:
                    act.wait_ge(proj_psum, t)
                    step(s.activation(prod[:, t - 1, :], pair(2 * ((t - 1) % 2)), ACT.Copy), proj_ready)

            for t in range(T):
                proj(t)
                if t == 1:
                    first_choice(0)
                if t == 3:
                    y_rms(0)
                    first_choice(1)
                if t == 5:
                    y_rms(1)
                    first_choice(2)
            act.wait_ge(proj_psum, T)
            step(s.activation(prod[:, T - 1, :], pair(2 * ((T - 1) % 2)), ACT.Copy), proj_ready)
            inT_half(0)
            for t in range(T):
                if t + 2 < T:
                    y_rms(t + 2)
                if t + 3 < T:
                    first_choice(t + 3)
                if t + 1 < T:
                    inT_half(t + 1)
                act.wait_ge(gate_biased, t + 1)
                step(s.activation(gate_row[:, :], gate_row[:, :], ACT.Sigmoid), gate_done)
                act.wait_ge(gated, t + 1)
                step(s.activation(m.junk[:, :], prod[:, t, :], ACT.Square, accum_out=gs[:, t:t + 1]))
                step(s.activation(gs[:, t:t + 1], gs[:, t:t + 1], ACT.Sqrt, scale=1.0 / D, bias=eps), gated_root)

        @block.vector
        def _(dve):
            v = nc.vector
            step = Chain(m, dve, m.dve_step)

            def combine(t):
                y = y_acc[:, t % 2, :]
                dve.wait_ge(first_ready, t + 1)
                for k in range(1, TOPK):
                    step(v.scalar_tensor_tensor(y, choices[:, t % 2, k, :], m.gates[:, t, k:k + 1], y, ALU.mult,
                                                ALU.add), y_ready if k == TOPK - 1 else None)
                dve.wait_ge(y_root, t + 1)
                step(v.reciprocal(ys[:, t:t + 1], ys[:, t:t + 1]))
                step(v.scalar_tensor_tensor(y, y, ys[:, t:t + 1], post_g[:, :], ALU.mult, ALU.mult))
                step(v.tensor_tensor(m.x_sb[:, t, :], m.x_sb[:, t, :], y, ALU.add), x2_ready)

            def inT_half(t):
                dve.wait_ge(inT_psum, t + 1)
                step(v.tensor_copy(inT[:, t % 2, 4:8, :], m.bank(5).rearrange("p (k s) -> p k s", k=4)), inT_dve)

            def finish(t):
                g = gs[:, t:t + 1]
                dve.wait_ge(gated_root, t + 1)
                step(v.reciprocal(g, g))
                step(v.scalar_tensor_tensor(prod[:, t, :], prod[:, t, :], g, norm_g[:, :], ALU.mult, ALU.mult),
                     embedding_ready)

            dve.wait_ge(gains_loaded, 48)
            combine(0)
            combine(1)
            inT_half(0)
            for t in range(T + 1):
                if t + 2 < T:
                    combine(t + 2)
                if t + 1 < T:
                    inT_half(t + 1)
                if t >= 1:
                    finish(t - 1)
                if t < T:
                    dve.wait_ge(gate_psum, t + 1)
                    step(v.tensor_tensor(gate_row[:, :], pair(2 * (t % 2)), gate_b[:, :], ALU.add), gate_biased)
                    dve.wait_ge(gate_done, t + 1)
                    dve.wait_ge(proj_ready, t + 1)
                    step(v.tensor_tensor(prod[:, t, :], prod[:, t, :], gate_row[:, :], ALU.mult), gated)

        @block.tensor
        def _(pe):
            mm, tr = nc.tensor.matmul, nc.tensor.transpose

            def transpose_p(t):
                for k in range(KP):
                    last = tr(m.bank(6 + t % 2)[:, k * P:(k + 1) * P], late.p_sb[:, t, k * P:(k + 1) * P],
                              m.ident[:, :])
                last.then_inc(pT_psum, 1)

            def transpose_x(t):
                pe.wait_ge(x2_ready, t + 1)
                if t >= 1:
                    pe.wait_ge(inT_act, t)
                    pe.wait_ge(inT_dve, t)
                for k in range(KD):
                    last = tr(m.bank(4 + k // 4)[:, (k % 4) * P:(k % 4 + 1) * P], m.x_sb[:, t, k * P:(k + 1) * P],
                              m.ident[:, :])
                last.then_inc(inT_psum, 1)

            pe.wait_ge(late.loaded, 16 * (2 * KD + 1))
            transpose_p(0)
            for t in range(T):
                if t + 1 < T:
                    if t >= 1:
                        pe.wait_ge(pT_ready, t)
                    transpose_p(t + 1)
                pe.wait_ge(pT_ready, t + 1)
                if t >= 2:
                    pe.wait_ge(proj_ready, t - 1)
                for j in range(2):
                    for k in range(KP):
                        last = mm(m.bank(2 * (t % 2) + j), pT[:, t % 2, k, :], late.w_proj[:, k, j * 512:(j + 1) * 512],
                                  start=(k == 0), stop=(k == KP - 1))
                last.then_inc(proj_psum, 1)
            transpose_x(0)
            for t in range(T):
                if t < 2:
                    pe.wait_ge(proj_ready, T - 1 + t)
                else:
                    pe.wait_ge(gate_biased, t - 1)
                pe.wait_ge(inT_act, t + 1)
                pe.wait_ge(inT_dve, t + 1)
                for j in range(2):
                    for k in range(KD):
                        if j == 1 and k == KD - 3 and t + 1 < T:
                            transpose_x(t + 1)
                        last = mm(m.bank(2 * (t % 2) + j), inT[:, t % 2, k, :], late.w_gate[:, k, j * 512:(j + 1) * 512],
                                  start=(k == 0), stop=(k == KD - 1))
                last.then_inc(gate_psum, 1)


def decoder_layer(nc, x, p, positions, attn_pre_g, w_in, q_norm_g, w_uq, kv_norm_g, w_ukv, sg_norm_g, w_spatial,
                  b_spatial, mla_out_g, sg_out_g, w_out, attn_post_g, ffn_pre_g, w_router, b_router, w_gate_up,
                  b_gate_up, w_down, b_down, ffn_post_g, w_ple_gate, b_ple_gate, w_ple_proj, ple_norm_g, out):
    with ExitStack() as ctx:
        ctx.enter_context(nc.allow_non_contiguous_dma(reason="vectors of 1024 elements as columns"))
        m = Buffers(nc, ctx)
        with ExitStack() as early:
            m.open_early(nc, early)
            input_projection(nc, m, x, positions, attn_pre_g, w_in, q_norm_g, w_uq, kv_norm_g, w_ukv, sg_norm_g,
                             b_spatial, mla_out_g, sg_out_g, b_router, b_gate_up, b_down)
            attention_operands(nc, m, w_spatial)
            w_out_loaded, w_out_scaled = m.sem("w_out_loaded"), m.sem("w_out_scaled")
            attention(nc, m, w_out, w_out_loaded, w_out_scaled)
            output_and_router(nc, m, x, w_out_scaled, attn_post_g, ffn_pre_g, w_router)
        late = LateWeights(nc, ctx, m)
        experts(nc, m, late, w_gate_up, w_down, p, w_ple_gate, w_ple_proj)
        combine_and_embed(nc, m, late, ffn_post_g, b_ple_gate, ple_norm_g, out)


_INS = ["x", "p", "positions", "attn_pre_g", "w_in", "q_norm_g", "w_uq", "kv_norm_g", "w_ukv", "sg_norm_g",
        "w_spatial", "b_spatial", "mla_out_g", "sg_out_g", "w_out", "attn_post_g", "ffn_pre_g", "w_router",
        "b_router", "w_gate_up", "b_gate_up", "w_down", "b_down", "ffn_post_g", "w_ple_gate", "b_ple_gate",
        "w_ple_proj", "ple_norm_g"]


def kernel(**inputs):
    import concourse.bacc as bacc
    from concourse.bass_utils import run_bass_kernel_spmd

    nc = bacc.Bacc("TRN2", target_bir_lowering=False, num_devices=1)
    arrays, args = {}, []
    for name in _INS:
        a = np.ascontiguousarray(inputs[name])
        arrays[f"in_{name}"] = a
        args.append(nc.dram_tensor(f"in_{name}", a.shape, mybir.dt.from_np(a.dtype), kind="ExternalInput").ap())
    out = nc.dram_tensor("out", (1, SEQ, D), F32, kind="ExternalOutput").ap()
    decoder_layer(nc, *args, out)
    r = run_bass_kernel_spmd(nc, [arrays], core_ids=[0])
    return r.results[0]["out"]
```
